# Optimizing a Trainium2 kernel written in Bass

```python
import jax, jax.numpy as jnp
from jax import lax
import numpy as np

D_MODEL = 1024
BATCH = 1
SEQ = 2048
DEPTH = 1
DEC_BATCH = 8
DEC_SEQ = 4
PAST_LEN = 16384
PAGE_SIZE = 128

D_MIX = D_MODEL
D_A = D_MIX // 2
N_BLK_A = 8
BLK_A = D_A // N_BLK_A
CONV_W = 4
C_RGLRU = 8.0
D_B = D_MIX - D_A
N_HEADS_B = 4
DK_B = D_B // N_HEADS_B
DV_B = D_B // N_HEADS_B
CHUNK = 64
P_IN = 2 * D_A + 4 * D_B
EPS = 1e-6
F_MIN = 1e-30

kernel_name = 'hymba_rglru_hgrn2_step'

def _rmsnorm(x, w):
    xf = x.astype(jnp.float32)
    y = xf * lax.rsqrt(jnp.mean(xf * xf, axis=-1, keepdims=True) + EPS)
    return y * w.astype(jnp.float32)

def _causal_conv(x, buf, w, b):
    L = x.shape[1]
    xp = jnp.concatenate([buf.astype(x.dtype), x], axis=1)
    y = b + sum(xp[:, j:j + L] * w[j] for j in range(CONV_W))
    return y, xp[:, L:]

def _lin_comb(e1, e2):
    a1, b1 = e1
    a2, b2 = e2
    return a1 * a2, a2 * b1 + b2

def _rglru(x, h0, wa, ba, wx, bx, lam):
    B, L, _ = x.shape
    xb = x.reshape(B, L, N_BLK_A, BLK_A)
    r = jax.nn.sigmoid(jnp.einsum('blnc,ncd->blnd', xb, wa).reshape(B, L, D_A) + ba)
    i = jax.nn.sigmoid(jnp.einsum('blnc,ncd->blnd', xb, wx).reshape(B, L, D_A) + bx)
    log_a = -C_RGLRU * jax.nn.softplus(-lam.astype(jnp.float32)) * r.astype(jnp.float32)
    a = jnp.exp(log_a)
    u = jnp.sqrt(jnp.maximum(-jnp.expm1(2.0 * log_a), 0.0)) * (i * x).astype(jnp.float32)
    u = u.at[:, 0].add(a[:, 0] * h0.astype(jnp.float32))
    _, h = lax.associative_scan(_lin_comb, (a, u), axis=1)
    return h, h[:, -1]

def _hgrn2(q, logf, k, v, S0):
    B, L, H, _ = q.shape
    DV = v.shape[-1]
    C = min(CHUNK, L)
    n = -(-L // C)
    pad = n * C - L

    def prep(t):
        t = jnp.pad(t, ((0, 0), (0, pad), (0, 0), (0, 0)))
        return jnp.moveaxis(t.reshape(B, n, C, H, t.shape[-1]), 1, 0)

    mask = jnp.tril(jnp.ones((C, C), bool))[None, :, :, None, None]

    def step(S, inp):
        qc, gc, kc, vc = inp
        b = jnp.cumsum(gc, axis=1)
        diff = b[:, :, None] - b[:, None, :]
        dec = jnp.where(mask, jnp.exp(jnp.where(mask, diff, 0.0)), 0.0)
        A = jnp.einsum('bthk,btshk,bshk->bhts', qc, dec, kc)
        o = (jnp.einsum('bhts,bshv->bthv', A, vc)
             + jnp.einsum('bthk,bhkv->bthv', qc * jnp.exp(b), S))
        bl = b[:, -1]
        S = (jnp.exp(bl)[..., None] * S
             + jnp.einsum('bshk,bshv->bhkv', kc * jnp.exp(bl[:, None] - b), vc))
        return S, o

    S_fin, o = lax.scan(step, S0, (prep(q), prep(logf), prep(k), prep(v)))
    o = jnp.moveaxis(o, 0, 1).reshape(B, n * C, H, DV)[:, :L]
    return o, S_fin

def _layer(x, c, h0, conv0, S0, lb, ada_w, ada_b, pre_w, post_w, w_in, conv_w, conv_b,
           rg_wa, rg_ba, rg_wx, rg_bx, rg_lam, onorm_w, w_out):
    B, L, _ = x.shape
    mod = jax.nn.silu(c) @ ada_w + ada_b
    shift, scale, gate = jnp.split(mod, 3, axis=-1)
    hn = (_rmsnorm(x, pre_w) * (1.0 + scale[:, None]) + shift[:, None]).astype(x.dtype)
    z = hn @ w_in
    xa, ga, q, fr, iv, gb = jnp.split(
        z, [D_A, 2 * D_A, 2 * D_A + D_B, 2 * D_A + 2 * D_B, 2 * D_A + 3 * D_B], axis=-1)
    xc, conv_new = _causal_conv(xa, conv0, conv_w, conv_b)
    ha, h_new = _rglru(xc, h0, rg_wa, rg_ba, rg_wx, rg_bx, rg_lam)
    ya = ha * jax.nn.silu(ga.astype(jnp.float32))
    frh = fr.astype(jnp.float32).reshape(B, L, N_HEADS_B, DK_B)
    lbh = lb.reshape(N_HEADS_B, DK_B)
    f = lbh + (1.0 - lbh) * jax.nn.sigmoid(frh)
    logf = jnp.log(jnp.maximum(f, F_MIN))
    k = (1.0 - lbh) * jax.nn.sigmoid(-frh)
    qh = q.astype(jnp.float32).reshape(B, L, N_HEADS_B, DK_B)
    vh = iv.astype(jnp.float32).reshape(B, L, N_HEADS_B, DV_B)
    ob, S_new = _hgrn2(qh, logf, k, vh, S0.astype(jnp.float32))
    ob = _rmsnorm(ob, onorm_w.reshape(N_HEADS_B, DV_B))
    yb = ob.reshape(B, L, D_B) * jax.nn.silu(gb.astype(jnp.float32))
    m = jnp.concatenate([ya, yb], axis=-1).astype(x.dtype) @ w_out
    x = x + (gate[:, None] * _rmsnorm(m, post_w)).astype(x.dtype)
    return x, h_new.astype(x.dtype), conv_new.astype(x.dtype), S_new.astype(x.dtype)

def setup_inputs(seed: int = 0) -> dict:
    key = jax.random.key(seed)
    ks = jax.random.split(key, 24)
    nrm = jax.random.normal
    f32 = jnp.float32
    u = jax.random.uniform(ks[18], (DEPTH, D_A), f32, minval=0.9, maxval=0.999)
    s = u ** (1.0 / C_RGLRU)
    return {
        'x_prompt': nrm(ks[0], (BATCH, SEQ, D_MODEL), f32),
        'x_sample': nrm(ks[1], (DEC_BATCH, DEC_SEQ, D_MODEL), f32),
        'state_rglru_h': 0.5 * nrm(ks[2], (DEPTH, DEC_BATCH, D_A), f32),
        'state_rglru_conv': nrm(ks[3], (DEPTH, DEC_BATCH, CONV_W - 1, D_A), f32),
        'state_hgrn_S': 0.3 * nrm(ks[4], (DEPTH, DEC_BATCH, N_HEADS_B, DK_B, DV_B), f32),
        'c_prompt': nrm(ks[5], (BATCH, D_MODEL), f32),
        'c_sample': nrm(ks[6], (DEC_BATCH, D_MODEL), f32),
        'ada_w': 0.5 * D_MODEL ** -0.5 * nrm(ks[7], (DEPTH, D_MODEL, 3 * D_MODEL), f32),
        'ada_b': 0.02 * nrm(ks[8], (DEPTH, 3 * D_MODEL), f32),
        'pre_norm_w': 1.0 + 0.1 * nrm(ks[9], (DEPTH, D_MODEL), f32),
        'post_norm_w': 1.0 + 0.1 * nrm(ks[10], (DEPTH, D_MODEL), f32),
        'w_in': D_MODEL ** -0.5 * nrm(ks[11], (DEPTH, D_MODEL, P_IN), f32),
        'conv_w': CONV_W ** -0.5 * nrm(ks[12], (DEPTH, CONV_W, D_A), f32),
        'conv_b': 0.02 * nrm(ks[13], (DEPTH, D_A), f32),
        'rg_wa': BLK_A ** -0.5 * nrm(ks[14], (DEPTH, N_BLK_A, BLK_A, BLK_A), f32),
        'rg_ba': 0.1 * nrm(ks[15], (DEPTH, D_A), f32),
        'rg_wx': BLK_A ** -0.5 * nrm(ks[16], (DEPTH, N_BLK_A, BLK_A, BLK_A), f32),
        'rg_bx': 0.1 * nrm(ks[17], (DEPTH, D_A), f32),
        'rg_lambda': jnp.log(s) - jnp.log1p(-s),
        'hg_lb_logits': nrm(ks[19], (DEPTH, D_B), f32),
        'hg_onorm_w': 1.0 + 0.1 * nrm(ks[20], (DEPTH, D_B), f32),
        'w_out': D_MIX ** -0.5 * nrm(ks[21], (DEPTH, D_MIX, D_MODEL), f32),
    }

def reference(x_prompt, x_sample, state_rglru_h, state_rglru_conv, state_hgrn_S, c_prompt, c_sample,
              ada_w, ada_b, pre_norm_w, post_norm_w, w_in, conv_w, conv_b, rg_wa, rg_ba, rg_wx, rg_bx,
              rg_lambda, hg_lb_logits, hg_onorm_w, w_out):
    probs = jax.nn.softmax(hg_lb_logits.astype(jnp.float32), axis=0)
    lb_all = jnp.cumsum(probs, axis=0) - probs[0]
    bp = x_prompt.shape[0]
    hp0 = jnp.zeros((bp, D_A), jnp.float32)
    cp0 = jnp.zeros((bp, CONV_W - 1, D_A), x_prompt.dtype)
    Sp0 = jnp.zeros((bp, N_HEADS_B, DK_B, DV_B), jnp.float32)
    xp, xs = x_prompt, x_sample
    hp, cvp, Sp, hs, cvs, Ss = [], [], [], [], [], []
    for l in range(DEPTH):
        w = (ada_w[l], ada_b[l], pre_norm_w[l], post_norm_w[l], w_in[l], conv_w[l], conv_b[l],
             rg_wa[l], rg_ba[l], rg_wx[l], rg_bx[l], rg_lambda[l], hg_onorm_w[l], w_out[l])
        xp, h, cv, S = _layer(xp, c_prompt, hp0, cp0, Sp0, lb_all[l], *w)
        hp.append(h); cvp.append(cv); Sp.append(S)
        xs, h, cv, S = _layer(xs, c_sample, state_rglru_h[l], state_rglru_conv[l], state_hgrn_S[l],
                              lb_all[l], *w)
        hs.append(h); cvs.append(cv); Ss.append(S)
    return (xp, xs, jnp.stack(hp), jnp.stack(cvp), jnp.stack(Sp), jnp.stack(hs), jnp.stack(cvs), jnp.stack(Ss))


_drawn_inputs = setup_inputs


def setup_inputs(seed=0):
    import zlib

    import numpy as np

    out = dict(_drawn_inputs(seed))
    spreads = {}
    factors = {'rg_ba': 2.916}
    for name, (base, spread) in spreads.items():
        noise = np.random.default_rng([zlib.crc32(name.encode()), seed]).standard_normal(out[name].shape)
        drawn = base * np.exp(spread * noise) if base else spread * noise
        out[name] = __import__('jax').numpy.asarray(drawn.astype(out[name].dtype))
    for name, factor in factors.items():
        out[name] = (out[name] * factor).astype(out[name].dtype)
    return out
```

```python
from contextlib import ExitStack

import concourse.bass as bass
from concourse import mybir

F32 = mybir.dt.float32
BF16 = mybir.dt.bfloat16
F16 = mybir.dt.float16
U8 = mybir.dt.uint8
I32 = mybir.dt.int32
ALU = mybir.AluOpType
ACT = mybir.ActivationFunctionType

P = 128
D = 1024
KT = D // P
DA = 512
CT = DA // P
HB = 4
PIN = 2 * DA + 4 * DA
SEQ = 2048
T = 256
NT = T // P
BODIES = SEQ // T
CW = 4
NB, NL = 8, 4
TD = NB * NL
NS = 1 + NB
EPS = 1e-6
F_MIN = 1e-30
C_RGLRU = 8.0
LEVELS = 7
DLEVELS = 2
NEWTON = 12
MAGIC = float(0x5F3759DF)

XA, GA, Q_, FR, IV, GB = (i * DA for i in range(6))
ROW = {}
_at = 0
for _name, _n in (("pre", KT), ("post", KT), ("cw", CW * CT), ("cb", CT), ("ba", CT), ("bx", CT), ("lam", CT),
                  ("lbl", CT), ("onw", CT), ("adab", 3 * KT)):
    ROW[_name] = _at
    _at += _n
NROW = _at


def build(nc, x_prompt, x_sample, state_rglru_h, state_rglru_conv, state_hgrn_S, c_prompt, c_sample, ada_w, ada_b,
          pre_norm_w, post_norm_w, w_in, conv_w, conv_b, rg_wa, rg_ba, rg_wx, rg_bx, rg_lambda, hg_lb_logits,
          hg_onorm_w, w_out, y_prompt, y_sample, h_prompt, conv_prompt, S_prompt, h_sample, conv_sample, S_sample):
    with ExitStack() as ctx:
        def sb(name, shape, dt=F32):
            return ctx.enter_context(nc.sbuf_tensor(name, shape, dt))

        def sem(name):
            return ctx.enter_context(nc.semaphore(name))

        wih = sb("wih", [P, KT, PIN], BF16)
        wil = sb("wil", [P, KT, PIN], F16)
        woh = sb("woh", [P, KT, D], BF16)
        wol = sb("wol", [P, KT, D], F16)
        work = sb("work", [P, 4096])
        stage = [work[:, 2048 * i:2048 * i + 2048].rearrange("p (k n) -> p k n", k=KT) for i in range(2)]
        xr = work[:, 0:D]
        mg = work[:, D:2 * D]
        yh = work[:, 2048:3072].bitcast(BF16).rearrange("p (k t) -> p k t", k=KT)
        yl = work[:, 3072:4096].bitcast(F16).rearrange("p (k t) -> p k t", k=KT)
        hnh = sb("hnh", [P, KT, T], BF16)
        hnl = sb("hnl", [P, KT, T], F16)
        xin = sb("xin", [P, NT, D])
        gp = sb("gp", [P, D])
        xa = sb("xa", [P, 2, T + CW - 1])
        halo = sb("halo", [P, CT, CW - 1])
        xc = sb("xc", [P, 2, T])
        rr = sb("rr", [P, 2, T])
        ii = sb("ii", [P, 2, T])
        aa = sb("aa", [P, 2, T])
        sil = sb("sil", [P, CT, T])
        wg = sb("wg", [P, 2, CT, P])
        qq = sb("qq", [P, 2 * T])
        kk = sb("kk", [P, 2 * T])
        ff = sb("ff", [P, 2 * T])
        gg = sb("gg", [P, 2 * T - 4])
        am = sb("am", [P, 4, P])
        ktr = sb("ktr", [P, 4, P])
        vv = sb("vv", [P, NT, DA])
        gbs = sb("gbs", [P, NT, DA])
        st = sb("st", [P, HB, P])
        ident = sb("ident", [P, P])
        eye = sb("eye", [P, P], U8)
        lmask = sb("lmask", [P, LEVELS, P // 2], U8)
        smask = sb("smask", [TD, NB])
        junk = sb("junk", [P, 640], BF16)
        cols = sb("cols", [P, 5 * CT])
        lb, omlb, cneg, cpos, hst = (cols[:, CT * i:CT * i + CT] for i in range(5))
        tmp = xc[:, 1, 0:8 * CT].rearrange("p (a b) -> p a b", b=CT)
        par = sb("par", [P, NROW])
        sc1 = sb("sc1", [P, KT, NS])
        shf = sb("shf", [P, KT, NS])
        gpt = sb("gpt", [P, KT, NS])
        stat = sb("stat", [P, 35])
        ussq, essq, xssq, one = stat[:, 0:4], stat[:, 4:8], stat[:, 8:12], stat[:, 33:34]
        urs = stat[:, 12:24].rearrange("p (a b) -> p a b", a=3)
        ers = stat[:, 24:27].rearrange("p (a b) -> p a b", a=3)
        xrs = stat[:, 27:33].rearrange("p (a b) -> p a b", a=3)

        def goff(m):
            return sum(2 * T // b for b in (2, 4, 8, 16, 32, 64) if b < m)

        ring = [ctx.enter_context(nc.psum_tensor(f"ring{i}", [P, 512], F32)) for i in range(2)]
        aux = [ctx.enter_context(nc.psum_tensor(f"aux{i}", [P, 512], F32)) for i in range(2)]
        lev = [ctx.enter_context(nc.psum_tensor(f"lev{i}", [P, 512], F32)) for i in range(2)]
        ops = ctx.enter_context(nc.psum_tensor("ops", [P, 512], F32))
        kvp = ctx.enter_context(nc.psum_tensor("kvp", [P, 512], F32))

        class Signal:

            def __init__(self, name, per):
                self.sem, self.per = sem(name), per

            def at(self, n, j):
                return n * self.per + j

        yt_ps, fr_ps, q_ps, iv_ps, gb_ps = (Signal(s, 2) for s in ("yt_ps", "fr_ps", "q_ps", "iv_ps", "gb_ps"))
        e_ps, xa_ps, ga_ps, tr_ps = Signal("e_ps", 4), Signal("xa_ps", 2), Signal("ga_ps", 2), Signal("tr_ps", 4)
        lev_ps, kt_ps, u_ps = Signal("lev_ps", 2 * (LEVELS + 1)), Signal("kt_ps", 2), Signal("u_ps", 4)
        gr_ps, gi_ps = Signal("gr_ps", 2), Signal("gi_ps", 2)
        yth, f_sig, k_sig, q_sb, v_sb, gb_sil = (Signal(s, 2) for s in ("yth", "f_sig", "k_sig", "q_sb", "v_sb", "gb_sil"))
        esq = [Signal("esq0", 2), Signal("esq1", 2)]
        kt_sb, usq, xa_sb, ga_sil, xsq = Signal("kt_sb", 2), Signal("usq", 8), Signal("xa_sb", 2), Signal("ga_sil", 2), Signal("xsq", 4)
        r_sig, i_sig, a_exp, th_ok, u_sqrt = (Signal(s, k) for s, k in (("r_sig", 4), ("i_sig", 4), ("a_exp", 4), ("th_ok", 4), ("u_sqrt", 2)))
        aff, hn_hi = Signal("aff", 8), Signal("hn_hi", 4)
        ytl, f_ok, amask, q_f = Signal("ytl", 2), Signal("f_ok", 2), Signal("amask", 16), Signal("q_f", 2)
        q_upd, k_upd, g_upd = Signal("q_upd", 14), Signal("k_upd", 14), Signal("g_upd", 14)
        mgd, newt_e, eo = Signal("mgd", 4), Signal("newt_e", 2 * (NEWTON + 1)), Signal("eo", 2)
        newt_u, yb_ok, s_upd = Signal("newt_u", 4 * NEWTON), Signal("yb_ok", 8), Signal("s_upd", 8)
        newt_x, xn_ok, hn_lo = Signal("newt_x", NEWTON + 1), Signal("xn_ok", 2), Signal("hn_lo", 4)
        cvc, rx, gd, iu, scan, y_ok, yl_ok = (Signal(s, k) for s, k in (("cvc", 16), ("rx", 2), ("gd", 2), ("iu", 2), ("scan", 4), ("y_ok", 2), ("yl_ok", 1)))
        f_af, k_ok, a_sq, ix_ok, yh_ok, hl_in, hl_sv, hst_ok = (Signal(s, k) for s, k in (
            ("f_af", 4), ("k_ok", 4), ("a_sq", 2), ("ix_ok", 2), ("yh_ok", 1), ("hl_in", 2), ("hl_sv", 2), ("hst_ok", 2)))
        xld = [Signal("xld0", 16), Signal("xld1", 16)]
        xrl, ost = Signal("xrl", 32), Signal("ost", 32)
        par_ld, c_ld, wg_ld = sem("par_ld"), sem("c_ld"), sem("wg_ld")
        st_ld = [sem("st_ld0"), sem("st_ld1")]
        fin = sem("fin")
        consts, zeroed, pre_ps, pre_act, pre_dve = sem("consts"), sem("zeroed"), sem("pre_ps"), sem("pre_act"), sem("pre_dve")
        ada_ps, w_hi, w_lo, w_fold = sem("ada_ps"), sem("w_hi"), sem("w_lo"), sem("w_fold")
        d_ld, d_s0 = sem("d_ld"), sem("d_s0")
        consts_dve, consts_pool = sem("chain_dve"), sem("chain_pool")
        decode_sems = {}

        def dv(name):
            if name not in decode_sems:
                decode_sems[name] = sem("d_" + name)
            return decode_sems[name]

        xp_rows = x_prompt[0].rearrange("(m p) d -> m p d", p=P)
        yp_rows = y_prompt[0].rearrange("(m p) d -> m p d", p=P)
        w_in_v = w_in[0].rearrange("(k p) n -> p k n", p=P)
        w_out_v = w_out[0].rearrange("(k p) n -> p k n", p=P)
        ada_v = ada_w[0].rearrange("(k p) n -> p k n", p=P)

        NADA, NWI, NWO = 3 * D // 256, PIN // 256, D // 256
        pieces = ([("ada", i) for i in range(NADA)] + [("wi", i) for i in range(NWI)] + [("wo", i) for i in range(NWO)])

        def blocks(t, m):
            return t.rearrange("p (b two m) -> p b two m", two=2, m=m)

        def products(m):
            g = ff[:, :] if m == 1 else gg[:, goff(m):goff(m) + 2 * T // m]
            return g.rearrange("p (b two) -> p b two", two=2)

        def pcol(name, i):
            return par[:, ROW[name] + i:ROW[name] + i + 1]

        W4 = CT * TD
        s0 = wih[:, :, 0:2 * HB * P].bitcast(F32)
        flat = lambda t: t[:, :, :].rearrange("p c t -> p (c t)")
        xad = flat(xa)[:, 0:CT * NB * (CW - 1 + NL)].rearrange("p (c b j) -> p c b j", c=CT, b=NB)
        xcd, rrd, iid, aad = (flat(t)[:, 0:W4] for t in (xc, rr, ii, aa))
        h0, hnew = flat(ii)[:, 256:256 + CT * NB], flat(ii)[:, 320:320 + CT * NB]
        halod = flat(ii)[:, 384:384 + CT * NB * (CW - 1)]

        def vseq(b):
            return (vv, gbs)[b % 2][0:TD, 1, :]

        block = ctx.enter_context(nc.Block())

        @block.sync
        def _(sp):
            loads = [("pre", pre_norm_w[0]), ("post", post_norm_w[0]), ("cw", conv_w[0].rearrange("j c -> (j c)")),
                     ("cb", conv_b[0]), ("ba", rg_ba[0]), ("bx", rg_bx[0]), ("lam", rg_lambda[0]),
                     ("lbl", hg_lb_logits[0]), ("onw", hg_onorm_w[0]), ("adab", ada_b[0])]
            for name, src in loads:
                rows = src.rearrange("(r c) -> r c", c=P)
                sp.dma_start(am[ROW[name]:ROW[name] + rows.shape[0], 0, :], rows).then_inc(par_ld, 16)
            sp.dma_start(gp[0:1, :], c_prompt).then_inc(c_ld, 16)
            sp.dma_start(gp[1:NS, :], c_sample).then_inc(c_ld, 16)
            for t in range(NT):
                sp.dma_start(xin[:, t, :], xp_rows[t]).then_inc(xld[t].sem, 16)
            for i, (kind, c) in enumerate(pieces):
                if i >= 2:
                    pk, pc = pieces[i - 2]
                    if pk == "ada":
                        sp.wait_ge(ada_ps, pc + 1)
                    else:
                        done = pc + 1 if pk == "wi" else NWI + pc + 1
                        sp.wait_ge(w_hi, done)
                        sp.wait_ge(w_lo, done)
                src = {"ada": ada_v, "wi": w_in_v, "wo": w_out_v}[kind]
                sp.dma_start(stage[i % 2], src[:, :, 256 * c:256 * c + 256]).then_inc(st_ld[i % 2], 16)
                if i == 1:
                    sp.wait_ge(zeroed, 1)
                    for w, src in ((0, rg_wa), (1, rg_wx)):
                        for odd in range(2):
                            v = src[0].rearrange("(t two) c d -> two c t d", two=2)[odd]
                            sp.dma_start(wg[64 * odd:64 * odd + 64, w, :, 64 * odd:64 * odd + 64], v).then_inc(wg_ld, 16)

            def load_x(m, t):
                sp.wait_ge(tr_ps.sem, tr_ps.at(m - 1, 4))
                sp.dma_start(xin[:, t, :], xp_rows[m * NT + t]).then_inc(xld[t].sem, 16)

            def residual(n, t):
                sp.dma_start(xr, xp_rows[n * NT + t]).then_inc(xrl.sem, 16)
                sp.wait_ge(eo.sem, eo.at(n, t + 1))
                sp.dma_start(yp_rows[n * NT + t], xr).then_inc(ost.sem, 16)
                sp.wait_ge(ost.sem, ost.at(n, 16 * t + 16))

            sp.wait_ge(w_hi, NWI + NWO)
            sp.wait_ge(w_lo, NWI + NWO)
            for m in (1, 2):
                for t in range(NT):
                    load_x(m, t)
            with sp.Fori(1, BODIES - 2) as n:
                residual(n - 1, 0)
                load_x(n + 2, 0)
                residual(n - 1, 1)
                load_x(n + 2, 1)
            for n in range(BODIES - 3, BODIES):
                for t in range(NT):
                    residual(n, t)

            sp.wait_ge(tr_ps.sem, tr_ps.at(BODIES - 1, 4))
            sp.dma_start(xin[0:TD, 0, :], x_sample.rearrange("b l d -> (b l) d")).then_inc(d_ld, 16)
            sp.dma_start(xin[0:NB, 1, 0:DA], state_rglru_h[0]).then_inc(d_ld, 16)
            sp.dma_start(xin[0:NB * (CW - 1), 1, DA:D], state_rglru_conv[0].rearrange("b j c -> (b j) c")).then_inc(d_ld, 16)
            sp.wait_ge(dv("gb_d"), 1)
            for b in range(NB):
                sp.dma_start(s0[:, b, :].rearrange("p (h v) -> p h v", h=HB),
                             state_hgrn_S[0, b].rearrange("h k v -> k h v")).then_inc(d_s0, 16)
            sp.dma_start(xr[0:TD, :], x_sample.rearrange("b l d -> (b l) d")).then_inc(dv("xres"), 16)
            sp.wait_ge(dv("y_rows"), 1)
            sp.dma_start(y_sample.rearrange("b l d -> (b l) d"), xr[0:TD, :]).then_inc(fin, 16)
            sp.dma_start(S_prompt[0, 0].rearrange("h k v -> k h v"), st[:, :, :]).then_inc(fin, 16)
            sp.wait_ge(dv("s_new"), NB * HB)
            for b in range(NB):
                sp.dma_start(S_sample[0, b].rearrange("h k v -> k h v"),
                             s0[:, b, :].rearrange("p (h v) -> p h v", h=HB)).then_inc(fin, 16)
            sp.wait_ge(dv("rows_sb"), 4)
            sp.dma_start(h_prompt[0].rearrange("a (c p) -> (a c) p", p=P), xin[0:CT, 1, 0:P]).then_inc(fin, 16)
            sp.dma_start(h_sample[0], xin[0:NB, 0, 0:DA]).then_inc(fin, 16)
            sp.dma_start(conv_prompt[0, 0], xin[0:CW - 1, 1, DA:D]).then_inc(fin, 16)
            sp.dma_start(conv_sample[0].rearrange("b j c -> (b j) c"), xin[0:NB * (CW - 1), 0, DA:D]).then_inc(fin, 16)
            sp.wait_ge(fin, 16 * (2 + NB + 4))

        @block.tensor
        def _(pe):
            mm = nc.tensor.matmul

            def split3(out, lh, ll, rh, rl, ks, start, stop):
                last = None
                for k in ks:
                    for j, (a, b) in enumerate(((lh, rh), (lh, rl), (ll, rh))):
                        last = mm(out, a(k), b(k), start=start and k == ks[0] and j == 0,
                                  stop=stop and k == ks[-1] and j == 2)
                return last

            def project(bank, col, c):
                lo = col + P * c
                return split3(bank[:, T * c:T * c + T], lambda k: wih[:, k, lo:lo + P], lambda k: wil[:, k, lo:lo + P],
                              lambda k: hnh[:, k, :], lambda k: hnl[:, k, :], range(KT), True, True)

            def project_rows(bank, col, t, half):
                lo = P * t
                ks = range(KT // 2) if half == 0 else range(KT // 2, KT)
                return split3(bank[:, :], lambda k: hnh[:, k, lo:lo + P], lambda k: hnl[:, k, lo:lo + P],
                              lambda k: wih[:, k, col:col + DA], lambda k: wil[:, k, col:col + DA], ks,
                              half == 0, half == 1)

            def out_rows(bank, t, cols, half):
                lo, co = P * t, 512 * cols
                ks = range(KT // 2) if half == 0 else range(KT // 2, KT)
                return split3(bank[:, :], lambda k: yh[:, k, lo:lo + P], lambda k: yl[:, k, lo:lo + P],
                              lambda k: woh[:, k, co:co + 512], lambda k: wol[:, k, co:co + 512], ks,
                              half == 0, half == 1)

            def turn_x(m, j):
                if j == 0:
                    pe.wait_ge(xn_ok.sem, xn_ok.at(m, NT))
                bank = aux[(j + 1) % 2]
                for k in (2 * j, 2 * j + 1):
                    for t in range(NT):
                        last = nc.tensor.transpose(bank[:, (k % 2) * T + P * t:(k % 2) * T + P * t + P],
                                                   xin[:, t, P * k:P * k + P], ident[:, :])
                last.then_inc(tr_ps.sem, 1)

            def turn_y(n, j):
                if j == 0:
                    pe.wait_ge(yb_ok.sem, yb_ok.at(n, 8))
                    pe.wait_ge(r_sig.sem, r_sig.at(n, 4))
                else:
                    pe.wait_ge(i_sig.sem, i_sig.at(n, 4))
                for h in range(2):
                    for t in range(NT):
                        last = nc.tensor.transpose(aux[j][:, T * h + P * t:T * h + P * t + P],
                                                   gbs[:, t, P * (2 * j + h):P * (2 * j + h) + P], ident[:, :])
                last.then_inc(yt_ps.sem, 1)

            def level(n, p, l):
                i = p * (LEVELS + 1) + l
                if i >= 2 or not isinstance(n, int) or n > 0:
                    pe.wait_ge(amask.sem, amask.at(n, i - 1))
                if l == 0:
                    pe.wait_ge(q_sb.sem, q_sb.at(n, p + 1))
                    pe.wait_ge(k_ok.sem, k_ok.at(n, 2 * p + 2))
                elif l == 1:
                    pe.wait_ge(q_f.sem, q_f.at(n, p + 1))
                else:
                    pe.wait_ge(q_upd.sem, q_upd.at(n, LEVELS * p + l - 1))
                    pe.wait_ge(k_upd.sem, k_upd.at(n, LEVELS * p + l - 1))
                for hc in range(4):
                    q = qq[:, P * hc:P * hc + P]
                    w = P
                    if l > 0:
                        q, w = blocks(q, 1 << (l - 1))[:, :, 1, :], P // 2
                    last = mm(lev[i % 2][:, w * hc:w * hc + w], kk[:, P * hc:P * hc + P], q, start=True, stop=True)
                last.then_inc(lev_ps.sem, 1)

            def turn_k(n, p):
                pe.wait_ge(q_upd.sem, q_upd.at(n, LEVELS * p + LEVELS))
                pe.wait_ge(k_upd.sem, k_upd.at(n, LEVELS * p + LEVELS))
                for hc in range(4):
                    last = nc.tensor.transpose(aux[p][:, P * hc:P * hc + P], kk[:, P * hc:P * hc + P], ident[:, :])
                last.then_inc(kt_ps.sem, 1)

            def unit(n, p, c):
                ui = 2 * p + c
                pe.wait_ge(amask.sem, amask.at(n, 8 * p + 8))
                pe.wait_ge(v_sb.sem, v_sb.at(n, c + 1))
                pe.wait_ge(kt_sb.sem, kt_sb.at(n, p + 1))
                pe.wait_ge(yb_ok.sem, yb_ok.at(n, 2 * ui))
                pe.wait_ge(s_upd.sem, s_upd.at(n, 2 * ui))
                for h in range(2):
                    hc, hd = 2 * h + c, 2 * p + h
                    v = vv[:, c, P * hd:P * hd + P]
                    mm(ops[:, P * h:P * h + P], am[:, hc, :], v, start=True, stop=False)
                    mm(ops[:, P * h:P * h + P], qq[:, P * hc:P * hc + P], st[:, hd, :], start=False, stop=True)
                    last = mm(kvp[:, P * h:P * h + P], ktr[:, hc, :], v, start=True, stop=True)
                last.then_inc(u_ps.sem, 1)

            def gates(n, p):
                pe.wait_ge(cvc.sem, cvc.at(n, 8 * p + 8))
                for w, s in ((0, gr_ps), (1, gi_ps)):
                    if p == 0 and w == 0:
                        if not isinstance(n, int) or n > 0:
                            pe.wait_ge(ytl.sem, ytl.at(n - 1, 2))
                    elif w == 1:
                        pe.wait_ge(kt_sb.sem, kt_sb.at(n, p + 1))
                    elif not (isinstance(n, int) and n == BODIES - 1):
                        pe.wait_ge(hn_lo.sem, hn_lo.at(n + 1, 4))
                    for c in range(2):
                        last = mm(aux[(1 + w + p) % 2][:, T * c:T * c + T], wg[:, w, 2 * p + c, :], xc[:, c, :],
                                  start=True, stop=True)
                    last.then_inc(s.sem, 1)

            def body(n, first, last_body):
                if not first:
                    turn_y(n - 1, 0)
                    turn_y(n - 1, 1)
                for k in range(4):
                    pe.wait_ge(hn_lo.sem, hn_lo.at(n, k + 1))
                project(ring[0], FR, 0)
                project(ring[0], FR, 1).then_inc(fr_ps.sem, 1)
                project(ring[1], Q_, 0)
                project(ring[1], Q_, 1).then_inc(q_ps.sem, 1)
                pe.wait_ge(k_sig.sem, k_sig.at(n, 1))
                project_rows(ring[0], IV, 0, 0)
                project_rows(ring[0], IV, 0, 1).then_inc(iv_ps.sem, 1)
                level(n, 0, 0)
                pe.wait_ge(q_sb.sem, q_sb.at(n, 1))
                project_rows(ring[1], IV, 1, 0)
                level(n, 0, 1)
                project_rows(ring[1], IV, 1, 1).then_inc(iv_ps.sem, 1)
                level(n, 0, 2)
                pe.wait_ge(v_sb.sem, v_sb.at(n, 1))
                project_rows(ring[0], GB, 0, 0)
                level(n, 0, 3)
                project_rows(ring[0], GB, 0, 1).then_inc(gb_ps.sem, 1)
                level(n, 0, 4)
                pe.wait_ge(v_sb.sem, v_sb.at(n, 2))
                project_rows(ring[1], GB, 1, 0)
                level(n, 0, 5)
                project_rows(ring[1], GB, 1, 1).then_inc(gb_ps.sem, 1)
                level(n, 0, 6)
                if not first:
                    pe.wait_ge(yl_ok.sem, yl_ok.at(n - 1, 1))
                    pe.wait_ge(ytl.sem, ytl.at(n - 1, 2))
                    pe.wait_ge(gb_sil.sem, gb_sil.at(n, 1))
                    out_rows(ring[0], 0, 0, 0)
                level(n, 0, 7)
                if not first:
                    out_rows(ring[0], 0, 0, 1).then_inc(e_ps.sem, 1)
                if not first:
                    pe.wait_ge(ytl.sem, ytl.at(n - 1, 1))
                turn_k(n, 0)
                if not first:
                    pe.wait_ge(gb_sil.sem, gb_sil.at(n, 2))
                    out_rows(ring[1], 0, 1, 0)
                unit(n, 0, 0)
                if not first:
                    out_rows(ring[1], 0, 1, 1).then_inc(e_ps.sem, 1)
                unit(n, 0, 1)
                pe.wait_ge(gb_sil.sem, gb_sil.at(n, 1))
                if not first:
                    pe.wait_ge(esq[0].sem, esq[0].at(n - 1, 1))
                project(ring[0], FR + 2 * P, 0)
                project(ring[0], FR + 2 * P, 1).then_inc(fr_ps.sem, 1)
                pe.wait_ge(gb_sil.sem, gb_sil.at(n, 2))
                if not first:
                    pe.wait_ge(esq[1].sem, esq[1].at(n - 1, 1))
                project(ring[1], Q_ + 2 * P, 0)
                project(ring[1], Q_ + 2 * P, 1).then_inc(q_ps.sem, 1)
                pe.wait_ge(k_sig.sem, k_sig.at(n, 2))
                project(ring[0], XA, 0)
                project(ring[0], XA, 1).then_inc(xa_ps.sem, 1)
                level(n, 1, 0)
                pe.wait_ge(q_sb.sem, q_sb.at(n, 2))
                project(ring[1], GA, 0)
                level(n, 1, 1)
                project(ring[1], GA, 1).then_inc(ga_ps.sem, 1)
                level(n, 1, 2)
                pe.wait_ge(xa_sb.sem, xa_sb.at(n, 1))
                project(ring[0], XA + 2 * P, 0)
                level(n, 1, 3)
                gates(n, 0)
                project(ring[0], XA + 2 * P, 1).then_inc(xa_ps.sem, 1)
                level(n, 1, 4)
                pe.wait_ge(ga_sil.sem, ga_sil.at(n, 1))
                project(ring[1], GA + 2 * P, 0)
                level(n, 1, 5)
                project(ring[1], GA + 2 * P, 1).then_inc(ga_ps.sem, 1)
                level(n, 1, 6)
                if not last_body:
                    pe.wait_ge(r_sig.sem, r_sig.at(n, 2))
                    turn_x(n + 1, 0)
                    pe.wait_ge(i_sig.sem, i_sig.at(n, 2))
                    turn_x(n + 1, 1)
                if not first:
                    pe.wait_ge(xa_sb.sem, xa_sb.at(n, 2))
                    out_rows(ring[0], 1, 0, 0)
                level(n, 1, 7)
                if not last_body:
                    pe.wait_ge(hn_lo.sem, hn_lo.at(n + 1, 1))
                    turn_x(n + 1, 2)
                    pe.wait_ge(hn_lo.sem, hn_lo.at(n + 1, 2))
                    turn_x(n + 1, 3)
                if not first:
                    out_rows(ring[0], 1, 0, 1).then_inc(e_ps.sem, 1)
                if last_body:
                    pe.wait_ge(r_sig.sem, r_sig.at(n, 2))
                else:
                    pe.wait_ge(hn_lo.sem, hn_lo.at(n + 1, 3))
                turn_k(n, 1)
                if not first:
                    pe.wait_ge(ga_sil.sem, ga_sil.at(n, 2))
                    out_rows(ring[1], 1, 1, 0)
                if last_body:
                    pe.wait_ge(i_sig.sem, i_sig.at(n, 2))
                gates(n, 1)
                unit(n, 1, 0)
                if not first:
                    out_rows(ring[1], 1, 1, 1).then_inc(e_ps.sem, 1)
                unit(n, 1, 1)

            pe.wait_ge(consts, 1)
            pe.wait_ge(par_ld, 160)
            nc.tensor.transpose(aux[0][:, 0:NROW], am[0:NROW, 0, :], ident[0:NROW, 0:NROW]).then_inc(pre_ps, 1)
            pe.wait_ge(c_ld, 32)
            for k in range(KT):
                last = nc.tensor.transpose(aux[1][:, NS * k:NS * k + NS], gp[0:NS, P * k:P * k + P], ident[0:NS, 0:NS])
            last.then_inc(pre_ps, 1)
            pe.wait_ge(pre_act, 2)
            siluc = xc[:, 0, 0:KT * NS].rearrange("p (k s) -> p k s", k=KT)
            for i in range(NADA):
                pe.wait_ge(st_ld[i % 2], 16 * (i // 2 + 1))
                for c in range(2):
                    o = (2 * i + c) * NS
                    for k in range(KT):
                        last = mm(ops[:, o:o + NS], stage[i % 2][:, k, P * c:P * c + P], siluc[:, k, :],
                                  start=k == 0, stop=k == KT - 1)
                last.then_inc(ada_ps, 1)
            pe.wait_ge(pre_dve, 1)
            for k in range(KT):
                last = mm(lev[k // 4][:, P * (k % 4):P * (k % 4) + P], gpt[:, k, 0:1].to_broadcast([P, P]), ident[:, :],
                          start=True, stop=True)
            last.then_inc(pre_ps, 1)
            for j in range(4):
                if j >= 2:
                    pe.wait_ge(hn_lo.sem, j - 1)
                turn_x(0, j)
            pe.wait_ge(w_hi, NWI)
            pe.wait_ge(w_lo, NWI)
            pe.wait_ge(wg_ld, 64)
            pe.wait_ge(zeroed, 3)
            pe.wait_ge(pre_act, 3)

            body(0, True, False)
            pe.wait_ge(w_hi, NWI + NWO)
            pe.wait_ge(w_lo, NWI + NWO)
            with pe.Fori(1, BODIES - 1) as n:
                body(n, False, False)
            body(BODIES - 1, False, True)
            n = BODIES
            turn_y(n - 1, 0)
            turn_y(n - 1, 1)
            pe.wait_ge(yl_ok.sem, yl_ok.at(n - 1, 1))
            pe.wait_ge(ytl.sem, ytl.at(n - 1, 2))
            for j in range(4):
                pe.wait_ge(esq[j % 2].sem, esq[j % 2].at(n - 1, j // 2))
                if j < 2:
                    pe.wait_ge(ga_sil.sem, ga_sil.at(n - 1, 2))
                out_rows(ring[j % 2], j // 2, j % 2, 0)
                out_rows(ring[j % 2], j // 2, j % 2, 1).then_inc(e_ps.sem, 1)

            pe.wait_ge(dv("xn"), 1)
            pe.wait_ge(d_ld, 48)
            for k in range(KT):
                nc.tensor.transpose(aux[0][:, TD * k:TD * k + TD], xin[0:TD, 0, P * k:P * k + P], ident[0:TD, 0:TD])
            for c in range(CT):
                nc.tensor.transpose(aux[1][:, NB * c:NB * c + NB], xin[0:NB, 1, P * c:P * c + P], ident[0:NB, 0:NB])
            nj = NB * (CW - 1)
            for c in range(CT):
                last = nc.tensor.transpose(aux[1][:, TD + nj * c:TD + nj * c + nj], xin[0:nj, 1, DA + P * c:DA + P * c + P],
                                           ident[0:nj, 0:nj])
            last.then_inc(dv("turned"), 1)
            gprow = aa[:, 1, :].rearrange("p (k t) -> p k t", k=KT)
            pe.wait_ge(dv("gprow"), 1)
            for k in range(KT):
                last = mm(lev[k // 4][0:TD, P * (k % 4):P * (k % 4) + P], gprow[:, k, :], ident[:, :], start=True, stop=True)
            last.then_inc(dv("gp_ps"), 1)
            pe.wait_ge(dv("hn"), 1)
            pe.wait_ge(dv("carried"), 2)
            pe.wait_ge(esq[0].sem, esq[0].at(n, 0))
            for i, col in enumerate([b + P * c for b in (XA, GA, Q_, FR) for c in range(CT)]):
                last = split3(ring[0][:, TD * i:TD * i + TD], lambda k: wih[:, k, col:col + P], lambda k: wil[:, k, col:col + P],
                              lambda k: hnh[:, k, 0:TD], lambda k: hnl[:, k, 0:TD], range(KT), True, True)
            last.then_inc(dv("proj_ps"), 1)
            pe.wait_ge(esq[1].sem, esq[1].at(n, 0))
            for bank, col, s in ((ring[1], IV, "iv_d"), (aux[0], GB, "gb_d")):
                split3(bank[0:TD, :], lambda k: hnh[:, k, 0:TD], lambda k: hnl[:, k, 0:TD],
                       lambda k: wih[:, k, col:col + DA], lambda k: wil[:, k, col:col + DA], range(KT), True, True)\
                    .then_inc(dv(s), 1)
            for l in range(DLEVELS + 1):
                pe.wait_ge(dv("level_in"), l + 1)
                if l == 0:
                    pe.wait_ge(dv("gp_sb"), 1)
                if l == 2:
                    pe.wait_ge(dv("masked"), 1)
                for h in range(HB):
                    q, w = qq[:, TD * h:TD * h + TD], TD
                    if l > 0:
                        q, w = blocks(q, 1 << (l - 1))[:, :, 1, :], TD // 2
                    last = mm(lev[l % 2][0:TD, w * h:w * h + w], kk[:, TD * h:TD * h + TD], q, start=True, stop=True)
                last.then_inc(dv("level_ps"), 1)
            pe.wait_ge(dv("level_in"), DLEVELS + 2)
            for h in range(HB):
                last = nc.tensor.transpose(aux[1][0:TD, P * h:P * h + P], kk[:, TD * h:TD * h + TD], ident[:, :])
            last.then_inc(dv("kt_d"), 1)
            pe.wait_ge(dv("masked"), DLEVELS + 1)
            pe.wait_ge(dv("v_d"), 1)
            pe.wait_ge(d_s0, 16 * NB)
            for h in range(HB):
                mm(ops[:, TD * h:TD * h + TD], vv[0:TD, 0, P * h:P * h + P], am[0:TD, h, 0:TD], start=True, stop=False,
                   skip_group_check=True)
                for b in range(NB):
                    o = TD * h + NL * b
                    last = mm(ops[:, o:o + NL], s0[:, b, P * h:P * h + P], qq[:, o:o + NL], start=False, stop=b == NB - 1,
                              skip_group_check=True)
            last.then_inc(dv("ot_ps"), 1)
            pe.wait_ge(dv("ot_sb"), 1)
            for h in range(HB):
                last = nc.tensor.transpose(lev[1][0:TD, P * h:P * h + P], ff[:, TD * h:TD * h + TD], ident[:, :])
            last.then_inc(dv("o_ps"), 1)
            pe.wait_ge(dv("conv_d"), 16)
            for w in range(2):
                for c in range(CT):
                    o = TD * CT * w + TD * c
                    last = mm(ring[1][:, o:o + TD], wg[:, w, c, :], xcd[:, TD * c:TD * c + TD], start=True, stop=True)
            last.then_inc(dv("gates_ps"), 1)
            pe.wait_ge(dv("yb_d"), HB)
            for h in range(HB):
                last = nc.tensor.transpose(lev[0][:, TD * h:TD * h + TD], gbs[0:TD, 0, P * h:P * h + P], ident[0:TD, 0:TD])
            last.then_inc(dv("ybt_ps"), 1)
            pe.wait_ge(dv("y_dec"), 4)
            for c in range(2):
                split3(ring[c][0:TD, :], lambda k: yh[:, k, 0:TD], lambda k: yl[:, k, 0:TD],
                       lambda k: woh[:, k, 512 * c:512 * c + 512], lambda k: wol[:, k, 512 * c:512 * c + 512],
                       range(KT), True, True).then_inc(dv("m_ps"), 1)
            for c in range(CT):
                nc.tensor.transpose(aux[0][0:nj, P * c:P * c + P], halod[:, nj * c:nj * c + nj], ident[:, :])
            for c in range(CT):
                nc.tensor.transpose(aux[1][0:NB, P * c:P * c + P], hnew[:, NB * c:NB * c + NB], ident[:, :])
            for c in range(CT):
                nc.tensor.transpose(ops[0:CW - 1, P * c:P * c + P], halo[:, c, :], ident[:, :])
            pe.wait_ge(hst_ok.sem, hst_ok.at(BODIES, 0))
            nc.tensor.transpose(lev[1][0:CT, 0:P], hst[:, :], ident[:, :]).then_inc(dv("rows_ps"), 1)
            for b in range(NB):
                pe.wait_ge(dv("v_seq"), b + 1)
                if b == 0:
                    pe.wait_ge(dv("kt_sbd"), 1)
                else:
                    pe.wait_ge(dv("s_new"), HB * b)
                for h in range(HB):
                    last = mm(kvp[:, P * h:P * h + P], ktr[0:TD, h, :], vseq(b)[:, P * h:P * h + P], start=True, stop=True)
                last.then_inc(dv("kv_ps"), 1)

        @block.scalar
        def _(act):
            A = nc.scalar.activation

            def gate_out(n, p):
                act.wait_ge(fr_ps.sem, fr_ps.at(n, p + 1))
                act.wait_ge(u_ps.sem, u_ps.at(n, 2 * p))
                A(ff[:, :], ring[0][:, :], ACT.Sigmoid).then_inc(f_sig.sem, 1)
                A(kk[:, :], ring[0][:, :], ACT.Sigmoid, scale=-1.0).then_inc(k_sig.sem, 1)

            def q_out(n, p):
                act.wait_ge(q_ps.sem, q_ps.at(n, p + 1))
                A(qq[:, :], ring[1][:, :], ACT.Copy).then_inc(q_sb.sem, 1)

            def squares_m(n, j):
                act.wait_ge(e_ps.sem, e_ps.at(n, j + 1))
                act.wait_ge(mgd.sem, mgd.at(n, j + 1))
                A(ring[j % 2][:, :], ring[j % 2][:, :], ACT.Square, accum_out=essq[:, j:j + 1]).then_inc(esq[j % 2].sem, 1)

            def k_out(n, p):
                act.wait_ge(kt_ps.sem, kt_ps.at(n, p + 1))
                A(ktr[:, :, :], aux[p][:, :].rearrange("p (h k) -> p h k", h=4), ACT.Copy).then_inc(kt_sb.sem, 1)

            def squares_o(n, ui):
                act.wait_ge(u_ps.sem, u_ps.at(n, ui + 1))
                for h in range(2):
                    act.wait_ge(usq.sem, usq.at(n, 2 * ui + h))
                    A(junk[:, 512:640], ops[:, P * h:P * h + P], ACT.Square, accum_out=ussq[:, h:h + 1]).then_inc(usq.sem, 1)

            def xa_out(n, p):
                act.wait_ge(xa_ps.sem, xa_ps.at(n, p + 1))
                act.wait_ge(cvc.sem, cvc.at(n, 8 * p))
                act.wait_ge(hl_sv.sem, hl_sv.at(n, p))
                A(xa[:, :, CW - 1:], ring[0][:, :].rearrange("p (c t) -> p c t", c=2), ACT.Copy).then_inc(xa_sb.sem, 1)

            def ga_out(n, p):
                act.wait_ge(ga_ps.sem, ga_ps.at(n, p + 1))
                act.wait_ge(yl_ok.sem, yl_ok.at(n, 0))
                act.wait_ge(yh_ok.sem, yh_ok.at(n, 0))
                A(sil[:, 2 * p:2 * p + 2, :], ring[1][:, :].rearrange("p (c t) -> p c t", c=2), ACT.Silu)\
                    .then_inc(ga_sil.sem, 1)

            def squares_x(m):
                for t in range(NT):
                    act.wait_ge(xld[t].sem, xld[t].at(m + 1, 0))
                    if t == 0:
                        act.wait_ge(xn_ok.sem, xn_ok.at(m, 0))
                    for c in range(2):
                        act.wait_ge(xsq.sem, xsq.at(m, 2 * t + c))
                        A(junk[:, 0:512], xin[:, t, 512 * c:512 * c + 512], ACT.Square,
                          accum_out=xssq[:, 2 * t + c:2 * t + c + 1]).then_inc(xsq.sem, 1)

            def gates_out(n, p):
                act.wait_ge(gr_ps.sem, gr_ps.at(n, p + 1))
                act.wait_ge(iu.sem, iu.at(n, p))
                for c in range(2):
                    A(rr[:, c, :], aux[(1 + p) % 2][:, T * c:T * c + T], ACT.Sigmoid,
                      bias=pcol("ba", 2 * p + c)).then_inc(r_sig.sem, 1)
                act.wait_ge(gi_ps.sem, gi_ps.at(n, p + 1))
                act.wait_ge(scan.sem, scan.at(n, 2 * p))
                for c in range(2):
                    A(ii[:, c, :], aux[p][:, T * c:T * c + T], ACT.Sigmoid, bias=pcol("bx", 2 * p + c)).then_inc(i_sig.sem, 1)

            def decay(n, p):
                act.wait_ge(r_sig.sem, r_sig.at(n, 2 * p + 2))
                for c in range(2):
                    A(aa[:, c, :], rr[:, c, :], ACT.Exp, scale=cneg[:, 2 * p + c:2 * p + c + 1]).then_inc(a_exp.sem, 1)
                for c in range(2):
                    A(rr[:, c, :], rr[:, c, :], ACT.Tanh, scale=cpos[:, 2 * p + c:2 * p + c + 1]).then_inc(th_ok.sem, 1)

            def root(n, p):
                act.wait_ge(gd.sem, gd.at(n, p + 1))
                A(rr[:, :, :], rr[:, :, :], ACT.Sqrt).then_inc(u_sqrt.sem, 1)

            def hn_out(m, j):
                bank = aux[(j + 1) % 2]
                act.wait_ge(tr_ps.sem, tr_ps.at(m, j + 1))
                for i in range(2):
                    k = 2 * j + i
                    A(bank[:, T * i:T * i + T], bank[:, T * i:T * i + T], ACT.Identity, scale=sc1[:, k, 0:1],
                      bias=shf[:, k, 0:1]).then_inc(aff.sem, 1)
                act.wait_ge(aff.sem, aff.at(m, 2 * j + 2))
                A(hnh[:, 2 * j:2 * j + 2, :], bank[:, :].rearrange("p (k t) -> p k t", k=2), ACT.Copy).then_inc(hn_hi.sem, 1)

            def y_turned(n, j):
                act.wait_ge(yt_ps.sem, yt_ps.at(n, j + 1))
                A(yh[:, CT + 2 * j:CT + 2 * j + 2, :], aux[j][:, :].rearrange("p (k t) -> p k t", k=2), ACT.Copy)\
                    .then_inc(yth.sem, 1)

            def body(n, first, last_body):
                if not first:
                    y_turned(n - 1, 0)
                    y_turned(n - 1, 1)
                gate_out(n, 0)
                if not first:
                    root(n - 1, 1)
                q_out(n, 0)
                for t in range(NT):
                    act.wait_ge(iv_ps.sem, iv_ps.at(n, t + 1))
                    A(vv[:, t, :], ring[t][:, :], ACT.Copy).then_inc(v_sb.sem, 1)
                for t in range(NT):
                    act.wait_ge(gb_ps.sem, gb_ps.at(n, t + 1))
                    A(gbs[:, t, :], ring[t][:, :], ACT.Silu).then_inc(gb_sil.sem, 1)
                if not first:
                    squares_m(n - 1, 0)
                k_out(n, 0)
                squares_o(n, 0)
                if not first:
                    squares_m(n - 1, 1)
                squares_o(n, 1)
                if not last_body:
                    squares_x(n + 1)
                gate_out(n, 1)
                q_out(n, 1)
                xa_out(n, 0)
                ga_out(n, 0)
                gates_out(n, 0)
                xa_out(n, 1)
                decay(n, 0)
                ga_out(n, 1)
                root(n, 0)
                if not last_body:
                    for j in range(4):
                        hn_out(n + 1, j)
                if not first:
                    squares_m(n - 1, 2)
                k_out(n, 1)
                gates_out(n, 1)
                squares_o(n, 2)
                if not first:
                    squares_m(n - 1, 3)
                squares_o(n, 3)
                decay(n, 1)

            act.wait_ge(pre_ps, 1)
            A(par[:, :], aux[0][:, 0:NROW], ACT.Copy).then_inc(pre_act, 1)
            act.wait_ge(pre_ps, 2)
            A(xc[:, 0, 0:KT * NS], aux[1][:, 0:KT * NS], ACT.Silu).then_inc(pre_act, 1)
            squares_x(0)
            act.wait_ge(pre_dve, 2)
            A(tmp[:, 1, :], tmp[:, 0, :], ACT.Exp, scale=-1.0).then_inc(w_fold, 1)
            A(tmp[:, 3, :], tmp[:, 2, :], ACT.Exp).then_inc(w_fold, 1)
            act.wait_ge(pre_ps, 3)
            for i in range(2):
                last = A(gp[:, 512 * i:512 * i + 512], lev[i][:, :], ACT.Copy)
            last.then_inc(pre_act, 1)
            for j in range(4):
                hn_out(0, j)
            for i, (kind, c) in enumerate(pieces):
                if kind == "ada":
                    continue
                act.wait_ge(st_ld[i % 2], 16 * (i // 2 + 1))
                s = stage[i % 2]
                if kind == "wo":
                    for h in range(HB):
                        A(s[:, CT + h, :], s[:, CT + h, :], ACT.Copy, scale=pcol("onw", h)).then_inc(w_fold, 1)
                    act.wait_ge(w_fold, 2 + HB * (c + 1))
                dst = wih if kind == "wi" else woh
                A(dst[:, :, 256 * c:256 * c + 256], s, ACT.Copy).then_inc(w_hi, 1)

            body(0, True, False)
            with act.Fori(1, BODIES - 1) as n:
                body(n, False, False)
            body(BODIES - 1, False, True)
            n = BODIES
            y_turned(n - 1, 0)
            y_turned(n - 1, 1)
            root(n - 1, 1)
            for j in range(4):
                squares_m(n - 1, j)

            act.wait_ge(d_ld, 16 * 3)
            for c in range(2):
                if c:
                    act.wait_ge(dv("xsq_d"), 1)
                A(junk[0:TD, 0:512], xin[0:TD, 0, 512 * c:512 * c + 512], ACT.Square, accum_out=xssq[0:TD, c:c + 1])\
                    .then_inc(dv("xsq_d"), 1)
            act.wait_ge(dv("gp_ps"), 1)
            act.wait_ge(mgd.sem, mgd.at(BODIES, 0))
            for i in range(2):
                last = A(gp[0:TD, 512 * i:512 * i + 512], lev[i][0:TD, :], ACT.Copy)
            last.then_inc(dv("gp_sb"), 1)
            act.wait_ge(dv("proj_ps"), 1)
            W4 = CT * TD
            A(xad[:, :, :, CW - 1:], ring[0][:, 0:W4].rearrange("p (c b l) -> p c b l", c=CT, b=NB), ACT.Copy)\
                .then_inc(dv("xa_d"), 1)
            A(sil[:, 0, 0:W4], ring[0][:, W4:2 * W4], ACT.Silu).then_inc(dv("ga_d"), 1)
            A(qq[:, 0:W4], ring[0][:, 2 * W4:3 * W4], ACT.Copy).then_inc(dv("qfk_d"), 1)
            A(ff[:, 0:W4], ring[0][:, 3 * W4:4 * W4], ACT.Sigmoid).then_inc(dv("qfk_d"), 1)
            A(kk[:, 0:W4], ring[0][:, 3 * W4:4 * W4], ACT.Sigmoid, scale=-1.0).then_inc(dv("qfk_d"), 1)
            act.wait_ge(dv("iv_d"), 1)
            A(vv[0:TD, 0, :], ring[1][0:TD, :], ACT.Copy).then_inc(dv("v_d"), 1)
            act.wait_ge(dv("gb_d"), 1)
            A(gbs[0:TD, 0, :], aux[0][0:TD, :], ACT.Silu).then_inc(dv("gb_sb"), 1)
            act.wait_ge(dv("kt_d"), 1)
            A(ktr[0:TD, :, :], aux[1][0:TD, :].rearrange("p (h k) -> p h k", h=HB), ACT.Copy).then_inc(dv("kt_sbd"), 1)
            act.wait_ge(dv("ot_ps"), 1)
            act.wait_ge(dv("level_in"), DLEVELS + 2)
            A(ff[:, 0:W4], ops[:, 0:W4], ACT.Copy).then_inc(dv("ot_sb"), 1)
            act.wait_ge(dv("o_ps"), 1)
            for h in range(HB):
                if h:
                    act.wait_ge(dv("usq_d"), h)
                A(junk[0:TD, 512:640], lev[1][0:TD, P * h:P * h + P], ACT.Square, accum_out=ussq[0:TD, h:h + 1])\
                    .then_inc(dv("usq_d"), 1)
            act.wait_ge(dv("gates_ps"), 1)
            for w, dst, bias in ((0, rrd, "ba"), (1, iid, "bx")):
                for c in range(CT):
                    o = W4 * w + TD * c
                    A(dst[:, TD * c:TD * c + TD], ring[1][:, o:o + TD], ACT.Sigmoid, bias=pcol(bias, c)).then_inc(dv("ri_d"), 1)
            act.wait_ge(dv("ri_d"), 2 * CT)
            for c in range(CT):
                A(aad[:, TD * c:TD * c + TD], rrd[:, TD * c:TD * c + TD], ACT.Exp, scale=cneg[:, c:c + 1]).then_inc(dv("a_d"), 1)
            for c in range(CT):
                A(rrd[:, TD * c:TD * c + TD], rrd[:, TD * c:TD * c + TD], ACT.Tanh, scale=cpos[:, c:c + 1]).then_inc(dv("a_d"), 1)
            act.wait_ge(dv("guard_d"), 1)
            A(rrd, rrd, ACT.Sqrt).then_inc(dv("root_d"), 1)
            for c in range(2):
                act.wait_ge(dv("m_ps"), c + 1)
                act.wait_ge(dv("mg_d"), c + 1)
                A(ring[c][0:TD, :], ring[c][0:TD, :], ACT.Square, accum_out=essq[0:TD, c:c + 1]).then_inc(dv("msq_d"), 1)
            act.wait_ge(dv("rows_ps"), 1)
            A(xin[0:NB * (CW - 1), 0, DA:D], aux[0][0:NB * (CW - 1), :], ACT.Copy).then_inc(dv("rows_sb"), 1)
            A(xin[0:NB, 0, 0:DA], aux[1][0:NB, :], ACT.Copy).then_inc(dv("rows_sb"), 1)
            A(xin[0:CW - 1, 1, DA:D], ops[0:CW - 1, :], ACT.Copy).then_inc(dv("rows_sb"), 1)
            A(xin[0:CT, 1, 0:P], lev[1][0:CT, 0:P], ACT.Copy).then_inc(dv("rows_sb"), 1)

        @block.vector
        def _(dve):
            V = nc.vector

            def rsqrt_steps(w, ssq, out, count, base, s):
                y, v, t = out[:, 0, :], out[:, 1, :], out[:, 2, :]
                k = 0

                def done(ins):
                    nonlocal k
                    k += 1
                    ins.then_inc(s, 1)
                    dve.wait_ge(s, base + k)
                done(V.tensor_scalar(v, ssq, 1.0 / count, EPS, ALU.mult, ALU.add))
                done(V.tensor_scalar(t.bitcast(I32), v.bitcast(I32), 1, None, ALU.logical_shift_right))
                done(V.tensor_scalar(y.bitcast(I32), t.bitcast(I32), -1.0, MAGIC, ALU.mult, ALU.add))
                for _ in range(3):
                    done(V.tensor_tensor(t, y, y, ALU.mult))
                    done(V.scalar_tensor_tensor(t, t, -0.5, v, ALU.mult, ALU.mult))
                    done(V.scalar_tensor_tensor(y, t, 1.5, y, ALU.add, ALU.mult))

            def y_rest(n, j):
                dve.wait_ge(yth.sem, yth.at(n, j + 1))
                V.tensor_tensor(yl[:, CT + 2 * j:CT + 2 * j + 2, :], aux[j][:, :].rearrange("p (k t) -> p k t", k=2),
                                yh[:, CT + 2 * j:CT + 2 * j + 2, :], ALU.subtract).then_inc(ytl.sem, 1)

            def forget(n, p):
                dve.wait_ge(f_af.sem, f_af.at(n, 2 * p + 2))
                V.tensor_scalar_max(ff[:, :], ff[:, :], F_MIN).then_inc(f_ok.sem, 1)

            def take(n, p, l):
                i = p * (LEVELS + 1) + l
                dve.wait_ge(lev_ps.sem, lev_ps.at(n, i + 1))
                if l == 0:
                    dve.wait_ge(u_ps.sem, u_ps.at(n, 2 * p))
                    dve.wait_ge(f_ok.sem, f_ok.at(n, p + 1))
                    V.tensor_tensor(qq[:, :], qq[:, :], ff[:, :], ALU.mult).then_inc(q_f.sem, 1)
                    V.copy_predicated(am[:, :, :], eye[:, :].unsqueeze(1).to_broadcast([P, 4, P]),
                                      lev[i % 2][:, :].rearrange("p (h t) -> p h t", h=4)).then_inc(amask.sem, 1)
                    return
                dve.wait_ge(amask.sem, amask.at(n, i))
                m = 1 << (l - 1)
                nb = 2 * T // (2 * m)
                j = LEVELS * p + l
                if l == 1:
                    dve.wait_ge(q_f.sem, q_f.at(n, p + 1))
                else:
                    dve.wait_ge(q_upd.sem, q_upd.at(n, j - 1))
                    dve.wait_ge(k_upd.sem, k_upd.at(n, j - 1))
                    dve.wait_ge(g_upd.sem, g_upd.at(n, j - 1))
                g = products(m)
                qo, ke = blocks(qq[:, :], m)[:, :, 1, :], blocks(kk[:, :], m)[:, :, 0, :]
                V.tensor_tensor(qo, qo, g[:, :, 0:1].to_broadcast([P, nb, m]), ALU.mult).then_inc(q_upd.sem, 1)
                V.tensor_tensor(ke, ke, g[:, :, 1:2].to_broadcast([P, nb, m]), ALU.mult).then_inc(k_upd.sem, 1)
                o = goff(2 * m)
                V.tensor_tensor(gg[:, o:o + nb], g[:, :, 0], g[:, :, 1], ALU.mult).then_inc(g_upd.sem, 1)
                a = am[:, :, :].rearrange("p h (b two m) -> p h b two m", two=2, m=m)
                x = lev[i % 2][:, 0:256].rearrange("p (h b m) -> p h b m", h=4, m=m)
                msk = lmask[:, l - 1, :].rearrange("p (b m) -> p b m", m=m).unsqueeze(1).to_broadcast([P, 4, P // (2 * m), m])
                V.copy_predicated(a[:, :, :, 1, :], msk, x).then_inc(amask.sem, 1)

            def state(n, p, c):
                ui = 2 * p + c
                dve.wait_ge(u_ps.sem, u_ps.at(n, ui + 1))
                dve.wait_ge(g_upd.sem, g_upd.at(n, LEVELS * p + LEVELS))
                dve.wait_ge(s_upd.sem, s_upd.at(n, 2 * ui))
                for h in range(2):
                    hd, o = 2 * p + h, goff(P) + 2 * h + c
                    V.scalar_tensor_tensor(st[:, hd, :], st[:, hd, :], gg[:, o:o + 1], kvp[:, P * h:P * h + P],
                                           ALU.mult, ALU.add).then_inc(s_upd.sem, 1)

            def rows(n, p, c):
                ui = 2 * p + c
                dve.wait_ge(usq.sem, usq.at(n, 2 * ui + 2))
                rsqrt_steps(2, ussq[:, 0:2], urs[:, :, 0:2], P, newt_u.at(n, NEWTON * ui), newt_u.sem)
                dve.wait_ge(gb_sil.sem, gb_sil.at(n, c + 1))
                for h in range(2):
                    y = gbs[:, c, P * (2 * p + h):P * (2 * p + h) + P]
                    V.scalar_tensor_tensor(y, ops[:, P * h:P * h + P], urs[:, 0, h:h + 1], y, ALU.mult, ALU.mult)\
                        .then_inc(yb_ok.sem, 1)

            def m_out(n, j):
                dve.wait_ge(e_ps.sem, e_ps.at(n, j + 1))
                if j == 2:
                    dve.wait_ge(eo.sem, eo.at(n, 1))
                c = j % 2
                V.tensor_tensor(mg[:, 512 * c:512 * c + 512], ring[c][:, :], gp[:, 512 * c:512 * c + 512], ALU.mult)\
                    .then_inc(mgd.sem, 1)

            def x_out(n, t):
                for c in range(2):
                    dve.wait_ge(esq[c].sem, esq[c].at(n, t + 1))
                base = newt_e.at(n, (NEWTON + 1) * t)
                V.tensor_tensor(essq[:, 2 * t:2 * t + 1], essq[:, 2 * t:2 * t + 1], essq[:, 2 * t + 1:2 * t + 2], ALU.add)\
                    .then_inc(newt_e.sem, 1)
                dve.wait_ge(newt_e.sem, base + 1)
                rsqrt_steps(1, essq[:, 2 * t:2 * t + 1], ers, D, base + 1, newt_e.sem)
                dve.wait_ge(mgd.sem, mgd.at(n, 2 * t + 2))
                dve.wait_ge(xrl.sem, xrl.at(n, 16 * t + 16))
                V.scalar_tensor_tensor(xr, mg, ers[:, 0, 0:1], xr, ALU.mult, ALU.add).then_inc(eo.sem, 1)

            def conv(n, p):
                dve.wait_ge(xa_sb.sem, xa_sb.at(n, p + 1))
                dve.wait_ge(hl_in.sem, hl_in.at(n, p + 1))
                dve.wait_ge(hst_ok.sem, hst_ok.at(n, p))
                dve.wait_ge(y_ok.sem, y_ok.at(n, p))
                for j in range(CW):
                    if j:
                        dve.wait_ge(cvc.sem, cvc.at(n, 8 * p + 2 * j))
                    for c in range(2):
                        src, w = xa[:, c, j:j + T], pcol("cw", CT * j + 2 * p + c)
                        if j == 0:
                            V.tensor_scalar(xc[:, c, :], src, w, pcol("cb", 2 * p + c), ALU.mult, ALU.add).then_inc(cvc.sem, 1)
                        else:
                            V.scalar_tensor_tensor(xc[:, c, :], src, w, xc[:, c, :], ALU.mult, ALU.add).then_inc(cvc.sem, 1)

            def input_scale(n, p):
                dve.wait_ge(a_sq.sem, a_sq.at(n, p + 1))
                dve.wait_ge(th_ok.sem, th_ok.at(n, 2 * p + 2))
                V.scalar_tensor_tensor(rr[:, :, :], xc[:, :, :], 1.0, rr[:, :, :], ALU.add, ALU.mult).then_inc(rx.sem, 1)
                dve.wait_ge(rx.sem, rx.at(n, p + 1))
                V.tensor_scalar_max(rr[:, :, :], rr[:, :, :], 0.0).then_inc(gd.sem, 1)

            def recur(n, p):
                dve.wait_ge(u_sqrt.sem, u_sqrt.at(n, p + 1))
                dve.wait_ge(ix_ok.sem, ix_ok.at(n, p + 1))
                V.tensor_tensor(ii[:, :, :], rr[:, :, :], ii[:, :, :], ALU.mult).then_inc(iu.sem, 1)
                dve.wait_ge(iu.sem, iu.at(n, p + 1))
                for c in range(2):
                    V.tensor_tensor_scan(xc[:, c, :], aa[:, c, :], ii[:, c, :], hst[:, 2 * p + c:2 * p + c + 1],
                                         ALU.mult, ALU.add).then_inc(scan.sem, 1)
                dve.wait_ge(scan.sem, scan.at(n, 2 * p + 2))
                dve.wait_ge(ga_sil.sem, ga_sil.at(n, p + 1))
                s = sil[:, 2 * p:2 * p + 2, :]
                V.tensor_tensor(s, xc[:, :, :], s, ALU.mult).then_inc(y_ok.sem, 1)

            def y_split(n):
                dve.wait_ge(yh_ok.sem, yh_ok.at(n, 1))
                V.tensor_tensor(yl[:, 0:CT, :], sil[:, :, :], yh[:, 0:CT, :], ALU.subtract).then_inc(yl_ok.sem, 1)

            def x_norm(m):
                dve.wait_ge(xsq.sem, xsq.at(m, 4))
                base = newt_x.at(m, 0)
                pairs = xssq[:, :].rearrange("p (t c) -> p t c", c=2)
                V.tensor_tensor(xssq[:, 0:2], pairs[:, :, 0], pairs[:, :, 1], ALU.add).then_inc(newt_x.sem, 1)
                dve.wait_ge(newt_x.sem, base + 1)
                rsqrt_steps(2, xssq[:, 0:2], xrs, D, base + 1, newt_x.sem)
                for t in range(NT):
                    V.tensor_scalar(xin[:, t, :], xin[:, t, :], xrs[:, 0, t:t + 1], None, ALU.mult).then_inc(xn_ok.sem, 1)

            def hn_rest(m, j):
                dve.wait_ge(hn_hi.sem, hn_hi.at(m, j + 1))
                V.tensor_tensor(hnl[:, 2 * j:2 * j + 2, :], aux[(j + 1) % 2][:, :].rearrange("p (k t) -> p k t", k=2),
                                hnh[:, 2 * j:2 * j + 2, :], ALU.subtract).then_inc(hn_lo.sem, 1)

            def body(n, first, last_body):
                if not first:
                    y_rest(n - 1, 0)
                    y_rest(n - 1, 1)
                    input_scale(n - 1, 1)
                forget(n, 0)
                if not first:
                    recur(n - 1, 1)
                    y_split(n - 1)
                for l in range(LEVELS + 1):
                    take(n, 0, l)
                if not first:
                    m_out(n - 1, 0)
                state(n, 0, 0)
                rows(n, 0, 0)
                if not first:
                    m_out(n - 1, 1)
                state(n, 0, 1)
                rows(n, 0, 1)
                if not first:
                    x_out(n - 1, 0)
                forget(n, 1)
                take(n, 1, 0)
                conv(n, 0)
                take(n, 1, 1)
                take(n, 1, 2)
                if not last_body:
                    x_norm(n + 1)
                take(n, 1, 3)
                take(n, 1, 4)
                take(n, 1, 5)
                input_scale(n, 0)
                take(n, 1, 6)
                recur(n, 0)
                conv(n, 1)
                if not last_body:
                    hn_rest(n + 1, 0)
                    hn_rest(n + 1, 1)
                take(n, 1, 7)
                if not last_body:
                    hn_rest(n + 1, 2)
                    hn_rest(n + 1, 3)
                if not first:
                    m_out(n - 1, 2)
                state(n, 1, 0)
                rows(n, 1, 0)
                if not first:
                    m_out(n - 1, 3)
                state(n, 1, 1)
                rows(n, 1, 1)
                if not first:
                    x_out(n - 1, 1)

            chain = [0]

            def link(ins):
                chain[0] += 1
                ins.then_inc(consts_dve, 1)
                dve.wait_ge(consts_dve, chain[0])

            dve.wait_ge(pre_act, 1)
            lam, lbl = par[:, ROW["lam"]:ROW["lam"] + CT], par[:, ROW["lbl"]:ROW["lbl"] + CT]
            link(V.tensor_scalar(tmp[:, 4, :], lam, -1.0, None, ALU.mult))
            link(V.tensor_tensor(tmp[:, 0, :], lam, tmp[:, 4, :], ALU.max))
            link(V.tensor_tensor(tmp[:, 2, :], lbl, lbl, ALU.subtract))
            x_norm(0)
            dve.wait_ge(ada_ps, NADA)
            adab = par[:, ROW["adab"]:ROW["adab"] + 3 * KT].unsqueeze(2).to_broadcast([P, 3 * KT, NS])
            mod = ops[:, 0:3 * KT * NS].rearrange("p (k s) -> p k s", s=NS)
            for i, dst in enumerate((shf, sc1, gpt)):
                link(V.tensor_tensor(dst[:, :, :], mod[:, KT * i:KT * i + KT, :], adab[:, KT * i:KT * i + KT, :], ALU.add))
            pre = par[:, ROW["pre"]:ROW["pre"] + KT].unsqueeze(2).to_broadcast([P, KT, NS])
            post = par[:, ROW["post"]:ROW["post"] + KT].unsqueeze(2).to_broadcast([P, KT, NS])
            link(V.scalar_tensor_tensor(sc1[:, :, :], sc1[:, :, :], 1.0, pre, ALU.add, ALU.mult))
            V.tensor_tensor(gpt[:, :, :], gpt[:, :, :], post, ALU.mult).then_inc(pre_dve, 1)
            link(V.memset(st[:, :, :], 0.0))
            V.memset(tmp[:, 5, :], 0.0).then_inc(pre_dve, 1)
            dve.wait_ge(w_fold, 2)
            e, z, z2, s = tmp[:, 1, :], tmp[:, 5, :], tmp[:, 6, :], tmp[:, 7, :]
            dve.wait_ge(pre_dve, 2)
            link(V.tensor_scalar(s, e, 2.0, None, ALU.add))
            link(V.reciprocal(s, s))
            link(V.tensor_tensor(z, e, s, ALU.mult))
            link(V.tensor_tensor(z2, z, z, ALU.mult))
            link(V.tensor_scalar(s, z2, 1.0 / 17, None, ALU.mult))
            for d in (15, 13, 11, 9, 7, 5, 3):
                link(V.scalar_tensor_tensor(s, s, 1.0 / d, z2, ALU.add, ALU.mult))
            link(V.scalar_tensor_tensor(s, s, 1.0, z, ALU.add, ALU.mult))
            link(V.tensor_scalar(tmp[:, 4, :], tmp[:, 4, :], 0.0, None, ALU.max))
            link(V.scalar_tensor_tensor(s, s, 2.0, tmp[:, 4, :], ALU.mult, ALU.add))
            link(V.tensor_scalar(cpos[:, :], s, C_RGLRU, None, ALU.mult))
            link(V.tensor_scalar(cneg[:, :], s, -C_RGLRU, None, ALU.mult))
            link(V.reciprocal(s, tmp[:, 3, :]))
            link(V.tensor_tensor(s, tmp[:, 3, :], s, ALU.mult))
            link(V.tensor_tensor(lb[:, :], s, s, ALU.subtract))
            link(V.tensor_scalar(omlb[:, :], lb[:, :], -1.0, 1.0, ALU.mult, ALU.add))
            V.memset(halo[:, :, :], 0.0).then_inc(pre_dve, 1)
            for j in range(4):
                hn_rest(0, j)
            for i, (kind, c) in enumerate(pieces):
                if kind == "ada":
                    continue
                dst_h, dst_l = (wih, wil) if kind == "wi" else (woh, wol)
                dve.wait_ge(w_hi, c + 1 if kind == "wi" else NWI + c + 1)
                cols = slice(256 * c, 256 * c + 256)
                V.tensor_tensor(dst_l[:, :, cols], stage[i % 2], dst_h[:, :, cols], ALU.subtract).then_inc(w_lo, 1)
            dve.wait_ge(zeroed, 3)

            body(0, True, False)
            with dve.Fori(1, BODIES - 1) as n:
                body(n, False, False)
            body(BODIES - 1, False, True)
            n = BODIES
            y_rest(n - 1, 0)
            y_rest(n - 1, 1)
            input_scale(n - 1, 1)
            recur(n - 1, 1)
            y_split(n - 1)
            m_out(n - 1, 0)
            m_out(n - 1, 1)
            x_out(n - 1, 0)
            m_out(n - 1, 2)
            m_out(n - 1, 3)
            x_out(n - 1, 1)

            W4 = CT * TD
            dve.wait_ge(u_ps.sem, u_ps.at(BODIES, 0))
            link(V.memset(am[0:TD, :, 0:TD], 0.0))
            dve.wait_ge(scan.sem, scan.at(BODIES, 0))
            V.tensor_copy(aa[:, 1, :].rearrange("p (k b l) -> p k b l", k=KT, b=NB),
                          gpt[:, :, 1:].unsqueeze(3).to_broadcast([P, KT, NB, NL])).then_inc(dv("gprow"), 1)
            dve.wait_ge(dv("xsq_d"), 2)
            link(V.tensor_tensor(xssq[0:TD, 0:1], xssq[0:TD, 0:1], xssq[0:TD, 1:2], ALU.add))
            rsqrt_steps(1, xssq[0:TD, 0:1], xrs[0:TD, :, 0:1], D, 0, dv("newt_xd"))
            V.tensor_scalar(xin[0:TD, 0, :], xin[0:TD, 0, :], xrs[0:TD, 0, 0:1], None, ALU.mult).then_inc(dv("xn"), 1)
            dve.wait_ge(dv("turned"), 1)
            hx = rr[:, :, :].rearrange("p c t -> p (c t)")[:, 0:KT * TD]
            hx4 = hx.rearrange("p (k b l) -> p k b l", k=KT, b=NB)
            hx3 = hx.rearrange("p (k t) -> p k t", k=KT)
            seqs = lambda t: t[:, :, 1:].unsqueeze(3).to_broadcast([P, KT, NB, NL])
            link(V.tensor_tensor(hx4, aux[0][:, 0:KT * TD].rearrange("p (k b l) -> p k b l", k=KT, b=NB), seqs(sc1), ALU.mult))
            link(V.tensor_tensor(hx4, hx4, seqs(shf), ALU.add))
            link(V.tensor_copy(hnh[:, :, 0:TD], hx3))
            V.tensor_tensor(hnl[:, :, 0:TD], hx3, hnh[:, :, 0:TD], ALU.subtract).then_inc(dv("hn"), 1)
            V.tensor_copy(h0, aux[1][:, 0:TD]).then_inc(dv("carried"), 1)
            nj = NB * (CW - 1)
            V.tensor_copy(xad[:, :, :, 0:CW - 1],
                          aux[1][:, TD:TD + CT * nj].rearrange("p (c b j) -> p c b j", c=CT, b=NB)).then_inc(dv("carried"), 1)
            dve.wait_ge(dv("qfk_d"), 3)
            heads = lambda t: t[:, 0:W4].rearrange("p (h t) -> p h t", h=HB)
            percol = lambda t: t[:, :].unsqueeze(2).to_broadcast([P, HB, TD])
            link(V.tensor_tensor(heads(ff), heads(ff), percol(omlb), ALU.mult))
            link(V.tensor_tensor(heads(ff), heads(ff), percol(lb), ALU.add))
            link(V.tensor_scalar_max(ff[:, 0:W4], ff[:, 0:W4], F_MIN))
            V.tensor_tensor(heads(kk), heads(kk), percol(omlb), ALU.mult).then_inc(dv("level_in"), 1)
            dve.wait_ge(dv("level_in"), 1)
            for l in range(DLEVELS + 1):
                dve.wait_ge(dv("level_ps"), l + 1)
                if l == 0:
                    V.copy_predicated(am[0:TD, :, 0:TD], eye[0:TD, 0:TD].unsqueeze(1).to_broadcast([TD, HB, TD]),
                                      lev[0][0:TD, 0:W4].rearrange("p (h t) -> p h t", h=HB)).then_inc(dv("masked"), 1)
                    V.tensor_tensor(qq[:, 0:W4], qq[:, 0:W4], ff[:, 0:W4], ALU.mult).then_inc(dv("level_in"), 1)
                    dve.wait_ge(dv("level_in"), 2)
                    continue
                m = 1 << (l - 1)
                g = (ff[:, 0:W4] if m == 1 else gg[:, 0:W4 // 2]).rearrange("p (b two) -> p b two", two=2)
                nb = W4 // (2 * m)
                a = am[0:TD, :, 0:TD].rearrange("p h (b two m) -> p h b two m", two=2, m=m)
                x = lev[l % 2][0:TD, 0:W4 // 2].rearrange("p (h b m) -> p h b m", h=HB, m=m)
                msk = lmask[0:TD, l - 1, 0:TD // 2].rearrange("p (b m) -> p b m", m=m).unsqueeze(1)\
                    .to_broadcast([TD, HB, TD // (2 * m), m])
                dve.wait_ge(dv("masked"), l)
                V.copy_predicated(a[:, :, :, 1, :], msk, x).then_inc(dv("masked"), 1)
                qo, ke = blocks(qq[:, 0:W4], m)[:, :, 1, :], blocks(kk[:, 0:W4], m)[:, :, 0, :]
                link(V.tensor_tensor(qo, qo, g[:, :, 0:1].to_broadcast([P, nb, m]), ALU.mult))
                link(V.tensor_tensor(gg[:, (m - 1) * W4 // 2:(m - 1) * W4 // 2 + nb], g[:, :, 0], g[:, :, 1], ALU.mult))
                V.tensor_tensor(ke, ke, g[:, :, 1:2].to_broadcast([P, nb, m]), ALU.mult).then_inc(dv("level_in"), 1)
                dve.wait_ge(dv("level_in"), l + 2)
            g4 = gg[:, W4 // 2:W4 // 2 + HB * NB]
            dve.wait_ge(dv("xa_d"), 1)
            dve.wait_ge(dv("carried"), 2)
            for j in range(CW):
                for c in range(CT):
                    src, w = xad[:, c, :, j:j + NL], pcol("cw", CT * j + c)
                    dst = xcd[:, TD * c:TD * c + TD].rearrange("p (b l) -> p b l", b=NB)
                    if j == 0:
                        V.tensor_scalar(dst, src, w, pcol("cb", c), ALU.mult, ALU.add).then_inc(dv("conv_d"), 1)
                    else:
                        V.scalar_tensor_tensor(dst, src, w, dst, ALU.mult, ALU.add).then_inc(dv("conv_d"), 1)
                dve.wait_ge(dv("conv_d"), CT * (j + 1))
            link(V.tensor_copy(halod.rearrange("p (c b j) -> p c b j", c=CT, b=NB), xad[:, :, :, NL:]))
            dve.wait_ge(dv("usq_d"), HB)
            rsqrt_steps(HB, ussq[0:TD, :], urs[0:TD, :, :], P, 0, dv("newt_ud"))
            dve.wait_ge(dv("gb_sb"), 1)
            for h in range(HB):
                y = gbs[0:TD, 0, P * h:P * h + P]
                V.scalar_tensor_tensor(y, lev[1][0:TD, P * h:P * h + P], urs[0:TD, 0, h:h + 1], y, ALU.mult, ALU.mult)\
                    .then_inc(dv("yb_d"), 1)
            dve.wait_ge(dv("a_d"), 2 * CT)
            dve.wait_ge(dv("ri_d"), 2 * CT)
            link(V.tensor_tensor(iid, iid, xcd, ALU.mult))
            link(V.tensor_tensor(xcd, aad, aad, ALU.mult))
            link(V.scalar_tensor_tensor(rrd, xcd, 1.0, rrd, ALU.add, ALU.mult))
            V.tensor_scalar_max(rrd, rrd, 0.0).then_inc(dv("guard_d"), 1)
            dve.wait_ge(dv("root_d"), 1)
            link(V.tensor_tensor(iid, iid, rrd, ALU.mult))
            a0, u0 = (t.rearrange("p (s l) -> p s l", l=NL)[:, :, 0] for t in (aad, iid))
            link(V.tensor_tensor(h0, h0, a0, ALU.mult))
            link(V.tensor_tensor(u0, u0, h0, ALU.add))
            link(V.memset(a0, 0.0))
            link(V.tensor_tensor_scan(xcd, aad, iid, 0.0, ALU.mult, ALU.add))
            link(V.tensor_copy(hnew, xcd.rearrange("p (s l) -> p s l", l=NL)[:, :, NL - 1]))
            dve.wait_ge(dv("ga_d"), 1)
            yd = sil[:, 0, 0:W4]
            link(V.tensor_tensor(yd, xcd, yd, ALU.mult))
            V.tensor_copy(yh[:, 0:CT, 0:TD], yd.rearrange("p (c t) -> p c t", c=CT)).then_inc(dv("y_dec"), 1)
            dve.wait_ge(dv("y_dec"), 1)
            V.tensor_tensor(yl[:, 0:CT, 0:TD], yd.rearrange("p (c t) -> p c t", c=CT), yh[:, 0:CT, 0:TD], ALU.subtract)\
                .then_inc(dv("y_dec"), 1)
            dve.wait_ge(dv("ybt_ps"), 1)
            src = lev[0][:, 0:W4].rearrange("p (c t) -> p c t", c=CT)
            V.tensor_copy(yh[:, CT:, 0:TD], src).then_inc(dv("y_dec"), 1)
            dve.wait_ge(dv("y_dec"), 3)
            V.tensor_tensor(yl[:, CT:, 0:TD], src, yh[:, CT:, 0:TD], ALU.subtract).then_inc(dv("y_dec"), 1)
            for c in range(2):
                dve.wait_ge(dv("m_ps"), c + 1)
                V.tensor_tensor(mg[0:TD, 512 * c:512 * c + 512], ring[c][0:TD, :], gp[0:TD, 512 * c:512 * c + 512], ALU.mult)\
                    .then_inc(dv("mg_d"), 1)
            dve.wait_ge(dv("msq_d"), 2)
            link(V.tensor_tensor(essq[0:TD, 0:1], essq[0:TD, 0:1], essq[0:TD, 1:2], ALU.add))
            rsqrt_steps(1, essq[0:TD, 0:1], ers[0:TD, :, :], D, 0, dv("newt_md"))
            dve.wait_ge(dv("mg_d"), 2)
            dve.wait_ge(dv("xres"), 16)
            V.scalar_tensor_tensor(xr[0:TD, :], mg[0:TD, :], ers[0:TD, 0, 0:1], xr[0:TD, :], ALU.mult, ALU.add)\
                .then_inc(dv("y_rows"), 1)
            for b in range(NB):
                dve.wait_ge(dv("kv_ps"), b + 1)
                for h in range(HB):
                    s_ = s0[:, b, P * h:P * h + P]
                    V.scalar_tensor_tensor(s_, s_, g4[:, NB * h + b:NB * h + b + 1], kvp[:, P * h:P * h + P], ALU.mult, ALU.add)\
                        .then_inc(dv("s_new"), 1)

        @block.gpsimd
        def _(pool):
            G = nc.gpsimd

            def copy(out, src):
                ones = one[:, 0:1]
                for _ in range(len(src.shape) - 2):
                    ones = ones.unsqueeze(1)
                return G.tensor_tensor(out, src, ones.to_broadcast(list(src.shape)), ALU.mult)

            def bounds(n, p):
                pool.wait_ge(k_sig.sem, k_sig.at(n, p + 1))
                for h in range(2):
                    hd, cols = 2 * p + h, slice(T * h, T * h + T)
                    G.tensor_tensor(kk[:, cols], kk[:, cols], omlb[:, hd:hd + 1].to_broadcast([P, T]), ALU.mult)\
                        .then_inc(k_ok.sem, 1)
                for h in range(2):
                    hd, cols = 2 * p + h, slice(T * h, T * h + T)
                    G.tensor_scalar(ff[:, cols], ff[:, cols], omlb[:, hd:hd + 1], lb[:, hd:hd + 1], ALU.mult, ALU.add)\
                        .then_inc(f_af.sem, 1)

            def halo_in(n, p):
                pool.wait_ge(cvc.sem, cvc.at(n, 8 * p))
                pool.wait_ge(hl_sv.sem, hl_sv.at(n, p))
                copy(xa[:, :, 0:CW - 1], halo[:, 2 * p:2 * p + 2, :]).then_inc(hl_in.sem, 1)

            def halo_save(n, p):
                pool.wait_ge(xa_sb.sem, xa_sb.at(n, p + 1))
                pool.wait_ge(hl_in.sem, hl_in.at(n, p + 1))
                copy(halo[:, 2 * p:2 * p + 2, :], xa[:, :, T:T + CW - 1]).then_inc(hl_sv.sem, 1)

            def gated(n, p):
                pool.wait_ge(i_sig.sem, i_sig.at(n, 2 * p + 2))
                G.tensor_tensor(ii[:, :, :], ii[:, :, :], xc[:, :, :], ALU.mult).then_inc(ix_ok.sem, 1)
                pool.wait_ge(a_exp.sem, a_exp.at(n, 2 * p + 2))
                pool.wait_ge(ix_ok.sem, ix_ok.at(n, p + 1))
                G.tensor_tensor(xc[:, :, :], aa[:, :, :], aa[:, :, :], ALU.mult).then_inc(a_sq.sem, 1)

            def h_save(n, p):
                pool.wait_ge(scan.sem, scan.at(n, 2 * p + 2))
                copy(hst[:, 2 * p:2 * p + 2], xc[:, :, T - 1]).then_inc(hst_ok.sem, 1)

            def y_head(n):
                pool.wait_ge(y_ok.sem, y_ok.at(n, 2))
                pool.wait_ge(u_ps.sem, u_ps.at(n, 4))
                copy(yh[:, 0:CT, :], sil[:, :, :]).then_inc(yh_ok.sem, 1)

            def body(n, first):
                bounds(n, 0)
                if not first:
                    h_save(n - 1, 1)
                    y_head(n - 1)
                halo_in(n, 0)
                bounds(n, 1)
                halo_save(n, 0)
                gated(n, 0)
                halo_in(n, 1)
                h_save(n, 0)
                halo_save(n, 1)
                gated(n, 1)

            gc = [0]

            def link(ins):
                gc[0] += 1
                ins.then_inc(consts_pool, 1)
                pool.wait_ge(consts_pool, gc[0])

            link(G.memset(one[:, :], 1.0))
            link(G.memset(ident[:, :], 0.0))
            G.affine_select(out=ident[:, :], in_=ident[:, :], pattern=[[-1, P]], compare_op=ALU.not_equal, fill=1.0,
                            base=0, channel_multiplier=1).then_inc(consts, 1)
            G.memset(wg[:, :, :, :], 0.0).then_inc(zeroed, 1)
            pool.wait_ge(consts, 1)
            link(G.tensor_copy(eye[:, :], ident[:, :]))
            mf = ktr[:, 0, 0:P // 2]
            for l in range(LEVELS):
                m = 1 << l
                v = mf.rearrange("p (b m) -> p b m", m=m)
                pat = [[-2 * m, P // (2 * m)], [0, m]]
                link(G.memset(mf, 1.0))
                link(G.affine_select(out=v, in_=v, pattern=pat, compare_op=ALU.is_ge, fill=0.0, base=0, channel_multiplier=1))
                link(G.affine_select(out=v, in_=v, pattern=[[2 * m, P // (2 * m)], [0, m]], compare_op=ALU.is_ge, fill=0.0,
                                     base=m - 1, channel_multiplier=-1))
                link(G.tensor_copy(lmask[:, l, :], mf))
            sm = ktr[0:TD, 1, 0:NB]
            link(G.memset(sm, 1.0))
            link(G.affine_select(out=sm, in_=sm, pattern=[[-NL, NB]], compare_op=ALU.is_ge, fill=0.0, base=0, channel_multiplier=1))
            link(G.affine_select(out=sm, in_=sm, pattern=[[NL, NB]], compare_op=ALU.is_ge, fill=0.0, base=NL - 1,
                                 channel_multiplier=-1))
            link(G.tensor_copy(smask[:, :], sm))
            G.memset(hst[:, :], 0.0).then_inc(zeroed, 1)
            pool.wait_ge(pre_ps, 1)
            G.memset(am[:, :, :], 0.0).then_inc(zeroed, 1)
            pool.wait_ge(pre_dve, 3)

            body(0, True)
            with pool.Fori(1, BODIES - 1) as n:
                body(n, False)
            body(BODIES - 1, False)
            h_save(BODIES - 1, 1)
            y_head(BODIES - 1)
            pool.wait_ge(dv("v_d"), 1)
            pool.wait_ge(dv("gb_sb"), 1)
            for b in range(NB):
                if b >= 2:
                    pool.wait_ge(dv("kv_ps"), b - 1)
                G.tensor_scalar(vseq(b), vv[0:TD, 0, :], smask[:, b:b + 1], None, ALU.mult).then_inc(dv("v_seq"), 1)


_INS = ['x_prompt', 'x_sample', 'state_rglru_h', 'state_rglru_conv', 'state_hgrn_S', 'c_prompt', 'c_sample', 'ada_w',
        'ada_b', 'pre_norm_w', 'post_norm_w', 'w_in', 'conv_w', 'conv_b', 'rg_wa', 'rg_ba', 'rg_wx', 'rg_bx',
        'rg_lambda', 'hg_lb_logits', 'hg_onorm_w', 'w_out']
_OUTS = [(1, SEQ, D), (NB, NL, D), (1, 1, DA), (1, 1, CW - 1, DA), (1, 1, HB, P, P), (1, NB, DA), (1, NB, CW - 1, DA),
         (1, NB, HB, P, P)]


def kernel(**inputs):
    import numpy as _np
    import concourse.bacc as _bacc
    from concourse import mybir as _mybir
    from concourse.bass_utils import run_bass_kernel_spmd as _run

    nc = _bacc.Bacc("TRN2", target_bir_lowering=False, num_devices=1)
    arrays, args = {}, []
    for name in _INS:
        a = _np.ascontiguousarray(inputs[name])
        arrays[f"in_{name}_dram"] = a
        args.append(nc.dram_tensor(f"in_{name}_dram", a.shape, _mybir.dt.from_np(a.dtype), kind="ExternalInput").ap())
    for i, shape in enumerate(_OUTS):
        args.append(nc.dram_tensor(f"out_{i}_dram", shape, _mybir.dt.float32, kind="ExternalOutput").ap())
    build(nc, *args)
    r = _run(nc, [arrays], core_ids=[0])
    return tuple(r.results[0][f"out_{i}_dram"] for i in range(len(_OUTS)))
```

```python
from contextlib import ExitStack

import concourse.bass as bass
from concourse import mybir

F32 = mybir.dt.float32
BF16 = mybir.dt.bfloat16
F16 = mybir.dt.float16
U8 = mybir.dt.uint8
I32 = mybir.dt.int32
ALU = mybir.AluOpType
ACT = mybir.ActivationFunctionType

P = 128
D = 1024
KT = D // P
DA = 512
CT = DA // P
HB = 4
PIN = 2 * DA + 4 * DA
SEQ = 2048
T = 256
NT = T // P
BODIES = SEQ // T
CW = 4
NB, NL = 8, 4
TD = NB * NL
NS = 1 + NB
EPS = 1e-6
F_MIN = 1e-30
C_RGLRU = 8.0
LEVELS = 7
DLEVELS = 2
NEWTON = 12
MAGIC = float(0x5F3759DF)

XA, GA, Q_, FR, IV, GB = (i * DA for i in range(6))
ROW = {}
_at = 0
for _name, _n in (("pre", KT), ("post", KT), ("cw", CW * CT), ("cb", CT), ("ba", CT), ("bx", CT), ("lam", CT),
                  ("lbl", CT), ("onw", CT), ("adab", 3 * KT)):
    ROW[_name] = _at
    _at += _n
NROW = _at


def build(nc, x_prompt, x_sample, state_rglru_h, state_rglru_conv, state_hgrn_S, c_prompt, c_sample, ada_w, ada_b,
          pre_norm_w, post_norm_w, w_in, conv_w, conv_b, rg_wa, rg_ba, rg_wx, rg_bx, rg_lambda, hg_lb_logits,
          hg_onorm_w, w_out, y_prompt, y_sample, h_prompt, conv_prompt, S_prompt, h_sample, conv_sample, S_sample):
    with ExitStack() as ctx:
        def sb(name, shape, dt=F32):
            return ctx.enter_context(nc.sbuf_tensor(name, shape, dt))

        def sem(name):
            return ctx.enter_context(nc.semaphore(name))

        wih = sb("wih", [P, KT, PIN], F16)
        wil = sb("wil", [P, KT, PIN], BF16)
        woh = sb("woh", [P, KT, D], F16)
        wol = sb("wol", [P, KT, D], BF16)
        work = sb("work", [P, 4096])
        halves = lambda t: [t[:, 2048 * i:2048 * i + 2048].rearrange("p (k n) -> p k n", k=KT)
                            for i in range(t.shape[1] // 2048)]
        as_f32 = lambda t: t[:, :, :].rearrange("p k n -> p (k n)").bitcast(F32)
        stage = halves(work[:, :]) + halves(as_f32(woh)) + halves(as_f32(wol))
        early = halves(as_f32(wil))[0:2]
        xr = work[:, 0:D]
        mg = work[:, D:2 * D]
        yh = work[:, 2048:3072].bitcast(BF16).rearrange("p (k t) -> p k t", k=KT)
        yl = work[:, 3072:4096].bitcast(F16).rearrange("p (k t) -> p k t", k=KT)
        hnh = sb("hnh", [P, KT, T], BF16)
        hnl = sb("hnl", [P, KT, T], F16)
        xin = sb("xin", [P, NT, D])
        gp = sb("gp", [P, D])
        xa = sb("xa", [P, 2, T + CW - 1])
        halo = sb("halo", [P, CT, CW - 1])
        xc = sb("xc", [P, 2, T])
        rr = sb("rr", [P, 2, T])
        ii = sb("ii", [P, 2, T])
        aa = sb("aa", [P, 2, T])
        sil = sb("sil", [P, CT, T])
        wg = sb("wg", [P, 2, CT, P])
        qq = sb("qq", [P, 2 * T])
        kk = sb("kk", [P, 2 * T])
        ff = sb("ff", [P, 2 * T])
        gg = sb("gg", [P, 2 * T - 4])
        am = sb("am", [P, 4, P])
        ktr = sb("ktr", [P, 4, P])
        vv = sb("vv", [P, NT, DA])
        gbs = sb("gbs", [P, NT, DA])
        st = sb("st", [P, HB, P])
        ident = sb("ident", [P, P])
        eye = sb("eye", [P, P], U8)
        lmask = sb("lmask", [P, LEVELS, P // 2], U8)
        smask = sb("smask", [TD, NB])
        junk = sb("junk", [P, 640], BF16)
        cols = sb("cols", [P, 5 * CT])
        lb, omlb, cneg, cpos, hst = (cols[:, CT * i:CT * i + CT] for i in range(5))
        tmp = xc[:, 1, 0:8 * CT].rearrange("p (a b) -> p a b", b=CT)
        par = sb("par", [P, NROW])
        sc1 = sb("sc1", [P, KT, NS])
        shf = sb("shf", [P, KT, NS])
        gpt = sb("gpt", [P, KT, NS])
        stat = sb("stat", [P, 35])
        ussq, essq, xssq, one = stat[:, 0:4], stat[:, 4:8], stat[:, 8:12], stat[:, 33:34]
        urs = stat[:, 12:24].rearrange("p (a b) -> p a b", a=3)
        ers = stat[:, 24:27].rearrange("p (a b) -> p a b", a=3)
        xrs = stat[:, 27:33].rearrange("p (a b) -> p a b", a=3)

        def goff(m):
            return sum(2 * T // b for b in (2, 4, 8, 16, 32, 64) if b < m)

        ring = [ctx.enter_context(nc.psum_tensor(f"ring{i}", [P, 512], F32)) for i in range(2)]
        aux = [ctx.enter_context(nc.psum_tensor(f"aux{i}", [P, 512], F32)) for i in range(2)]
        lev = [ctx.enter_context(nc.psum_tensor(f"lev{i}", [P, 512], F32)) for i in range(2)]
        okv = [ctx.enter_context(nc.psum_tensor(f"okv{i}", [P, 512], F32)) for i in range(2)]
        ops, kvp = okv

        class Signal:

            def __init__(self, name, per):
                self.sem, self.per = sem(name), per

            def at(self, n, j):
                return n * self.per + j

        yt_ps, fr_ps, q_ps, iv_ps, gb_ps = (Signal(s, 2) for s in ("yt_ps", "fr_ps", "q_ps", "iv_ps", "gb_ps"))
        e_ps, xa_ps, ga_ps, tr_ps = Signal("e_ps", 4), Signal("xa_ps", 2), Signal("ga_ps", 2), Signal("tr_ps", 4)
        lev_ps, kt_ps, u_ps = Signal("lev_ps", 2 * (LEVELS + 1)), Signal("kt_ps", 2), Signal("u_ps", 4)
        gr_ps, gi_ps = Signal("gr_ps", 2), Signal("gi_ps", 2)
        yth, f_sig, k_sig, q_sb, v_sb, gb_sil = (Signal(s, 2) for s in ("yth", "f_sig", "k_sig", "q_sb", "v_sb", "gb_sil"))
        esq = [Signal("esq0", 2), Signal("esq1", 2)]
        kt_sb, usq, xa_sb, ga_sil, xsq = Signal("kt_sb", 2), Signal("usq", 8), Signal("xa_sb", 2), Signal("ga_sil", 2), Signal("xsq", 4)
        r_sig, i_sig, a_exp, th_ok, u_sqrt = (Signal(s, k) for s, k in (("r_sig", 4), ("i_sig", 4), ("a_exp", 4), ("th_ok", 4), ("u_sqrt", 2)))
        aff, hn_hi = Signal("aff", 8), Signal("hn_hi", 4)
        ytl, f_ok, amask, q_f = Signal("ytl", 2), Signal("f_ok", 2), Signal("amask", 16), Signal("q_f", 2)
        q_upd, k_upd, g_upd = Signal("q_upd", 14), Signal("k_upd", 14), Signal("g_upd", 14)
        mgd, newt_e, eo = Signal("mgd", 4), Signal("newt_e", 2 * (NEWTON + 1)), Signal("eo", 2)
        newt_u, yb_ok, s_upd = Signal("newt_u", 2 * NEWTON), Signal("yb_ok", 8), Signal("s_upd", 8)
        newt_x, xn_ok, hn_lo = Signal("newt_x", NEWTON + 1), Signal("xn_ok", 2), Signal("hn_lo", 4)
        cvc, rx, gd, iu, scan, y_ok, yl_ok = (Signal(s, k) for s, k in (("cvc", 16), ("rx", 2), ("gd", 2), ("iu", 2), ("scan", 4), ("y_ok", 2), ("yl_ok", 1)))
        f_af, k_ok, a_sq, ix_ok, yh_ok, hl_in, hl_sv, hst_ok = (Signal(s, k) for s, k in (
            ("f_af", 4), ("k_ok", 4), ("a_sq", 2), ("ix_ok", 2), ("yh_ok", 1), ("hl_in", 2), ("hl_sv", 2), ("hst_ok", 2)))
        xld = [Signal("xld0", 16), Signal("xld1", 16)]
        xrl, ost = Signal("xrl", 32), Signal("ost", 32)
        par_ld, c_ld, wg_ld = sem("par_ld"), sem("c_ld"), sem("wg_ld")
        st_ld = [sem(f"st_ld{i}") for i in range(len(stage))]
        early_ld = [sem(f"early_ld{i}") for i in range(len(early))]
        fin = sem("fin")
        consts, zeroed, carry_zero, lb_ok = sem("consts"), sem("zeroed"), sem("carry_zero"), sem("lb_ok")
        pre_ps, pre_act = sem("pre_ps"), sem("pre_act")
        mod_sb, mod_ps, mod_ok = sem("mod_sb"), sem("mod_ps"), sem("mod_ok")
        ada_ps, gate_ok, gp_ps, gp_sb = sem("ada_ps"), sem("gate_ok"), sem("gp_ps"), sem("gp_sb")
        w_hi, w_lo, wo_lo, w_fold = sem("w_hi"), sem("w_lo"), sem("wo_lo"), sem("w_fold")
        d_ld, d_s0 = sem("d_ld"), sem("d_s0")
        chain_dve, chain_pool = sem("chain_dve"), sem("chain_pool")
        decode_sems = {}

        def dv(name):
            if name not in decode_sems:
                decode_sems[name] = sem("d_" + name)
            return decode_sems[name]

        xp_rows = x_prompt[0].rearrange("(m p) d -> m p d", p=P)
        yp_rows = y_prompt[0].rearrange("(m p) d -> m p d", p=P)
        w_in_v = w_in[0].rearrange("(k p) n -> p k n", p=P)
        w_out_v = w_out[0].rearrange("(k p) n -> p k n", p=P)
        ada_v = ada_w[0].rearrange("(k p) n -> p k n", p=P)

        NEARLY, NADA, NWI, NWO = 2 * D // 256, 3 * D // 256, PIN // 256, D // 256
        WI_COLS = (FR, Q_, IV, IV + 256, GB, GB + 256, FR + 256, Q_ + 256, XA, GA, XA + 256, GA + 256)
        pieces = ([("ada", i) for i in range(len(early), NEARLY)] + [("wi", i) for i in range(6)] + [("ada", i) for i in range(NEARLY, NADA)]
                  + [("wi", i) for i in range(6, NWI)] + [("wo", i) for i in range(NWO)])
        place, landed, before = {}, {}, {}
        users = [[] for _ in stage]
        for _i, _piece in enumerate(pieces):
            _s = _i % 2 if _piece[0] == "wo" else _i % len(stage)
            place[_piece], landed[_piece] = _s, 16 * (len(users[_s]) + 1)
            before[_piece] = users[_s][-1] if users[_s] else None
            users[_s].append(_piece)

        def blocks(t, m):
            return t.rearrange("p (b two m) -> p b two m", two=2, m=m)

        def products(m):
            g = ff[:, :] if m == 1 else gg[:, goff(m):goff(m) + 2 * T // m]
            return g.rearrange("p (b two) -> p b two", two=2)

        def pcol(name, i):
            return par[:, ROW[name] + i:ROW[name] + i + 1]

        W4 = CT * TD
        s0 = wih[:, :, 0:2 * HB * P].bitcast(F32)
        flat = lambda t: t[:, :, :].rearrange("p c t -> p (c t)")
        xad = flat(xa)[:, 0:CT * NB * (CW - 1 + NL)].rearrange("p (c b j) -> p c b j", c=CT, b=NB)
        xcd, rrd, iid, aad = (flat(t)[:, 0:W4] for t in (xc, rr, ii, aa))
        h0, hnew = flat(ii)[:, 256:256 + CT * NB], flat(ii)[:, 320:320 + CT * NB]
        halod = flat(ii)[:, 384:384 + CT * NB * (CW - 1)]

        def vseq(b):
            return (vv, gbs)[b % 2][0:TD, 1, :]

        mod_rows = [qq[:, :], kk[:, :], ff[:, :], vv[:, 0, :], flat(rr), flat(ii)]

        block = ctx.enter_context(nc.Block())

        @block.sync
        def _(sp):
            def load_x(m, t):
                sp.wait_ge(tr_ps.sem, tr_ps.at(m - 1, 4))
                sp.dma_start(xin[:, t, :], xp_rows[m * NT + t]).then_inc(xld[t].sem, 16)

            loads = [("pre", pre_norm_w[0]), ("post", post_norm_w[0]), ("cw", conv_w[0].rearrange("j c -> (j c)")),
                     ("cb", conv_b[0]), ("ba", rg_ba[0]), ("bx", rg_bx[0]), ("lam", rg_lambda[0]),
                     ("lbl", hg_lb_logits[0]), ("onw", hg_onorm_w[0]), ("adab", ada_b[0])]
            for name, src in loads:
                rows = src.rearrange("(r c) -> r c", c=P)
                sp.dma_start(am[ROW[name]:ROW[name] + rows.shape[0], 0, :], rows).then_inc(par_ld, 16)
            sp.dma_start(gp[0:1, :], c_prompt).then_inc(c_ld, 16)
            sp.dma_start(gp[1:NS, :], c_sample).then_inc(c_ld, 16)
            for t in range(NT):
                sp.dma_start(xin[:, t, :], xp_rows[t]).then_inc(xld[t].sem, 16)
            for i in range(len(early)):
                sp.dma_start(early[i], ada_v[:, :, 256 * i:256 * i + 256]).then_inc(early_ld[i], 16)
            for i, (kind, c) in enumerate(pieces):
                if i == 13:
                    for t in range(NT):
                        load_x(1, t)
                if before[kind, c]:
                    pk, pc = before[kind, c]
                    if pk == "ada":
                        sp.wait_ge(ada_ps, pc + 1)
                    else:
                        sp.wait_ge(*((w_lo, pc + 1) if pk == "wi" else (wo_lo, pc + 1)))
                src, col = {"ada": (ada_v, 256 * c), "wi": (w_in_v, WI_COLS[c % NWI]), "wo": (w_out_v, 256 * c)}[kind]
                sp.dma_start(stage[place[kind, c]], src[:, :, col:col + 256]).then_inc(st_ld[place[kind, c]], 16)
                if i == 6:
                    sp.wait_ge(zeroed, 1)
                    for w, src in ((0, rg_wa), (1, rg_wx)):
                        for odd in range(2):
                            v = src[0].rearrange("(t two) c d -> two c t d", two=2)[odd]
                            sp.dma_start(wg[64 * odd:64 * odd + 64, w, :, 64 * odd:64 * odd + 64], v).then_inc(wg_ld, 16)

            def residual(n, t):
                sp.dma_start(xr, xp_rows[n * NT + t]).then_inc(xrl.sem, 16)
                sp.wait_ge(eo.sem, eo.at(n, t + 1))
                sp.dma_start(yp_rows[n * NT + t], xr).then_inc(ost.sem, 16)
                sp.wait_ge(ost.sem, ost.at(n, 16 * t + 16))

            sp.wait_ge(wo_lo, NWO)
            for t in range(NT):
                load_x(2, t)
            with sp.Fori(1, BODIES - 2) as n:
                residual(n - 1, 0)
                load_x(n + 2, 0)
                residual(n - 1, 1)
                load_x(n + 2, 1)
            for n in range(BODIES - 3, BODIES):
                for t in range(NT):
                    residual(n, t)

            sp.wait_ge(tr_ps.sem, tr_ps.at(BODIES - 1, 4))
            sp.dma_start(xin[0:TD, 0, :], x_sample.rearrange("b l d -> (b l) d")).then_inc(d_ld, 16)
            sp.dma_start(xin[0:NB, 1, 0:DA], state_rglru_h[0]).then_inc(d_ld, 16)
            sp.dma_start(xin[0:NB * (CW - 1), 1, DA:D], state_rglru_conv[0].rearrange("b j c -> (b j) c")).then_inc(d_ld, 16)
            sp.wait_ge(dv("gb_d"), 1)
            for b in range(NB):
                sp.dma_start(s0[:, b, :].rearrange("p (h v) -> p h v", h=HB),
                             state_hgrn_S[0, b].rearrange("h k v -> k h v")).then_inc(d_s0, 16)
            sp.dma_start(xr[0:TD, :], x_sample.rearrange("b l d -> (b l) d")).then_inc(dv("xres"), 16)
            sp.wait_ge(dv("y_rows"), 1)
            sp.dma_start(y_sample.rearrange("b l d -> (b l) d"), xr[0:TD, :]).then_inc(fin, 16)
            sp.dma_start(S_prompt[0, 0].rearrange("h k v -> k h v"), st[:, :, :]).then_inc(fin, 16)
            sp.wait_ge(dv("s_new"), NB * HB)
            for b in range(NB):
                sp.dma_start(S_sample[0, b].rearrange("h k v -> k h v"),
                             s0[:, b, :].rearrange("p (h v) -> p h v", h=HB)).then_inc(fin, 16)
            sp.wait_ge(dv("rows_sb"), 4)
            sp.dma_start(h_prompt[0].rearrange("a (c p) -> (a c) p", p=P), xin[0:CT, 1, 0:P]).then_inc(fin, 16)
            sp.dma_start(h_sample[0], xin[0:NB, 0, 0:DA]).then_inc(fin, 16)
            sp.dma_start(conv_prompt[0, 0], xin[0:CW - 1, 1, DA:D]).then_inc(fin, 16)
            sp.dma_start(conv_sample[0].rearrange("b j c -> (b j) c"), xin[0:NB * (CW - 1), 0, DA:D]).then_inc(fin, 16)
            sp.wait_ge(fin, 16 * (2 + NB + 4))

        @block.tensor
        def _(pe):
            mm = nc.tensor.matmul

            def split3(out, lh, ll, rh, rl, ks, start, stop):
                last = None
                for k in ks:
                    for j, (a, b) in enumerate(((lh, rh), (lh, rl), (ll, rh))):
                        last = mm(out, a(k), b(k), start=start and k == ks[0] and j == 0,
                                  stop=stop and k == ks[-1] and j == 2)
                return last

            def project(bank, col, c):
                lo = col + P * c
                return split3(bank[:, T * c:T * c + T], lambda k: wih[:, k, lo:lo + P], lambda k: wil[:, k, lo:lo + P],
                              lambda k: hnh[:, k, :], lambda k: hnl[:, k, :], range(KT), True, True)

            def project_rows(bank, col, t, half):
                lo = P * t
                ks = range(KT // 2) if half == 0 else range(KT // 2, KT)
                return split3(bank[:, :], lambda k: hnh[:, k, lo:lo + P], lambda k: hnl[:, k, lo:lo + P],
                              lambda k: wih[:, k, col:col + DA], lambda k: wil[:, k, col:col + DA], ks,
                              half == 0, half == 1)

            def out_rows(bank, t, cols, half):
                lo, co = P * t, 512 * cols
                ks = range(KT // 2) if half == 0 else range(KT // 2, KT)
                return split3(bank[:, :], lambda k: yh[:, k, lo:lo + P], lambda k: yl[:, k, lo:lo + P],
                              lambda k: woh[:, k, co:co + 512], lambda k: wol[:, k, co:co + 512], ks,
                              half == 0, half == 1)

            def turn_x(m, j):
                if j == 0:
                    pe.wait_ge(xn_ok.sem, xn_ok.at(m, NT))
                bank = aux[(j + 1) % 2]
                for k in (2 * j, 2 * j + 1):
                    for t in range(NT):
                        last = nc.tensor.transpose(bank[:, (k % 2) * T + P * t:(k % 2) * T + P * t + P],
                                                   xin[:, t, P * k:P * k + P], ident[:, :])
                last.then_inc(tr_ps.sem, 1)

            def turn_y(n, j):
                if j == 0:
                    pe.wait_ge(yb_ok.sem, yb_ok.at(n, 8))
                    pe.wait_ge(r_sig.sem, r_sig.at(n, 4))
                else:
                    pe.wait_ge(i_sig.sem, i_sig.at(n, 4))
                for h in range(2):
                    for t in range(NT):
                        last = nc.tensor.transpose(aux[j][:, T * h + P * t:T * h + P * t + P],
                                                   gbs[:, t, P * (2 * j + h):P * (2 * j + h) + P], ident[:, :])
                last.then_inc(yt_ps.sem, 1)

            def level(n, p, l):
                i = p * (LEVELS + 1) + l
                if i >= 2 or not isinstance(n, int) or n > 0:
                    pe.wait_ge(amask.sem, amask.at(n, i - 1))
                if l == 0:
                    pe.wait_ge(q_sb.sem, q_sb.at(n, p + 1))
                    pe.wait_ge(k_ok.sem, k_ok.at(n, 2 * p + 2))
                elif l == 1:
                    pe.wait_ge(q_f.sem, q_f.at(n, p + 1))
                else:
                    pe.wait_ge(q_upd.sem, q_upd.at(n, LEVELS * p + l - 1))
                    pe.wait_ge(k_upd.sem, k_upd.at(n, LEVELS * p + l - 1))
                for hc in range(4):
                    q = qq[:, P * hc:P * hc + P]
                    w = P
                    if l > 0:
                        q, w = blocks(q, 1 << (l - 1))[:, :, 1, :], P // 2
                    last = mm(lev[i % 2][:, w * hc:w * hc + w], kk[:, P * hc:P * hc + P], q, start=True, stop=True)
                last.then_inc(lev_ps.sem, 1)

            def turn_k(n, p):
                pe.wait_ge(q_upd.sem, q_upd.at(n, LEVELS * p + LEVELS))
                pe.wait_ge(k_upd.sem, k_upd.at(n, LEVELS * p + LEVELS))
                for hc in range(4):
                    last = nc.tensor.transpose(aux[p][:, P * hc:P * hc + P], kk[:, P * hc:P * hc + P], ident[:, :])
                last.then_inc(kt_ps.sem, 1)

            def unit(n, p, c):
                ui = 2 * p + c
                pe.wait_ge(amask.sem, amask.at(n, 8 * p + 8))
                pe.wait_ge(v_sb.sem, v_sb.at(n, c + 1))
                pe.wait_ge(kt_sb.sem, kt_sb.at(n, p + 1))
                pe.wait_ge(yb_ok.sem, yb_ok.at(n, 4 * p))
                pe.wait_ge(s_upd.sem, s_upd.at(n, 2 * ui))
                for h in range(2):
                    hc, hd = 2 * h + c, 2 * p + h
                    v = vv[:, c, P * hd:P * hd + P]
                    mm(okv[c][:, P * h:P * h + P], am[:, hc, :], v, start=True, stop=False)
                    mm(okv[c][:, P * h:P * h + P], qq[:, P * hc:P * hc + P], st[:, hd, :], start=False, stop=True)
                    last = mm(okv[c][:, 2 * P + P * h:3 * P + P * h], ktr[:, hc, :], v, start=True, stop=True)
                last.then_inc(u_ps.sem, 1)

            def gates(n, p):
                pe.wait_ge(cvc.sem, cvc.at(n, 8 * p + 8))
                for w, s in ((0, gr_ps), (1, gi_ps)):
                    if p == 0 and w == 0:
                        if not isinstance(n, int) or n > 0:
                            pe.wait_ge(ytl.sem, ytl.at(n - 1, 2))
                    elif w == 1:
                        pe.wait_ge(kt_sb.sem, kt_sb.at(n, p + 1))
                    elif not (isinstance(n, int) and n == BODIES - 1):
                        pe.wait_ge(hn_lo.sem, hn_lo.at(n + 1, 4))
                    for c in range(2):
                        last = mm(aux[(1 + w + p) % 2][:, T * c:T * c + T], wg[:, w, 2 * p + c, :], xc[:, c, :],
                                  start=True, stop=True)
                    last.then_inc(s.sem, 1)

            def ada(i, bank):
                if i < len(early):
                    pe.wait_ge(early_ld[i], 16)
                    w = early[i]
                else:
                    pe.wait_ge(st_ld[place["ada", i]], landed["ada", i])
                    w = stage[place["ada", i]]
                o = 256 * (i % 2)
                for k in range(KT):
                    last = mm(bank[0:NS, o:o + 256], siluc[:, k, :], w[:, k, :], start=k == 0, stop=k == KT - 1)
                last.then_inc(ada_ps, 1)

            def turn_mod(b, bank, o):
                pe.wait_ge(mod_sb, b + 1)
                for j in range(4):
                    last = nc.tensor.transpose(bank[:, o + NS * j:o + NS * j + NS], mod_rows[b][0:NS, P * j:P * j + P],
                                               ident[0:NS, 0:NS])
                last.then_inc(mod_ps, 1)

            def body(n, first, last_body):
                def weights(i):
                    if first:
                        pe.wait_ge(w_lo, i)

                weights(1)
                if not first:
                    pe.wait_ge(i_sig.sem, i_sig.at(n - 1, 4))
                for k in range(4):
                    pe.wait_ge(hn_lo.sem, hn_lo.at(n, k + 1))
                project(ring[0], FR, 0)
                project(ring[0], FR, 1).then_inc(fr_ps.sem, 1)
                if not first:
                    turn_y(n - 1, 0)
                    turn_y(n - 1, 1)
                weights(2)
                project(ring[1], Q_, 0)
                project(ring[1], Q_, 1).then_inc(q_ps.sem, 1)
                pe.wait_ge(k_sig.sem, k_sig.at(n, 1))
                weights(4)
                project_rows(ring[0], IV, 0, 0)
                project_rows(ring[0], IV, 0, 1).then_inc(iv_ps.sem, 1)
                level(n, 0, 0)
                pe.wait_ge(q_sb.sem, q_sb.at(n, 1))
                project_rows(ring[1], IV, 1, 0)
                level(n, 0, 1)
                project_rows(ring[1], IV, 1, 1).then_inc(iv_ps.sem, 1)
                level(n, 0, 2)
                pe.wait_ge(v_sb.sem, v_sb.at(n, 1))
                weights(6)
                project_rows(ring[0], GB, 0, 0)
                level(n, 0, 3)
                project_rows(ring[0], GB, 0, 1).then_inc(gb_ps.sem, 1)
                level(n, 0, 4)
                pe.wait_ge(v_sb.sem, v_sb.at(n, 2))
                project_rows(ring[1], GB, 1, 0)
                level(n, 0, 5)
                project_rows(ring[1], GB, 1, 1).then_inc(gb_ps.sem, 1)
                level(n, 0, 6)
                if not first:
                    pe.wait_ge(wo_lo, NWO)
                    pe.wait_ge(yl_ok.sem, yl_ok.at(n - 1, 1))
                    pe.wait_ge(ytl.sem, ytl.at(n - 1, 2))
                    pe.wait_ge(gb_sil.sem, gb_sil.at(n, 1))
                    out_rows(ring[0], 0, 0, 0)
                level(n, 0, 7)
                if not first:
                    out_rows(ring[0], 0, 0, 1).then_inc(e_ps.sem, 1)
                if not first:
                    pe.wait_ge(ytl.sem, ytl.at(n - 1, 1))
                turn_k(n, 0)
                if not first:
                    pe.wait_ge(gb_sil.sem, gb_sil.at(n, 2))
                    out_rows(ring[1], 0, 1, 0)
                unit(n, 0, 0)
                if not first:
                    out_rows(ring[1], 0, 1, 1).then_inc(e_ps.sem, 1)
                unit(n, 0, 1)
                if first:
                    pe.wait_ge(hn_lo.sem, hn_lo.at(0, 4))
                    pe.wait_ge(kt_sb.sem, kt_sb.at(0, 1))
                    for i in range(NEARLY, NADA):
                        ada(i, aux[i // 2 % 2])
                weights(7)
                pe.wait_ge(gb_sil.sem, gb_sil.at(n, 1))
                if not first:
                    pe.wait_ge(esq[0].sem, esq[0].at(n - 1, 1))
                project(ring[0], FR + 2 * P, 0)
                project(ring[0], FR + 2 * P, 1).then_inc(fr_ps.sem, 1)
                pe.wait_ge(gb_sil.sem, gb_sil.at(n, 2))
                if not first:
                    pe.wait_ge(esq[1].sem, esq[1].at(n - 1, 1))
                if first:
                    for b in (4, 5):
                        turn_mod(b, aux[0], 4 * NS * (b - 4))
                weights(8)
                project(ring[1], Q_ + 2 * P, 0)
                project(ring[1], Q_ + 2 * P, 1).then_inc(q_ps.sem, 1)
                if first:
                    pe.wait_ge(gate_ok, 1)
                    for k in range(KT):
                        last = mm(lev[k // 4][:, P * (k % 4):P * (k % 4) + P], gpt[:, k, 0:1].to_broadcast([P, P]),
                                  ident[:, :], start=True, stop=True)
                    last.then_inc(gp_ps, 1)
                pe.wait_ge(k_sig.sem, k_sig.at(n, 2))
                weights(9)
                project(ring[0], XA, 0)
                project(ring[0], XA, 1).then_inc(xa_ps.sem, 1)
                if first:
                    pe.wait_ge(gp_sb, 1)
                level(n, 1, 0)
                pe.wait_ge(q_sb.sem, q_sb.at(n, 2))
                weights(10)
                project(ring[1], GA, 0)
                level(n, 1, 1)
                project(ring[1], GA, 1).then_inc(ga_ps.sem, 1)
                level(n, 1, 2)
                pe.wait_ge(xa_sb.sem, xa_sb.at(n, 1))
                weights(11)
                project(ring[0], XA + 2 * P, 0)
                level(n, 1, 3)
                gates(n, 0)
                project(ring[0], XA + 2 * P, 1).then_inc(xa_ps.sem, 1)
                level(n, 1, 4)
                pe.wait_ge(ga_sil.sem, ga_sil.at(n, 1))
                weights(12)
                project(ring[1], GA + 2 * P, 0)
                level(n, 1, 5)
                project(ring[1], GA + 2 * P, 1).then_inc(ga_ps.sem, 1)
                level(n, 1, 6)
                if not last_body:
                    pe.wait_ge(r_sig.sem, r_sig.at(n, 2))
                    turn_x(n + 1, 0)
                    pe.wait_ge(i_sig.sem, i_sig.at(n, 2))
                    turn_x(n + 1, 1)
                if not first:
                    pe.wait_ge(xa_sb.sem, xa_sb.at(n, 2))
                    out_rows(ring[0], 1, 0, 0)
                level(n, 1, 7)
                if not first:
                    out_rows(ring[0], 1, 0, 1).then_inc(e_ps.sem, 1)
                if not last_body:
                    pe.wait_ge(hn_lo.sem, hn_lo.at(n + 1, 1))
                    turn_x(n + 1, 2)
                    pe.wait_ge(hn_lo.sem, hn_lo.at(n + 1, 2))
                    turn_x(n + 1, 3)
                if not first:
                    pe.wait_ge(ga_sil.sem, ga_sil.at(n, 2))
                    out_rows(ring[1], 1, 1, 0)
                if last_body:
                    pe.wait_ge(r_sig.sem, r_sig.at(n, 2))
                else:
                    pe.wait_ge(hn_lo.sem, hn_lo.at(n + 1, 3))
                turn_k(n, 1)
                if last_body:
                    pe.wait_ge(i_sig.sem, i_sig.at(n, 2))
                gates(n, 1)
                unit(n, 1, 0)
                if not first:
                    out_rows(ring[1], 1, 1, 1).then_inc(e_ps.sem, 1)
                unit(n, 1, 1)

            pe.wait_ge(consts, 1)
            pe.wait_ge(par_ld, 160)
            nc.tensor.transpose(aux[0][:, 0:NROW], am[0:NROW, 0, :], ident[0:NROW, 0:NROW]).then_inc(pre_ps, 1)
            pe.wait_ge(c_ld, 32)
            for k in range(KT):
                last = nc.tensor.transpose(aux[1][:, NS * k:NS * k + NS], gp[0:NS, P * k:P * k + P], ident[0:NS, 0:NS])
            last.then_inc(pre_ps, 1)
            siluc = xc[:, 0, 0:KT * NS].rearrange("p (k s) -> p k s", k=KT)
            pe.wait_ge(pre_act, 2)
            for i in range(NEARLY):
                ada(i, (okv + lev)[i // 2])
                if i % 2 and i > 1:
                    turn_mod(i // 2 - 1, ring[0], 4 * NS * (i // 2 - 1))
            turn_mod(3, ring[0], 12 * NS)
            for j in range(4):
                if j >= 2:
                    pe.wait_ge(hn_lo.sem, j - 1)
                turn_x(0, j)
            pe.wait_ge(wg_ld, 64)
            pe.wait_ge(zeroed, 3)
            pe.wait_ge(carry_zero, 2)

            body(0, True, False)
            with pe.Fori(1, BODIES - 1) as n:
                body(n, False, False)
            body(BODIES - 1, False, True)
            n = BODIES
            turn_y(n - 1, 0)
            turn_y(n - 1, 1)
            pe.wait_ge(yl_ok.sem, yl_ok.at(n - 1, 1))
            pe.wait_ge(ytl.sem, ytl.at(n - 1, 2))
            for j in range(4):
                pe.wait_ge(esq[j % 2].sem, esq[j % 2].at(n - 1, j // 2))
                if j < 2:
                    pe.wait_ge(ga_sil.sem, ga_sil.at(n - 1, 2))
                out_rows(ring[j % 2], j // 2, j % 2, 0)
                out_rows(ring[j % 2], j // 2, j % 2, 1).then_inc(e_ps.sem, 1)

            pe.wait_ge(dv("xn"), 1)
            pe.wait_ge(d_ld, 48)
            for k in range(KT):
                nc.tensor.transpose(aux[0][:, TD * k:TD * k + TD], xin[0:TD, 0, P * k:P * k + P], ident[0:TD, 0:TD])
            for c in range(CT):
                nc.tensor.transpose(aux[1][:, NB * c:NB * c + NB], xin[0:NB, 1, P * c:P * c + P], ident[0:NB, 0:NB])
            nj = NB * (CW - 1)
            for c in range(CT):
                last = nc.tensor.transpose(aux[1][:, TD + nj * c:TD + nj * c + nj], xin[0:nj, 1, DA + P * c:DA + P * c + P],
                                           ident[0:nj, 0:nj])
            last.then_inc(dv("turned"), 1)
            gprow = aa[:, 1, :].rearrange("p (k t) -> p k t", k=KT)
            pe.wait_ge(dv("gprow"), 1)
            for k in range(KT):
                last = mm(lev[k // 4][0:TD, P * (k % 4):P * (k % 4) + P], gprow[:, k, :], ident[:, :], start=True, stop=True)
            last.then_inc(dv("gp_ps"), 1)
            pe.wait_ge(dv("hn"), 1)
            pe.wait_ge(dv("carried"), 2)
            pe.wait_ge(esq[0].sem, esq[0].at(n, 0))
            for i, col in enumerate([b + P * c for b in (XA, GA, Q_, FR) for c in range(CT)]):
                last = split3(ring[0][:, TD * i:TD * i + TD], lambda k: wih[:, k, col:col + P], lambda k: wil[:, k, col:col + P],
                              lambda k: hnh[:, k, 0:TD], lambda k: hnl[:, k, 0:TD], range(KT), True, True)
            last.then_inc(dv("proj_ps"), 1)
            pe.wait_ge(esq[1].sem, esq[1].at(n, 0))
            for bank, col, s in ((ring[1], IV, "iv_d"), (aux[0], GB, "gb_d")):
                split3(bank[0:TD, :], lambda k: hnh[:, k, 0:TD], lambda k: hnl[:, k, 0:TD],
                       lambda k: wih[:, k, col:col + DA], lambda k: wil[:, k, col:col + DA], range(KT), True, True)\
                    .then_inc(dv(s), 1)
            for l in range(DLEVELS + 1):
                pe.wait_ge(dv("level_in"), l + 1)
                if l == 0:
                    pe.wait_ge(dv("gp_sb"), 1)
                if l == 2:
                    pe.wait_ge(dv("masked"), 1)
                for h in range(HB):
                    q, w = qq[:, TD * h:TD * h + TD], TD
                    if l > 0:
                        q, w = blocks(q, 1 << (l - 1))[:, :, 1, :], TD // 2
                    last = mm(lev[l % 2][0:TD, w * h:w * h + w], kk[:, TD * h:TD * h + TD], q, start=True, stop=True)
                last.then_inc(dv("level_ps"), 1)
            pe.wait_ge(dv("level_in"), DLEVELS + 2)
            for h in range(HB):
                last = nc.tensor.transpose(aux[1][0:TD, P * h:P * h + P], kk[:, TD * h:TD * h + TD], ident[:, :])
            last.then_inc(dv("kt_d"), 1)
            pe.wait_ge(dv("masked"), DLEVELS + 1)
            pe.wait_ge(dv("v_d"), 1)
            pe.wait_ge(d_s0, 16 * NB)
            for h in range(HB):
                mm(ops[:, TD * h:TD * h + TD], vv[0:TD, 0, P * h:P * h + P], am[0:TD, h, 0:TD], start=True, stop=False,
                   skip_group_check=True)
                for b in range(NB):
                    o = TD * h + NL * b
                    last = mm(ops[:, o:o + NL], s0[:, b, P * h:P * h + P], qq[:, o:o + NL], start=False, stop=b == NB - 1,
                              skip_group_check=True)
            last.then_inc(dv("ot_ps"), 1)
            pe.wait_ge(dv("ot_sb"), 1)
            for h in range(HB):
                last = nc.tensor.transpose(lev[1][0:TD, P * h:P * h + P], ff[:, TD * h:TD * h + TD], ident[:, :])
            last.then_inc(dv("o_ps"), 1)
            pe.wait_ge(dv("conv_d"), 16)
            for w in range(2):
                for c in range(CT):
                    o = TD * CT * w + TD * c
                    last = mm(ring[1][:, o:o + TD], wg[:, w, c, :], xcd[:, TD * c:TD * c + TD], start=True, stop=True)
            last.then_inc(dv("gates_ps"), 1)
            pe.wait_ge(dv("yb_d"), HB)
            for h in range(HB):
                last = nc.tensor.transpose(lev[0][:, TD * h:TD * h + TD], gbs[0:TD, 0, P * h:P * h + P], ident[0:TD, 0:TD])
            last.then_inc(dv("ybt_ps"), 1)
            pe.wait_ge(dv("y_dec"), 4)
            for c in range(2):
                split3(ring[c][0:TD, :], lambda k: yh[:, k, 0:TD], lambda k: yl[:, k, 0:TD],
                       lambda k: woh[:, k, 512 * c:512 * c + 512], lambda k: wol[:, k, 512 * c:512 * c + 512],
                       range(KT), True, True).then_inc(dv("m_ps"), 1)
            for c in range(CT):
                nc.tensor.transpose(aux[0][0:nj, P * c:P * c + P], halod[:, nj * c:nj * c + nj], ident[:, :])
            for c in range(CT):
                nc.tensor.transpose(aux[1][0:NB, P * c:P * c + P], hnew[:, NB * c:NB * c + NB], ident[:, :])
            for c in range(CT):
                nc.tensor.transpose(ops[0:CW - 1, P * c:P * c + P], halo[:, c, :], ident[:, :])
            pe.wait_ge(hst_ok.sem, hst_ok.at(BODIES, 0))
            nc.tensor.transpose(lev[1][0:CT, 0:P], hst[:, :], ident[:, :]).then_inc(dv("rows_ps"), 1)
            for b in range(NB):
                pe.wait_ge(dv("v_seq"), b + 1)
                if b == 0:
                    pe.wait_ge(dv("kt_sbd"), 1)
                else:
                    pe.wait_ge(dv("s_new"), HB * b)
                for h in range(HB):
                    last = mm(kvp[:, P * h:P * h + P], ktr[0:TD, h, :], vseq(b)[:, P * h:P * h + P], start=True, stop=True)
                last.then_inc(dv("kv_ps"), 1)

        @block.scalar
        def _(act):
            A = nc.scalar.activation

            def gate_out(n, p):
                act.wait_ge(fr_ps.sem, fr_ps.at(n, p + 1))
                act.wait_ge(u_ps.sem, u_ps.at(n, 2 * p))
                A(ff[:, :], ring[0][:, :], ACT.Sigmoid).then_inc(f_sig.sem, 1)
                A(kk[:, :], ring[0][:, :], ACT.Sigmoid, scale=-1.0).then_inc(k_sig.sem, 1)

            def q_out(n, p):
                act.wait_ge(q_ps.sem, q_ps.at(n, p + 1))
                A(qq[:, :], ring[1][:, :], ACT.Copy).then_inc(q_sb.sem, 1)

            def squares_m(n, j):
                act.wait_ge(e_ps.sem, e_ps.at(n, j + 1))
                act.wait_ge(mgd.sem, mgd.at(n, j + 1))
                A(ring[j % 2][:, :], ring[j % 2][:, :], ACT.Square, accum_out=essq[:, j:j + 1]).then_inc(esq[j % 2].sem, 1)

            def k_out(n, p):
                act.wait_ge(kt_ps.sem, kt_ps.at(n, p + 1))
                A(ktr[:, :, :], aux[p][:, :].rearrange("p (h k) -> p h k", h=4), ACT.Copy).then_inc(kt_sb.sem, 1)

            def squares_o(n, ui):
                act.wait_ge(s_upd.sem, s_upd.at(n, 2 * ui + 2))
                c = ui % 2
                for h in range(2):
                    act.wait_ge(usq.sem, usq.at(n, 2 * ui + h))
                    A(junk[:, 512:640], okv[c][:, P * h:P * h + P], ACT.Square, accum_out=ussq[:, 2 * c + h:2 * c + h + 1])\
                        .then_inc(usq.sem, 1)

            def xa_out(n, p):
                act.wait_ge(xa_ps.sem, xa_ps.at(n, p + 1))
                act.wait_ge(cvc.sem, cvc.at(n, 8 * p))
                act.wait_ge(hl_sv.sem, hl_sv.at(n, p))
                A(xa[:, :, CW - 1:], ring[0][:, :].rearrange("p (c t) -> p c t", c=2), ACT.Copy).then_inc(xa_sb.sem, 1)

            def ga_out(n, p):
                act.wait_ge(ga_ps.sem, ga_ps.at(n, p + 1))
                act.wait_ge(yl_ok.sem, yl_ok.at(n, 0))
                act.wait_ge(yh_ok.sem, yh_ok.at(n, 0))
                A(sil[:, 2 * p:2 * p + 2, :], ring[1][:, :].rearrange("p (c t) -> p c t", c=2), ACT.Silu)\
                    .then_inc(ga_sil.sem, 1)

            def squares_x(m):
                for t in range(NT):
                    act.wait_ge(xld[t].sem, xld[t].at(m + 1, 0))
                    if t == 0:
                        act.wait_ge(xn_ok.sem, xn_ok.at(m, 0))
                    for c in range(2):
                        act.wait_ge(xsq.sem, xsq.at(m, 2 * t + c))
                        A(junk[:, 0:512], xin[:, t, 512 * c:512 * c + 512], ACT.Square,
                          accum_out=xssq[:, 2 * t + c:2 * t + c + 1]).then_inc(xsq.sem, 1)

            def gates_out(n, p):
                act.wait_ge(gr_ps.sem, gr_ps.at(n, p + 1))
                act.wait_ge(iu.sem, iu.at(n, p))
                for c in range(2):
                    A(rr[:, c, :], aux[(1 + p) % 2][:, T * c:T * c + T], ACT.Sigmoid,
                      bias=pcol("ba", 2 * p + c)).then_inc(r_sig.sem, 1)
                act.wait_ge(gi_ps.sem, gi_ps.at(n, p + 1))
                act.wait_ge(scan.sem, scan.at(n, 2 * p))
                for c in range(2):
                    A(ii[:, c, :], aux[p][:, T * c:T * c + T], ACT.Sigmoid, bias=pcol("bx", 2 * p + c)).then_inc(i_sig.sem, 1)

            def decay(n, p):
                act.wait_ge(r_sig.sem, r_sig.at(n, 2 * p + 2))
                for c in range(2):
                    A(aa[:, c, :], rr[:, c, :], ACT.Exp, scale=cneg[:, 2 * p + c:2 * p + c + 1]).then_inc(a_exp.sem, 1)
                for c in range(2):
                    A(rr[:, c, :], rr[:, c, :], ACT.Tanh, scale=cpos[:, 2 * p + c:2 * p + c + 1]).then_inc(th_ok.sem, 1)

            def root(n, p):
                act.wait_ge(gd.sem, gd.at(n, p + 1))
                A(rr[:, :, :], rr[:, :, :], ACT.Sqrt).then_inc(u_sqrt.sem, 1)

            def hn_out(m, j):
                bank = aux[(j + 1) % 2]
                act.wait_ge(tr_ps.sem, tr_ps.at(m, j + 1))
                for i in range(2):
                    k = 2 * j + i
                    A(bank[:, T * i:T * i + T], bank[:, T * i:T * i + T], ACT.Identity, scale=sc1[:, k, 0:1],
                      bias=shf[:, k, 0:1]).then_inc(aff.sem, 1)
                act.wait_ge(aff.sem, aff.at(m, 2 * j + 2))
                A(hnh[:, 2 * j:2 * j + 2, :], bank[:, :].rearrange("p (k t) -> p k t", k=2), ACT.Copy).then_inc(hn_hi.sem, 1)

            def y_turned(n, j):
                act.wait_ge(yt_ps.sem, yt_ps.at(n, j + 1))
                A(yh[:, CT + 2 * j:CT + 2 * j + 2, :], aux[j][:, :].rearrange("p (k t) -> p k t", k=2), ACT.Copy)\
                    .then_inc(yth.sem, 1)

            def mod_out(b, bank):
                act.wait_ge(ada_ps, 2 * b + 2)
                A(mod_rows[b][0:NS, :], bank[0:NS, :], ACT.Copy).then_inc(mod_sb, 1)

            def head(kind, c):
                s = stage[place[kind, c]]
                act.wait_ge(st_ld[place[kind, c]], landed[kind, c])
                if kind == "wo":
                    for h in range(HB):
                        A(s[:, CT + h, :], s[:, CT + h, :], ACT.Copy, scale=pcol("onw", h)).then_inc(w_fold, 1)
                    act.wait_ge(w_fold, HB * (c + 1))
                    act.wait_ge(w_lo, NWI)
                dst, col = (wih, WI_COLS[c]) if kind == "wi" else (woh, 256 * c)
                A(dst[:, :, col:col + 256], s, ACT.Copy).then_inc(w_hi, 1)

            def body(n, first, last_body):
                def weights(kind, *which):
                    if first:
                        for c in which:
                            head(kind, c)

                weights("wi", 3)
                gate_out(n, 0)
                if not first:
                    act.wait_ge(wo_lo, NWO)
                    y_turned(n - 1, 0)
                    y_turned(n - 1, 1)
                q_out(n, 0)
                weights("wi", 4)
                for t in range(NT):
                    act.wait_ge(iv_ps.sem, iv_ps.at(n, t + 1))
                    A(vv[:, t, :], ring[t][:, :], ACT.Copy).then_inc(v_sb.sem, 1)
                    if t == 0:
                        weights("wi", 5)
                for t in range(NT):
                    act.wait_ge(gb_ps.sem, gb_ps.at(n, t + 1))
                    A(gbs[:, t, :], ring[t][:, :], ACT.Silu).then_inc(gb_sil.sem, 1)
                if not first:
                    squares_m(n - 1, 0)
                k_out(n, 0)
                weights("wi", 6)
                squares_o(n, 0)
                if not first:
                    squares_m(n - 1, 1)
                squares_o(n, 1)
                weights("wi", 7)
                if not last_body:
                    squares_x(n + 1)
                if first:
                    for b in (4, 5):
                        mod_out(b, aux[b % 2])
                weights("wi", 8)
                gate_out(n, 1)
                q_out(n, 1)
                weights("wi", 9, 10)
                if first:
                    act.wait_ge(gp_ps, 1)
                    for i in range(2):
                        last = A(gp[:, 512 * i:512 * i + 512], lev[i][:, :], ACT.Copy)
                    last.then_inc(gp_sb, 1)
                xa_out(n, 0)
                weights("wi", 11)
                ga_out(n, 0)
                gates_out(n, 0)
                weights("wo", 0)
                xa_out(n, 1)
                decay(n, 0)
                ga_out(n, 1)
                root(n, 0)
                weights("wo", 1)
                if not last_body:
                    for j in range(4):
                        hn_out(n + 1, j)
                weights("wo", 2)
                if not first:
                    squares_m(n - 1, 2)
                k_out(n, 1)
                gates_out(n, 1)
                squares_o(n, 2)
                if not first:
                    squares_m(n - 1, 3)
                squares_o(n, 3)
                decay(n, 1)
                root(n, 1)
                weights("wo", 3)

            act.wait_ge(pre_ps, 1)
            A(par[:, :], aux[0][:, 0:NROW], ACT.Copy).then_inc(pre_act, 1)
            act.wait_ge(pre_ps, 2)
            A(xc[:, 0, 0:KT * NS], aux[1][:, 0:KT * NS], ACT.Silu).then_inc(pre_act, 1)
            squares_x(0)
            act.wait_ge(chain_dve, 3)
            A(tmp[:, 1, :], tmp[:, 0, :], ACT.Exp, scale=-1.0).then_inc(pre_act, 1)
            A(tmp[:, 3, :], tmp[:, 2, :], ACT.Exp).then_inc(pre_act, 1)
            for b in range(3):
                mod_out(b, (okv + lev)[b])
            head("wi", 0)
            mod_out(3, lev[1])
            head("wi", 1)
            act.wait_ge(mod_ok, 1)
            for j in range(4):
                hn_out(0, j)
            head("wi", 2)

            body(0, True, False)
            with act.Fori(1, BODIES - 1) as n:
                body(n, False, False)
            body(BODIES - 1, False, True)
            n = BODIES
            y_turned(n - 1, 0)
            y_turned(n - 1, 1)
            for j in range(4):
                squares_m(n - 1, j)

            act.wait_ge(d_ld, 16 * 3)
            for c in range(2):
                if c:
                    act.wait_ge(dv("xsq_d"), 1)
                A(junk[0:TD, 0:512], xin[0:TD, 0, 512 * c:512 * c + 512], ACT.Square, accum_out=xssq[0:TD, c:c + 1])\
                    .then_inc(dv("xsq_d"), 1)
            act.wait_ge(dv("gp_ps"), 1)
            act.wait_ge(mgd.sem, mgd.at(BODIES, 0))
            for i in range(2):
                last = A(gp[0:TD, 512 * i:512 * i + 512], lev[i][0:TD, :], ACT.Copy)
            last.then_inc(dv("gp_sb"), 1)
            act.wait_ge(dv("proj_ps"), 1)
            W4 = CT * TD
            A(xad[:, :, :, CW - 1:], ring[0][:, 0:W4].rearrange("p (c b l) -> p c b l", c=CT, b=NB), ACT.Copy)\
                .then_inc(dv("xa_d"), 1)
            A(sil[:, 0, 0:W4], ring[0][:, W4:2 * W4], ACT.Silu).then_inc(dv("ga_d"), 1)
            A(qq[:, 0:W4], ring[0][:, 2 * W4:3 * W4], ACT.Copy).then_inc(dv("qfk_d"), 1)
            A(ff[:, 0:W4], ring[0][:, 3 * W4:4 * W4], ACT.Sigmoid).then_inc(dv("qfk_d"), 1)
            A(kk[:, 0:W4], ring[0][:, 3 * W4:4 * W4], ACT.Sigmoid, scale=-1.0).then_inc(dv("qfk_d"), 1)
            act.wait_ge(dv("iv_d"), 1)
            A(vv[0:TD, 0, :], ring[1][0:TD, :], ACT.Copy).then_inc(dv("v_d"), 1)
            act.wait_ge(dv("gb_d"), 1)
            A(gbs[0:TD, 0, :], aux[0][0:TD, :], ACT.Silu).then_inc(dv("gb_sb"), 1)
            act.wait_ge(dv("kt_d"), 1)
            A(ktr[0:TD, :, :], aux[1][0:TD, :].rearrange("p (h k) -> p h k", h=HB), ACT.Copy).then_inc(dv("kt_sbd"), 1)
            act.wait_ge(dv("ot_ps"), 1)
            act.wait_ge(dv("level_in"), DLEVELS + 2)
            A(ff[:, 0:W4], ops[:, 0:W4], ACT.Copy).then_inc(dv("ot_sb"), 1)
            act.wait_ge(dv("o_ps"), 1)
            for h in range(HB):
                if h:
                    act.wait_ge(dv("usq_d"), h)
                A(junk[0:TD, 512:640], lev[1][0:TD, P * h:P * h + P], ACT.Square, accum_out=ussq[0:TD, h:h + 1])\
                    .then_inc(dv("usq_d"), 1)
            act.wait_ge(dv("gates_ps"), 1)
            for w, dst, bias in ((0, rrd, "ba"), (1, iid, "bx")):
                for c in range(CT):
                    o = W4 * w + TD * c
                    A(dst[:, TD * c:TD * c + TD], ring[1][:, o:o + TD], ACT.Sigmoid, bias=pcol(bias, c)).then_inc(dv("ri_d"), 1)
            act.wait_ge(dv("ri_d"), 2 * CT)
            for c in range(CT):
                A(aad[:, TD * c:TD * c + TD], rrd[:, TD * c:TD * c + TD], ACT.Exp, scale=cneg[:, c:c + 1]).then_inc(dv("a_d"), 1)
            for c in range(CT):
                A(rrd[:, TD * c:TD * c + TD], rrd[:, TD * c:TD * c + TD], ACT.Tanh, scale=cpos[:, c:c + 1]).then_inc(dv("a_d"), 1)
            act.wait_ge(dv("guard_d"), 1)
            A(rrd, rrd, ACT.Sqrt).then_inc(dv("root_d"), 1)
            for c in range(2):
                act.wait_ge(dv("m_ps"), c + 1)
                act.wait_ge(dv("mg_d"), c + 1)
                A(ring[c][0:TD, :], ring[c][0:TD, :], ACT.Square, accum_out=essq[0:TD, c:c + 1]).then_inc(dv("msq_d"), 1)
            act.wait_ge(dv("rows_ps"), 1)
            A(xin[0:NB * (CW - 1), 0, DA:D], aux[0][0:NB * (CW - 1), :], ACT.Copy).then_inc(dv("rows_sb"), 1)
            A(xin[0:NB, 0, 0:DA], aux[1][0:NB, :], ACT.Copy).then_inc(dv("rows_sb"), 1)
            A(xin[0:CW - 1, 1, DA:D], ops[0:CW - 1, :], ACT.Copy).then_inc(dv("rows_sb"), 1)
            A(xin[0:CT, 1, 0:P], lev[1][0:CT, 0:P], ACT.Copy).then_inc(dv("rows_sb"), 1)

        @block.vector
        def _(dve):
            V = nc.vector

            def rsqrt_steps(w, ssq, out, count, base, s):
                y, v, t = out[:, 0, :], out[:, 1, :], out[:, 2, :]
                k = 0

                def done(ins):
                    nonlocal k
                    k += 1
                    ins.then_inc(s, 1)
                    dve.wait_ge(s, base + k)
                done(V.tensor_scalar(v, ssq, 1.0 / count, EPS, ALU.mult, ALU.add))
                done(V.tensor_scalar(t.bitcast(I32), v.bitcast(I32), 1, None, ALU.logical_shift_right))
                done(V.tensor_scalar(y.bitcast(I32), t.bitcast(I32), -1.0, MAGIC, ALU.mult, ALU.add))
                for _ in range(3):
                    done(V.tensor_tensor(t, y, y, ALU.mult))
                    done(V.scalar_tensor_tensor(t, t, -0.5, v, ALU.mult, ALU.mult))
                    done(V.scalar_tensor_tensor(y, t, 1.5, y, ALU.add, ALU.mult))

            def y_rest(n, j):
                dve.wait_ge(yth.sem, yth.at(n, j + 1))
                V.tensor_tensor(yl[:, CT + 2 * j:CT + 2 * j + 2, :], aux[j][:, :].rearrange("p (k t) -> p k t", k=2),
                                yh[:, CT + 2 * j:CT + 2 * j + 2, :], ALU.subtract).then_inc(ytl.sem, 1)

            def forget(n, p):
                dve.wait_ge(f_af.sem, f_af.at(n, 2 * p + 2))
                V.tensor_scalar_max(ff[:, :], ff[:, :], F_MIN).then_inc(f_ok.sem, 1)

            def take(n, p, l):
                i = p * (LEVELS + 1) + l
                dve.wait_ge(lev_ps.sem, lev_ps.at(n, i + 1))
                if l == 0:
                    dve.wait_ge(u_ps.sem, u_ps.at(n, 2 * p))
                    dve.wait_ge(f_ok.sem, f_ok.at(n, p + 1))
                    V.tensor_tensor(qq[:, :], qq[:, :], ff[:, :], ALU.mult).then_inc(q_f.sem, 1)
                    V.copy_predicated(am[:, :, :], eye[:, :].unsqueeze(1).to_broadcast([P, 4, P]),
                                      lev[i % 2][:, :].rearrange("p (h t) -> p h t", h=4)).then_inc(amask.sem, 1)
                    return
                dve.wait_ge(amask.sem, amask.at(n, i))
                m = 1 << (l - 1)
                nb = 2 * T // (2 * m)
                j = LEVELS * p + l
                if l == 1:
                    dve.wait_ge(q_f.sem, q_f.at(n, p + 1))
                else:
                    dve.wait_ge(q_upd.sem, q_upd.at(n, j - 1))
                    dve.wait_ge(k_upd.sem, k_upd.at(n, j - 1))
                    dve.wait_ge(g_upd.sem, g_upd.at(n, j - 1))
                g = products(m)
                qo, ke = blocks(qq[:, :], m)[:, :, 1, :], blocks(kk[:, :], m)[:, :, 0, :]
                V.tensor_tensor(qo, qo, g[:, :, 0:1].to_broadcast([P, nb, m]), ALU.mult).then_inc(q_upd.sem, 1)
                V.tensor_tensor(ke, ke, g[:, :, 1:2].to_broadcast([P, nb, m]), ALU.mult).then_inc(k_upd.sem, 1)
                o = goff(2 * m)
                V.tensor_tensor(gg[:, o:o + nb], g[:, :, 0], g[:, :, 1], ALU.mult).then_inc(g_upd.sem, 1)
                a = am[:, :, :].rearrange("p h (b two m) -> p h b two m", two=2, m=m)
                x = lev[i % 2][:, 0:256].rearrange("p (h b m) -> p h b m", h=4, m=m)
                msk = lmask[:, l - 1, :].rearrange("p (b m) -> p b m", m=m).unsqueeze(1).to_broadcast([P, 4, P // (2 * m), m])
                V.copy_predicated(a[:, :, :, 1, :], msk, x).then_inc(amask.sem, 1)

            def state(n, p, c):
                ui = 2 * p + c
                dve.wait_ge(u_ps.sem, u_ps.at(n, ui + 1))
                dve.wait_ge(g_upd.sem, g_upd.at(n, LEVELS * p + LEVELS))
                dve.wait_ge(s_upd.sem, s_upd.at(n, 2 * ui))
                for h in range(2):
                    hd, o = 2 * p + h, goff(P) + 2 * h + c
                    V.scalar_tensor_tensor(st[:, hd, :], st[:, hd, :], gg[:, o:o + 1],
                                           okv[c][:, 2 * P + P * h:3 * P + P * h],
                                           ALU.mult, ALU.add).then_inc(s_upd.sem, 1)

            def rows(n, p):
                dve.wait_ge(usq.sem, usq.at(n, 4 * p + 4))
                rsqrt_steps(4, ussq, urs, P, newt_u.at(n, NEWTON * p), newt_u.sem)
                dve.wait_ge(gb_sil.sem, gb_sil.at(n, 2))
                for c in range(2):
                    for h in range(2):
                        y = gbs[:, c, P * (2 * p + h):P * (2 * p + h) + P]
                        V.scalar_tensor_tensor(y, okv[c][:, P * h:P * h + P], urs[:, 0, 2 * c + h:2 * c + h + 1], y,
                                               ALU.mult, ALU.mult).then_inc(yb_ok.sem, 1)

            def m_out(n, j):
                dve.wait_ge(e_ps.sem, e_ps.at(n, j + 1))
                if j == 2:
                    dve.wait_ge(eo.sem, eo.at(n, 1))
                c = j % 2
                V.tensor_tensor(mg[:, 512 * c:512 * c + 512], ring[c][:, :], gp[:, 512 * c:512 * c + 512], ALU.mult)\
                    .then_inc(mgd.sem, 1)

            def x_out(n, t):
                for c in range(2):
                    dve.wait_ge(esq[c].sem, esq[c].at(n, t + 1))
                base = newt_e.at(n, (NEWTON + 1) * t)
                V.tensor_tensor(essq[:, 2 * t:2 * t + 1], essq[:, 2 * t:2 * t + 1], essq[:, 2 * t + 1:2 * t + 2], ALU.add)\
                    .then_inc(newt_e.sem, 1)
                dve.wait_ge(newt_e.sem, base + 1)
                rsqrt_steps(1, essq[:, 2 * t:2 * t + 1], ers, D, base + 1, newt_e.sem)
                dve.wait_ge(mgd.sem, mgd.at(n, 2 * t + 2))
                dve.wait_ge(xrl.sem, xrl.at(n, 16 * t + 16))
                V.scalar_tensor_tensor(xr, mg, ers[:, 0, 0:1], xr, ALU.mult, ALU.add).then_inc(eo.sem, 1)

            def conv(n, p):
                dve.wait_ge(xa_sb.sem, xa_sb.at(n, p + 1))
                dve.wait_ge(hl_in.sem, hl_in.at(n, p + 1))
                dve.wait_ge(hst_ok.sem, hst_ok.at(n, p))
                dve.wait_ge(y_ok.sem, y_ok.at(n, p))
                for j in range(CW):
                    if j:
                        dve.wait_ge(cvc.sem, cvc.at(n, 8 * p + 2 * j))
                    for c in range(2):
                        src, w = xa[:, c, j:j + T], pcol("cw", CT * j + 2 * p + c)
                        if j == 0:
                            V.tensor_scalar(xc[:, c, :], src, w, pcol("cb", 2 * p + c), ALU.mult, ALU.add).then_inc(cvc.sem, 1)
                        else:
                            V.scalar_tensor_tensor(xc[:, c, :], src, w, xc[:, c, :], ALU.mult, ALU.add).then_inc(cvc.sem, 1)

            def input_scale(n, p):
                dve.wait_ge(a_sq.sem, a_sq.at(n, p + 1))
                dve.wait_ge(th_ok.sem, th_ok.at(n, 2 * p + 2))
                V.scalar_tensor_tensor(rr[:, :, :], xc[:, :, :], 1.0, rr[:, :, :], ALU.add, ALU.mult).then_inc(rx.sem, 1)
                dve.wait_ge(rx.sem, rx.at(n, p + 1))
                V.tensor_scalar_max(rr[:, :, :], rr[:, :, :], 0.0).then_inc(gd.sem, 1)

            def recur(n, p):
                dve.wait_ge(u_sqrt.sem, u_sqrt.at(n, p + 1))
                dve.wait_ge(ix_ok.sem, ix_ok.at(n, p + 1))
                V.tensor_tensor(ii[:, :, :], rr[:, :, :], ii[:, :, :], ALU.mult).then_inc(iu.sem, 1)
                dve.wait_ge(iu.sem, iu.at(n, p + 1))
                for c in range(2):
                    V.tensor_tensor_scan(xc[:, c, :], aa[:, c, :], ii[:, c, :], hst[:, 2 * p + c:2 * p + c + 1],
                                         ALU.mult, ALU.add).then_inc(scan.sem, 1)
                dve.wait_ge(scan.sem, scan.at(n, 2 * p + 2))
                dve.wait_ge(ga_sil.sem, ga_sil.at(n, p + 1))
                s = sil[:, 2 * p:2 * p + 2, :]
                V.tensor_tensor(s, xc[:, :, :], s, ALU.mult).then_inc(y_ok.sem, 1)

            def y_split(n):
                dve.wait_ge(yh_ok.sem, yh_ok.at(n, 1))
                V.tensor_tensor(yl[:, 0:CT, :], sil[:, :, :], yh[:, 0:CT, :], ALU.subtract).then_inc(yl_ok.sem, 1)

            def x_norm(m):
                dve.wait_ge(xsq.sem, xsq.at(m, 4))
                base = newt_x.at(m, 0)
                pairs = xssq[:, :].rearrange("p (t c) -> p t c", c=2)
                V.tensor_tensor(xssq[:, 0:2], pairs[:, :, 0], pairs[:, :, 1], ALU.add).then_inc(newt_x.sem, 1)
                dve.wait_ge(newt_x.sem, base + 1)
                rsqrt_steps(2, xssq[:, 0:2], xrs, D, base + 1, newt_x.sem)
                for t in range(NT):
                    V.tensor_scalar(xin[:, t, :], xin[:, t, :], xrs[:, 0, t:t + 1], None, ALU.mult).then_inc(xn_ok.sem, 1)

            def hn_rest(m, j):
                dve.wait_ge(hn_hi.sem, hn_hi.at(m, j + 1))
                V.tensor_tensor(hnl[:, 2 * j:2 * j + 2, :], aux[(j + 1) % 2][:, :].rearrange("p (k t) -> p k t", k=2),
                                hnh[:, 2 * j:2 * j + 2, :], ALU.subtract).then_inc(hn_lo.sem, 1)

            def rest(c):
                cols = slice(WI_COLS[c], WI_COLS[c] + 256)
                dve.wait_ge(w_hi, c + 1)
                V.tensor_tensor(wil[:, :, cols], stage[place["wi", c]], wih[:, :, cols], ALU.subtract).then_inc(w_lo, 1)

            def body(n, first, last_body):
                def weights(*which):
                    if first:
                        for c in which:
                            rest(c)

                if not first:
                    recur(n - 1, 1)
                weights(3)
                forget(n, 0)
                weights(4)
                if not first:
                    y_rest(n - 1, 0)
                    y_rest(n - 1, 1)
                    y_split(n - 1)
                for l in range(LEVELS + 1):
                    take(n, 0, l)
                    if l == 0:
                        weights(5)
                if not first:
                    m_out(n - 1, 0)
                state(n, 0, 0)
                if not first:
                    m_out(n - 1, 1)
                state(n, 0, 1)
                weights(6)
                rows(n, 0)
                weights(7, 8)
                if first:
                    dve.wait_ge(mod_ps, 6)
                    gate = aux[0][:, 0:KT * NS].rearrange("p (k s) -> p k s", s=NS)
                    link(V.tensor_tensor(gpt[:, :, :], gate, adab[:, 2 * KT:3 * KT, :], ALU.add))
                    V.tensor_tensor(gpt[:, :, :], gpt[:, :, :], post, ALU.mult).then_inc(gate_ok, 1)
                else:
                    x_out(n - 1, 0)
                forget(n, 1)
                weights(9, 10)
                take(n, 1, 0)
                conv(n, 0)
                weights(11)
                take(n, 1, 1)
                take(n, 1, 2)
                if not last_body:
                    x_norm(n + 1)
                take(n, 1, 3)
                take(n, 1, 4)
                take(n, 1, 5)
                input_scale(n, 0)
                take(n, 1, 6)
                recur(n, 0)
                if not last_body:
                    hn_rest(n + 1, 0)
                    hn_rest(n + 1, 1)
                take(n, 1, 7)
                conv(n, 1)
                if not last_body:
                    hn_rest(n + 1, 2)
                    hn_rest(n + 1, 3)
                if not first:
                    m_out(n - 1, 2)
                state(n, 1, 0)
                if not first:
                    m_out(n - 1, 3)
                state(n, 1, 1)
                rows(n, 1)
                input_scale(n, 1)
                if not first:
                    x_out(n - 1, 1)

            chain = [0]

            def link(ins):
                chain[0] += 1
                ins.then_inc(chain_dve, 1)
                dve.wait_ge(chain_dve, chain[0])

            dve.wait_ge(pre_act, 1)
            lam, lbl = par[:, ROW["lam"]:ROW["lam"] + CT], par[:, ROW["lbl"]:ROW["lbl"] + CT]
            link(V.tensor_scalar(tmp[:, 4, :], lam, -1.0, None, ALU.mult))
            link(V.tensor_tensor(tmp[:, 0, :], lam, tmp[:, 4, :], ALU.max))
            link(V.tensor_tensor(tmp[:, 2, :], lbl, lbl, ALU.subtract))
            V.memset(st[:, :, :], 0.0).then_inc(carry_zero, 1)
            V.memset(halo[:, :, :], 0.0).then_inc(carry_zero, 1)
            x_norm(0)
            dve.wait_ge(pre_act, 4)
            e, z, z2, s = tmp[:, 1, :], tmp[:, 5, :], tmp[:, 6, :], tmp[:, 7, :]
            link(V.tensor_scalar(s, e, 2.0, None, ALU.add))
            link(V.reciprocal(s, s))
            link(V.tensor_tensor(z, e, s, ALU.mult))
            link(V.tensor_tensor(z2, z, z, ALU.mult))
            link(V.tensor_scalar(s, z2, 1.0 / 17, None, ALU.mult))
            for d in (15, 13, 11, 9, 7, 5, 3):
                link(V.scalar_tensor_tensor(s, s, 1.0 / d, z2, ALU.add, ALU.mult))
            link(V.scalar_tensor_tensor(s, s, 1.0, z, ALU.add, ALU.mult))
            link(V.tensor_scalar(tmp[:, 4, :], tmp[:, 4, :], 0.0, None, ALU.max))
            link(V.scalar_tensor_tensor(s, s, 2.0, tmp[:, 4, :], ALU.mult, ALU.add))
            link(V.tensor_scalar(cpos[:, :], s, C_RGLRU, None, ALU.mult))
            link(V.tensor_scalar(cneg[:, :], s, -C_RGLRU, None, ALU.mult))
            link(V.reciprocal(s, tmp[:, 3, :]))
            link(V.tensor_tensor(s, tmp[:, 3, :], s, ALU.mult))
            link(V.tensor_tensor(lb[:, :], s, s, ALU.subtract))
            V.tensor_scalar(omlb[:, :], lb[:, :], -1.0, 1.0, ALU.mult, ALU.add).then_inc(lb_ok, 1)
            rest(0)
            dve.wait_ge(mod_ps, 4)
            adab = par[:, ROW["adab"]:ROW["adab"] + 3 * KT].unsqueeze(2).to_broadcast([P, 3 * KT, NS])
            pre = par[:, ROW["pre"]:ROW["pre"] + KT].unsqueeze(2).to_broadcast([P, KT, NS])
            post = par[:, ROW["post"]:ROW["post"] + KT].unsqueeze(2).to_broadcast([P, KT, NS])
            mod = ring[0][:, 0:2 * KT * NS].rearrange("p (k s) -> p k s", s=NS)
            link(V.tensor_tensor(shf[:, :, :], mod[:, 0:KT, :], adab[:, 0:KT, :], ALU.add))
            link(V.tensor_tensor(sc1[:, :, :], mod[:, KT:2 * KT, :], adab[:, KT:2 * KT, :], ALU.add))
            V.scalar_tensor_tensor(sc1[:, :, :], sc1[:, :, :], 1.0, pre, ALU.add, ALU.mult).then_inc(mod_ok, 1)
            rest(1)
            for j in range(4):
                hn_rest(0, j)
            rest(2)
            dve.wait_ge(zeroed, 3)

            body(0, True, False)
            with dve.Fori(1, BODIES - 1) as n:
                body(n, False, False)
            body(BODIES - 1, False, True)
            n = BODIES
            y_rest(n - 1, 0)
            y_rest(n - 1, 1)
            recur(n - 1, 1)
            y_split(n - 1)
            m_out(n - 1, 0)
            m_out(n - 1, 1)
            x_out(n - 1, 0)
            m_out(n - 1, 2)
            m_out(n - 1, 3)
            x_out(n - 1, 1)

            W4 = CT * TD
            dve.wait_ge(u_ps.sem, u_ps.at(BODIES, 0))
            link(V.memset(am[0:TD, :, 0:TD], 0.0))
            dve.wait_ge(scan.sem, scan.at(BODIES, 0))
            V.tensor_copy(aa[:, 1, :].rearrange("p (k b l) -> p k b l", k=KT, b=NB),
                          gpt[:, :, 1:].unsqueeze(3).to_broadcast([P, KT, NB, NL])).then_inc(dv("gprow"), 1)
            dve.wait_ge(dv("xsq_d"), 2)
            link(V.tensor_tensor(xssq[0:TD, 0:1], xssq[0:TD, 0:1], xssq[0:TD, 1:2], ALU.add))
            rsqrt_steps(1, xssq[0:TD, 0:1], xrs[0:TD, :, 0:1], D, 0, dv("newt_xd"))
            V.tensor_scalar(xin[0:TD, 0, :], xin[0:TD, 0, :], xrs[0:TD, 0, 0:1], None, ALU.mult).then_inc(dv("xn"), 1)
            dve.wait_ge(dv("turned"), 1)
            hx = rr[:, :, :].rearrange("p c t -> p (c t)")[:, 0:KT * TD]
            hx4 = hx.rearrange("p (k b l) -> p k b l", k=KT, b=NB)
            hx3 = hx.rearrange("p (k t) -> p k t", k=KT)
            seqs = lambda t: t[:, :, 1:].unsqueeze(3).to_broadcast([P, KT, NB, NL])
            link(V.tensor_tensor(hx4, aux[0][:, 0:KT * TD].rearrange("p (k b l) -> p k b l", k=KT, b=NB), seqs(sc1), ALU.mult))
            link(V.tensor_tensor(hx4, hx4, seqs(shf), ALU.add))
            link(V.tensor_copy(hnh[:, :, 0:TD], hx3))
            V.tensor_tensor(hnl[:, :, 0:TD], hx3, hnh[:, :, 0:TD], ALU.subtract).then_inc(dv("hn"), 1)
            V.tensor_copy(h0, aux[1][:, 0:TD]).then_inc(dv("carried"), 1)
            nj = NB * (CW - 1)
            V.tensor_copy(xad[:, :, :, 0:CW - 1],
                          aux[1][:, TD:TD + CT * nj].rearrange("p (c b j) -> p c b j", c=CT, b=NB)).then_inc(dv("carried"), 1)
            dve.wait_ge(dv("qfk_d"), 3)
            heads = lambda t: t[:, 0:W4].rearrange("p (h t) -> p h t", h=HB)
            percol = lambda t: t[:, :].unsqueeze(2).to_broadcast([P, HB, TD])
            link(V.tensor_tensor(heads(ff), heads(ff), percol(omlb), ALU.mult))
            link(V.tensor_tensor(heads(ff), heads(ff), percol(lb), ALU.add))
            link(V.tensor_scalar_max(ff[:, 0:W4], ff[:, 0:W4], F_MIN))
            V.tensor_tensor(heads(kk), heads(kk), percol(omlb), ALU.mult).then_inc(dv("level_in"), 1)
            dve.wait_ge(dv("level_in"), 1)
            for l in range(DLEVELS + 1):
                dve.wait_ge(dv("level_ps"), l + 1)
                if l == 0:
                    V.copy_predicated(am[0:TD, :, 0:TD], eye[0:TD, 0:TD].unsqueeze(1).to_broadcast([TD, HB, TD]),
                                      lev[0][0:TD, 0:W4].rearrange("p (h t) -> p h t", h=HB)).then_inc(dv("masked"), 1)
                    V.tensor_tensor(qq[:, 0:W4], qq[:, 0:W4], ff[:, 0:W4], ALU.mult).then_inc(dv("level_in"), 1)
                    dve.wait_ge(dv("level_in"), 2)
                    continue
                m = 1 << (l - 1)
                g = (ff[:, 0:W4] if m == 1 else gg[:, 0:W4 // 2]).rearrange("p (b two) -> p b two", two=2)
                nb = W4 // (2 * m)
                a = am[0:TD, :, 0:TD].rearrange("p h (b two m) -> p h b two m", two=2, m=m)
                x = lev[l % 2][0:TD, 0:W4 // 2].rearrange("p (h b m) -> p h b m", h=HB, m=m)
                msk = lmask[0:TD, l - 1, 0:TD // 2].rearrange("p (b m) -> p b m", m=m).unsqueeze(1)\
                    .to_broadcast([TD, HB, TD // (2 * m), m])
                dve.wait_ge(dv("masked"), l)
                V.copy_predicated(a[:, :, :, 1, :], msk, x).then_inc(dv("masked"), 1)
                qo, ke = blocks(qq[:, 0:W4], m)[:, :, 1, :], blocks(kk[:, 0:W4], m)[:, :, 0, :]
                link(V.tensor_tensor(qo, qo, g[:, :, 0:1].to_broadcast([P, nb, m]), ALU.mult))
                link(V.tensor_tensor(gg[:, (m - 1) * W4 // 2:(m - 1) * W4 // 2 + nb], g[:, :, 0], g[:, :, 1], ALU.mult))
                V.tensor_tensor(ke, ke, g[:, :, 1:2].to_broadcast([P, nb, m]), ALU.mult).then_inc(dv("level_in"), 1)
                dve.wait_ge(dv("level_in"), l + 2)
            g4 = gg[:, W4 // 2:W4 // 2 + HB * NB]
            dve.wait_ge(dv("xa_d"), 1)
            dve.wait_ge(dv("carried"), 2)
            for j in range(CW):
                for c in range(CT):
                    src, w = xad[:, c, :, j:j + NL], pcol("cw", CT * j + c)
                    dst = xcd[:, TD * c:TD * c + TD].rearrange("p (b l) -> p b l", b=NB)
                    if j == 0:
                        V.tensor_scalar(dst, src, w, pcol("cb", c), ALU.mult, ALU.add).then_inc(dv("conv_d"), 1)
                    else:
                        V.scalar_tensor_tensor(dst, src, w, dst, ALU.mult, ALU.add).then_inc(dv("conv_d"), 1)
                dve.wait_ge(dv("conv_d"), CT * (j + 1))
            link(V.tensor_copy(halod.rearrange("p (c b j) -> p c b j", c=CT, b=NB), xad[:, :, :, NL:]))
            dve.wait_ge(dv("usq_d"), HB)
            rsqrt_steps(HB, ussq[0:TD, :], urs[0:TD, :, :], P, 0, dv("newt_ud"))
            dve.wait_ge(dv("gb_sb"), 1)
            for h in range(HB):
                y = gbs[0:TD, 0, P * h:P * h + P]
                V.scalar_tensor_tensor(y, lev[1][0:TD, P * h:P * h + P], urs[0:TD, 0, h:h + 1], y, ALU.mult, ALU.mult)\
                    .then_inc(dv("yb_d"), 1)
            dve.wait_ge(dv("a_d"), 2 * CT)
            dve.wait_ge(dv("ri_d"), 2 * CT)
            link(V.tensor_tensor(iid, iid, xcd, ALU.mult))
            link(V.tensor_tensor(xcd, aad, aad, ALU.mult))
            link(V.scalar_tensor_tensor(rrd, xcd, 1.0, rrd, ALU.add, ALU.mult))
            V.tensor_scalar_max(rrd, rrd, 0.0).then_inc(dv("guard_d"), 1)
            dve.wait_ge(dv("root_d"), 1)
            link(V.tensor_tensor(iid, iid, rrd, ALU.mult))
            a0, u0 = (t.rearrange("p (s l) -> p s l", l=NL)[:, :, 0] for t in (aad, iid))
            link(V.tensor_tensor(h0, h0, a0, ALU.mult))
            link(V.tensor_tensor(u0, u0, h0, ALU.add))
            link(V.memset(a0, 0.0))
            link(V.tensor_tensor_scan(xcd, aad, iid, 0.0, ALU.mult, ALU.add))
            link(V.tensor_copy(hnew, xcd.rearrange("p (s l) -> p s l", l=NL)[:, :, NL - 1]))
            dve.wait_ge(dv("ga_d"), 1)
            yd = sil[:, 0, 0:W4]
            link(V.tensor_tensor(yd, xcd, yd, ALU.mult))
            V.tensor_copy(yh[:, 0:CT, 0:TD], yd.rearrange("p (c t) -> p c t", c=CT)).then_inc(dv("y_dec"), 1)
            dve.wait_ge(dv("y_dec"), 1)
            V.tensor_tensor(yl[:, 0:CT, 0:TD], yd.rearrange("p (c t) -> p c t", c=CT), yh[:, 0:CT, 0:TD], ALU.subtract)\
                .then_inc(dv("y_dec"), 1)
            dve.wait_ge(dv("ybt_ps"), 1)
            src = lev[0][:, 0:W4].rearrange("p (c t) -> p c t", c=CT)
            V.tensor_copy(yh[:, CT:, 0:TD], src).then_inc(dv("y_dec"), 1)
            dve.wait_ge(dv("y_dec"), 3)
            V.tensor_tensor(yl[:, CT:, 0:TD], src, yh[:, CT:, 0:TD], ALU.subtract).then_inc(dv("y_dec"), 1)
            for c in range(2):
                dve.wait_ge(dv("m_ps"), c + 1)
                V.tensor_tensor(mg[0:TD, 512 * c:512 * c + 512], ring[c][0:TD, :], gp[0:TD, 512 * c:512 * c + 512], ALU.mult)\
                    .then_inc(dv("mg_d"), 1)
            dve.wait_ge(dv("msq_d"), 2)
            link(V.tensor_tensor(essq[0:TD, 0:1], essq[0:TD, 0:1], essq[0:TD, 1:2], ALU.add))
            rsqrt_steps(1, essq[0:TD, 0:1], ers[0:TD, :, :], D, 0, dv("newt_md"))
            dve.wait_ge(dv("mg_d"), 2)
            dve.wait_ge(dv("xres"), 16)
            V.scalar_tensor_tensor(xr[0:TD, :], mg[0:TD, :], ers[0:TD, 0, 0:1], xr[0:TD, :], ALU.mult, ALU.add)\
                .then_inc(dv("y_rows"), 1)
            for b in range(NB):
                dve.wait_ge(dv("kv_ps"), b + 1)
                for h in range(HB):
                    s_ = s0[:, b, P * h:P * h + P]
                    V.scalar_tensor_tensor(s_, s_, g4[:, NB * h + b:NB * h + b + 1], kvp[:, P * h:P * h + P], ALU.mult, ALU.add)\
                        .then_inc(dv("s_new"), 1)

        @block.gpsimd
        def _(pool):
            G = nc.gpsimd

            def copy(out, src):
                ones = one[:, 0:1]
                for _ in range(len(src.shape) - 2):
                    ones = ones.unsqueeze(1)
                return G.tensor_tensor(out, src, ones.to_broadcast(list(src.shape)), ALU.mult)

            def bounds(n, p):
                pool.wait_ge(k_sig.sem, k_sig.at(n, p + 1))
                for h in range(2):
                    hd, cols = 2 * p + h, slice(T * h, T * h + T)
                    G.tensor_tensor(kk[:, cols], kk[:, cols], omlb[:, hd:hd + 1].to_broadcast([P, T]), ALU.mult)\
                        .then_inc(k_ok.sem, 1)
                for h in range(2):
                    hd, cols = 2 * p + h, slice(T * h, T * h + T)
                    G.tensor_scalar(ff[:, cols], ff[:, cols], omlb[:, hd:hd + 1], lb[:, hd:hd + 1], ALU.mult, ALU.add)\
                        .then_inc(f_af.sem, 1)

            def halo_in(n, p):
                pool.wait_ge(cvc.sem, cvc.at(n, 8 * p))
                pool.wait_ge(hl_sv.sem, hl_sv.at(n, p))
                copy(xa[:, :, 0:CW - 1], halo[:, 2 * p:2 * p + 2, :]).then_inc(hl_in.sem, 1)

            def halo_save(n, p):
                pool.wait_ge(xa_sb.sem, xa_sb.at(n, p + 1))
                pool.wait_ge(hl_in.sem, hl_in.at(n, p + 1))
                copy(halo[:, 2 * p:2 * p + 2, :], xa[:, :, T:T + CW - 1]).then_inc(hl_sv.sem, 1)

            def gated(n, p):
                pool.wait_ge(i_sig.sem, i_sig.at(n, 2 * p + 2))
                G.tensor_tensor(ii[:, :, :], ii[:, :, :], xc[:, :, :], ALU.mult).then_inc(ix_ok.sem, 1)
                pool.wait_ge(a_exp.sem, a_exp.at(n, 2 * p + 2))
                pool.wait_ge(ix_ok.sem, ix_ok.at(n, p + 1))
                G.tensor_tensor(xc[:, :, :], aa[:, :, :], aa[:, :, :], ALU.mult).then_inc(a_sq.sem, 1)

            def h_save(n, p):
                pool.wait_ge(scan.sem, scan.at(n, 2 * p + 2))
                copy(hst[:, 2 * p:2 * p + 2], xc[:, :, T - 1]).then_inc(hst_ok.sem, 1)

            def y_head(n):
                pool.wait_ge(y_ok.sem, y_ok.at(n, 2))
                pool.wait_ge(u_ps.sem, u_ps.at(n, 4))
                pool.wait_ge(wo_lo, NWO)
                copy(yh[:, 0:CT, :], sil[:, :, :]).then_inc(yh_ok.sem, 1)

            def rest(c):
                cols = slice(256 * c, 256 * c + 256)
                pool.wait_ge(w_lo, NWI)
                pool.wait_ge(w_hi, NWI + c + 1)
                G.tensor_tensor(wol[:, :, cols], stage[place["wo", c]], woh[:, :, cols], ALU.subtract).then_inc(wo_lo, 1)

            def body(n, first):
                bounds(n, 0)
                if not first:
                    h_save(n - 1, 1)
                    y_head(n - 1)
                halo_in(n, 0)
                bounds(n, 1)
                halo_save(n, 0)
                gated(n, 0)
                halo_in(n, 1)
                h_save(n, 0)
                halo_save(n, 1)
                if first:
                    rest(0)
                    rest(1)
                gated(n, 1)
                if first:
                    rest(2)
                    rest(3)

            gc = [0]

            def link(ins):
                gc[0] += 1
                ins.then_inc(chain_pool, 1)
                pool.wait_ge(chain_pool, gc[0])

            link(G.memset(one[:, :], 1.0))
            link(G.memset(ident[:, :], 0.0))
            G.affine_select(out=ident[:, :], in_=ident[:, :], pattern=[[-1, P]], compare_op=ALU.not_equal, fill=1.0,
                            base=0, channel_multiplier=1).then_inc(consts, 1)
            G.memset(wg[:, :, :, :], 0.0).then_inc(zeroed, 1)
            pool.wait_ge(consts, 1)
            link(G.tensor_copy(eye[:, :], ident[:, :]))
            mf = ktr[:, 0, 0:P // 2]
            for l in range(LEVELS):
                m = 1 << l
                v = mf.rearrange("p (b m) -> p b m", m=m)
                pat = [[-2 * m, P // (2 * m)], [0, m]]
                link(G.memset(mf, 1.0))
                link(G.affine_select(out=v, in_=v, pattern=pat, compare_op=ALU.is_ge, fill=0.0, base=0, channel_multiplier=1))
                link(G.affine_select(out=v, in_=v, pattern=[[2 * m, P // (2 * m)], [0, m]], compare_op=ALU.is_ge, fill=0.0,
                                     base=m - 1, channel_multiplier=-1))
                link(G.tensor_copy(lmask[:, l, :], mf))
            sm = ktr[0:TD, 1, 0:NB]
            link(G.memset(sm, 1.0))
            link(G.affine_select(out=sm, in_=sm, pattern=[[-NL, NB]], compare_op=ALU.is_ge, fill=0.0, base=0, channel_multiplier=1))
            link(G.affine_select(out=sm, in_=sm, pattern=[[NL, NB]], compare_op=ALU.is_ge, fill=0.0, base=NL - 1,
                                 channel_multiplier=-1))
            link(G.tensor_copy(smask[:, :], sm))
            G.memset(hst[:, :], 0.0).then_inc(zeroed, 1)
            pool.wait_ge(pre_ps, 1)
            G.memset(am[:, :, :], 0.0).then_inc(zeroed, 1)
            pool.wait_ge(carry_zero, 2)
            pool.wait_ge(lb_ok, 1)

            body(0, True)
            with pool.Fori(1, BODIES - 1) as n:
                body(n, False)
            body(BODIES - 1, False)
            h_save(BODIES - 1, 1)
            y_head(BODIES - 1)
            pool.wait_ge(dv("v_d"), 1)
            pool.wait_ge(dv("gb_sb"), 1)
            for b in range(NB):
                if b >= 2:
                    pool.wait_ge(dv("kv_ps"), b - 1)
                G.tensor_scalar(vseq(b), vv[0:TD, 0, :], smask[:, b:b + 1], None, ALU.mult).then_inc(dv("v_seq"), 1)


_INS = ['x_prompt', 'x_sample', 'state_rglru_h', 'state_rglru_conv', 'state_hgrn_S', 'c_prompt', 'c_sample', 'ada_w',
        'ada_b', 'pre_norm_w', 'post_norm_w', 'w_in', 'conv_w', 'conv_b', 'rg_wa', 'rg_ba', 'rg_wx', 'rg_bx',
        'rg_lambda', 'hg_lb_logits', 'hg_onorm_w', 'w_out']
_OUTS = [(1, SEQ, D), (NB, NL, D), (1, 1, DA), (1, 1, CW - 1, DA), (1, 1, HB, P, P), (1, NB, DA), (1, NB, CW - 1, DA),
         (1, NB, HB, P, P)]


def kernel(**inputs):
    import numpy as _np
    import concourse.bacc as _bacc
    from concourse import mybir as _mybir
    from concourse.bass_utils import run_bass_kernel_spmd as _run

    nc = _bacc.Bacc("TRN2", target_bir_lowering=False, num_devices=1)
    arrays, args = {}, []
    for name in _INS:
        a = _np.ascontiguousarray(inputs[name])
        arrays[f"in_{name}_dram"] = a
        args.append(nc.dram_tensor(f"in_{name}_dram", a.shape, _mybir.dt.from_np(a.dtype), kind="ExternalInput").ap())
    for i, shape in enumerate(_OUTS):
        args.append(nc.dram_tensor(f"out_{i}_dram", shape, _mybir.dt.float32, kind="ExternalOutput").ap())
    build(nc, *args)
    r = _run(nc, [arrays], core_ids=[0])
    return tuple(r.results[0][f"out_{i}_dram"] for i in range(len(_OUTS)))
```

```python
from contextlib import ExitStack

import concourse.bass as bass
from concourse import mybir

F32 = mybir.dt.float32
BF16 = mybir.dt.bfloat16
F16 = mybir.dt.float16
U8 = mybir.dt.uint8
I32 = mybir.dt.int32
ALU = mybir.AluOpType
ACT = mybir.ActivationFunctionType

P = 128
D = 1024
KT = D // P
DA = 512
CT = DA // P
HB = 4
PIN = 2 * DA + 4 * DA
SEQ = 2048
T = 256
NT = T // P
BODIES = SEQ // T
CW = 4
NB, NL = 8, 4
TD = NB * NL
NS = 1 + NB
EPS = 1e-6
F_MIN = 1e-30
C_RGLRU = 8.0
LEVELS = 7
DLEVELS = 2
NEWTON = 12
MAGIC = float(0x5F3759DF)

XA, GA, Q_, FR, IV, GB = (i * DA for i in range(6))
ROW = {}
_at = 0
for _name, _n in (("pre", KT), ("post", KT), ("cw", CW * CT), ("cb", CT), ("ba", CT), ("bx", CT), ("lam", CT),
                  ("lbl", CT), ("onw", CT), ("adab", 3 * KT)):
    ROW[_name] = _at
    _at += _n
NROW = _at


def build(nc, x_prompt, x_sample, state_rglru_h, state_rglru_conv, state_hgrn_S, c_prompt, c_sample, ada_w, ada_b,
          pre_norm_w, post_norm_w, w_in, conv_w, conv_b, rg_wa, rg_ba, rg_wx, rg_bx, rg_lambda, hg_lb_logits,
          hg_onorm_w, w_out, y_prompt, y_sample, h_prompt, conv_prompt, S_prompt, h_sample, conv_sample, S_sample):
    with ExitStack() as ctx:
        def sb(name, shape, dt=F32):
            return ctx.enter_context(nc.sbuf_tensor(name, shape, dt))

        def sem(name):
            return ctx.enter_context(nc.semaphore(name))

        wih = sb("wih", [P, KT, PIN], F16)
        wil = sb("wil", [P, KT, PIN], BF16)
        woh = sb("woh", [P, KT, D], F16)
        wol = sb("wol", [P, KT, D], BF16)
        work = sb("work", [P, 4 * D])
        halves = lambda t: [t[:, 2048 * i:2048 * i + 2048].rearrange("p (k n) -> p k n", k=KT)
                            for i in range(t.shape[1] // 2048)]
        as_f32 = lambda t: t[:, :, :].rearrange("p k n -> p (k n)").bitcast(F32)
        stage = halves(work[:, :]) + halves(as_f32(woh)) + halves(as_f32(wol))
        early = halves(as_f32(wil))[0:2]
        xr = work[:, 0:D]
        mg = work[:, D:2 * D]
        yh = work[:, 2048:3072].bitcast(BF16).rearrange("p (k t) -> p k t", k=KT)
        yl = work[:, 3072:4096].bitcast(F16).rearrange("p (k t) -> p k t", k=KT)
        hnh = sb("hnh", [P, KT, T], BF16)
        hnl = sb("hnl", [P, KT, T], F16)
        xin = sb("xin", [P, NT, D])
        gp = sb("gp", [P, D])
        xa = sb("xa", [P, 2, T + CW - 1])
        halo = sb("halo", [P, CT, CW - 1])
        xc = sb("xc", [P, 2, T])
        rr = sb("rr", [P, 2, T])
        ii = sb("ii", [P, 2, T])
        aa = sb("aa", [P, 2, T])
        sil = sb("sil", [P, CT, T])
        wg = sb("wg", [P, 2, CT, P])
        qq = sb("qq", [P, 2 * T])
        kk = sb("kk", [P, 2 * T])
        ff = sb("ff", [P, 2 * T])
        gg = sb("gg", [P, 2 * T - 4])
        am = sb("am", [P, 4, P])
        ktr = sb("ktr", [P, 4, P])
        vv = sb("vv", [P, NT, DA])
        gbs = sb("gbs", [P, NT, DA])
        st = sb("st", [P, HB, P])
        ident = sb("ident", [P, P])
        eye = sb("eye", [P, P], U8)
        lmask = sb("lmask", [P, LEVELS, P // 2], U8)
        smask = sb("smask", [TD, NB])
        junk = sb("junk", [P, 640], BF16)
        cols = sb("cols", [P, 5 * CT])
        lb, omlb, cneg, cpos, hst = (cols[:, CT * i:CT * i + CT] for i in range(5))
        tmp = xc[:, 1, 0:8 * CT].rearrange("p (a b) -> p a b", b=CT)
        par = sb("par", [P, NROW])
        sc1 = sb("sc1", [P, KT, NS])
        shf = sb("shf", [P, KT, NS])
        gpt = sb("gpt", [P, KT, NS])
        stat = sb("stat", [P, 35])
        ussq, essq, xssq, one = stat[:, 0:4], stat[:, 4:8], stat[:, 8:12], stat[:, 33:34]
        urs = stat[:, 12:24].rearrange("p (a b) -> p a b", a=3)
        ers = stat[:, 24:27].rearrange("p (a b) -> p a b", a=3)
        xrs = stat[:, 27:33].rearrange("p (a b) -> p a b", a=3)

        def goff(m):
            return sum(2 * T // b for b in (2, 4, 8, 16, 32, 64) if b < m)

        ring = [ctx.enter_context(nc.psum_tensor(f"ring{i}", [P, 512], F32)) for i in range(2)]
        aux = [ctx.enter_context(nc.psum_tensor(f"aux{i}", [P, 512], F32)) for i in range(2)]
        lev = [ctx.enter_context(nc.psum_tensor(f"lev{i}", [P, 512], F32)) for i in range(2)]
        okv = [ctx.enter_context(nc.psum_tensor(f"okv{i}", [P, 512], F32)) for i in range(2)]

        x_banks = (aux[1], aux[0], okv[0], okv[1])

        class Signal:

            def __init__(self, name, per):
                self.sem, self.per = sem(name), per

            def at(self, n, j):
                return n * self.per + j

        fr_ps, q_ps, iv_ps, gb_ps, xa_ps, ga_ps = (Signal(s, 2) for s in ("fr_ps", "q_ps", "iv_ps", "gb_ps", "xa_ps", "ga_ps"))
        e_ps = Signal("e_ps", 4)
        tr_ps, yt_ps, kt_ps = Signal("tr_ps", 4), Signal("yt_ps", 2), Signal("kt_ps", 2)
        lev_ps = Signal("lev_ps", 2 * (LEVELS + 1))
        u_ps = Signal("u_ps", 4)
        gr_ps, gi_ps = Signal("gr_ps", 2), Signal("gi_ps", 2)
        f_sig, k_sig, q_sb = Signal("f_sig", 2), Signal("k_sig", 2), Signal("q_sb", 2)
        v_sb, gb_sil, kt_sb = Signal("v_sb", 2), Signal("gb_sil", 2), Signal("kt_sb", 2)
        esq = [Signal("esq0", 2), Signal("esq1", 2)]
        usq, xsq = Signal("usq", 8), Signal("xsq", 4)
        xa_sb, ga_sil = Signal("xa_sb", 2), Signal("ga_sil", 2)
        r_sig, i_sig, a_exp, th_ok = (Signal(s, 4) for s in ("r_sig", "i_sig", "a_exp", "th_ok"))
        u_sqrt = Signal("u_sqrt", 2)
        aff, hn_hi, yth = Signal("aff", 8), Signal("hn_hi", 4), Signal("yth", 2)
        f_ok, q_f = Signal("f_ok", 2), Signal("q_f", 2)
        amask = Signal("amask", 2 * (LEVELS + 1))
        q_upd, k_upd, g_upd = (Signal(s, 2 * LEVELS) for s in ("q_upd", "k_upd", "g_upd"))
        s_upd, newt_u, yb_ok = Signal("s_upd", 8), Signal("newt_u", 2 * NEWTON), Signal("yb_ok", 8)
        mgd, newt_e, eo = Signal("mgd", 4), Signal("newt_e", 2 * (NEWTON + 1)), Signal("eo", 2)
        newt_x, xn_ok = Signal("newt_x", NEWTON + 1), Signal("xn_ok", 2)
        hn_lo, ytl, yl_ok = Signal("hn_lo", 4), Signal("ytl", 2), Signal("yl_ok", 1)
        cvc = Signal("cvc", 4 * CW)
        rx, gd, iu, scan, y_ok = Signal("rx", 2), Signal("gd", 2), Signal("iu", 2), Signal("scan", 4), Signal("y_ok", 2)
        k_ok, f_af = Signal("k_ok", 4), Signal("f_af", 4)
        ix_ok, a_sq, yh_ok = Signal("ix_ok", 2), Signal("a_sq", 2), Signal("yh_ok", 1)
        hl_in, hl_sv, hst_ok = Signal("hl_in", 2), Signal("hl_sv", 2), Signal("hst_ok", 2)
        xld = [Signal("xld0", 16), Signal("xld1", 16)]
        xrl, ost = Signal("xrl", 32), Signal("ost", 32)
        par_ld, c_ld, wg_ld = sem("par_ld"), sem("c_ld"), sem("wg_ld")
        st_ld = [sem(f"st_ld{i}") for i in range(len(stage))]
        early_ld = [sem(f"early_ld{i}") for i in range(len(early))]
        fin = sem("fin")
        ident_ok, lb_ok = sem("ident_ok"), sem("lb_ok")
        zeroed, carry_zero = sem("zeroed"), sem("carry_zero")
        pre_ps = sem("pre_ps")
        pre_sb = sem("pre_sb")
        ada_ps, mod_sb, mod_ps = sem("ada_ps"), sem("mod_sb"), sem("mod_ps")
        mod_ok, gate_ok, gp_ps, gp_sb = sem("mod_ok"), sem("gate_ok"), sem("gp_ps"), sem("gp_sb")
        w_hi = sem("w_hi")
        w_lo, wo_lo, w_fold = sem("w_lo"), sem("wo_lo"), sem("w_fold")
        d_ld, d_s0 = sem("d_ld"), sem("d_s0")
        chain_dve, chain_pool = sem("chain_dve"), sem("chain_pool")
        decode_sems = {}

        def dv(name):
            if name not in decode_sems:
                decode_sems[name] = sem("d_" + name)
            return decode_sems[name]

        xp_rows = x_prompt[0].rearrange("(m p) d -> m p d", p=P)
        yp_rows = y_prompt[0].rearrange("(m p) d -> m p d", p=P)
        w_in_v = w_in[0].rearrange("(k p) n -> p k n", p=P)
        w_out_v = w_out[0].rearrange("(k p) n -> p k n", p=P)
        ada_v = ada_w[0].rearrange("(k p) n -> p k n", p=P)

        NEARLY, NADA, NWI, NWO = 2 * D // 256, 3 * D // 256, PIN // 256, D // 256
        WI_COLS = (FR, Q_, IV, IV + 256, GB, GB + 256, FR + 256, Q_ + 256, XA, GA, XA + 256, GA + 256)
        pieces = ([("ada", i) for i in range(len(early), NEARLY)] + [("wi", i) for i in range(6)]
                  + [("ada", i) for i in range(NEARLY, NADA)] + [("wi", i) for i in range(6, NWI)] + [("wo", i) for i in range(NWO)])
        place, landed, before = {}, {}, {}
        users = [[] for _ in stage]
        for _i, _piece in enumerate(pieces):
            _s = _i % 2 if _piece[0] == "wo" else _i % len(stage)
            place[_piece], landed[_piece] = _s, 16 * (len(users[_s]) + 1)
            before[_piece] = users[_s][-1] if users[_s] else None
            users[_s].append(_piece)

        def blocks(t, m):
            return t.rearrange("p (b two m) -> p b two m", two=2, m=m)

        def products(m):
            g = ff[:, :] if m == 1 else gg[:, goff(m):goff(m) + 2 * T // m]
            return g.rearrange("p (b two) -> p b two", two=2)

        def pcol(name, i):
            return par[:, ROW[name] + i:ROW[name] + i + 1]

        W4 = CT * TD
        flat = lambda t: t[:, :, :].rearrange("p c t -> p (c t)")

        def of(t, start, size):
            return flat(t)[:, start:start + size]

        hx, gprow = of(xin, 0, KT * TD), of(xin, 256, KT * TD)
        xad = of(xin, 512, CT * NB * (CW - 1 + NL)).rearrange("p (c b j) -> p c b j", c=CT, b=NB)
        h0, hnew = of(xin, 736, CT * NB), of(xin, 768, CT * NB)
        halod, sild = of(xin, 800, CT * NB * (CW - 1)), of(xin, 896, W4)
        xcd, rrd, iid, aad = (of(xin, D + W4 * i, W4) for i in range(4))
        wilf = as_f32(wil)
        gpd, xrd, mgr = (wilf[0:TD, D * i:D * i + D] for i in range(3))
        yhd = wilf[:, 3 * D:3 * D + 128].bitcast(BF16).rearrange("p (k t) -> p k t", k=KT)
        yld = wilf[:, 3 * D + 128:3 * D + 256].bitcast(F16).rearrange("p (k t) -> p k t", k=KT)
        dsum = wilf[0:TD, 3 * D + 256:3 * D + 260]
        drs = wilf[0:TD, 3 * D + 260:3 * D + 272].rearrange("p (a b) -> p a b", a=3)
        qz = wilf[:, 6 * D:6 * D + HB * NB * (TD + NL)].rearrange("p (h b s) -> p h b s", h=HB, b=NB)
        qzh = wilf[:, 6 * D:6 * D + HB * NB * (TD + NL)].rearrange("p (h s) -> p h s", h=HB)
        rows_out = [wilf[:, 4 * D + 512 * i:4 * D + 512 * i + 512] for i in range(4)]
        s0 = wih[:, :, 0:2 * HB * P].bitcast(F32)

        def vseq(b):
            return (vv, gbs)[b % 2][0:TD, 1, :]

        mod_rows = [qq[:, :], kk[:, :], ff[:, :], vv[:, 0, :], flat(rr), flat(ii)]

        block = ctx.enter_context(nc.Block())

        @block.sync
        def _(sp):
            def load_x(m, t):
                sp.wait_ge(tr_ps.sem, tr_ps.at(m - 1, 4))
                sp.dma_start(xin[:, t, :], xp_rows[m * NT + t]).then_inc(xld[t].sem, 16)

            sp.dma_start(gp[0:1, :], c_prompt).then_inc(c_ld, 16)
            sp.dma_start(gp[1:NS, :], c_sample).then_inc(c_ld, 16)
            for i in range(len(early)):
                sp.dma_start(early[i], ada_v[:, :, 256 * i:256 * i + 256]).then_inc(early_ld[i], 16)
            loads = [("pre", pre_norm_w[0]), ("post", post_norm_w[0]), ("cw", conv_w[0].rearrange("j c -> (j c)")),
                     ("cb", conv_b[0]), ("ba", rg_ba[0]), ("bx", rg_bx[0]), ("lam", rg_lambda[0]),
                     ("lbl", hg_lb_logits[0]), ("onw", hg_onorm_w[0]), ("adab", ada_b[0])]
            for name, src in loads:
                rows = src.rearrange("(r c) -> r c", c=P)
                sp.dma_start(am[ROW[name]:ROW[name] + rows.shape[0], 0, :], rows).then_inc(par_ld, 16)
            for i, (kind, c) in enumerate(pieces):
                if i == 3:
                    for t in range(NT):
                        sp.dma_start(xin[:, t, :], xp_rows[t]).then_inc(xld[t].sem, 16)
                if i == 13:
                    for t in range(NT):
                        load_x(1, t)
                if before[kind, c]:
                    pk, pc = before[kind, c]
                    if pk == "ada":
                        sp.wait_ge(ada_ps, pc + 1)
                    else:
                        sp.wait_ge(*((w_lo, pc + 1) if pk == "wi" else (wo_lo, pc + 1)))
                src, col = {"ada": (ada_v, 256 * c), "wi": (w_in_v, WI_COLS[c % NWI]), "wo": (w_out_v, 256 * c)}[kind]
                sp.dma_start(stage[place[kind, c]], src[:, :, col:col + 256]).then_inc(st_ld[place[kind, c]], 16)
                if i == 6:
                    sp.wait_ge(zeroed, 1)
                    for w, src in ((0, rg_wa), (1, rg_wx)):
                        for odd in range(2):
                            v = src[0].rearrange("(t two) c d -> two c t d", two=2)[odd]
                            sp.dma_start(wg[64 * odd:64 * odd + 64, w, :, 64 * odd:64 * odd + 64], v).then_inc(wg_ld, 16)

            def residual(n, t):
                sp.dma_start(xr, xp_rows[n * NT + t]).then_inc(xrl.sem, 16)
                sp.wait_ge(eo.sem, eo.at(n, t + 1))
                sp.dma_start(yp_rows[n * NT + t], xr).then_inc(ost.sem, 16)
                sp.wait_ge(ost.sem, ost.at(n, 16 * t + 16))

            sp.wait_ge(wo_lo, NWO)
            for t in range(NT):
                load_x(2, t)
            with sp.Fori(1, BODIES - 2) as n:
                residual(n - 1, 0)
                load_x(n + 2, 0)
                residual(n - 1, 1)
                load_x(n + 2, 1)
            for t in range(NT):
                residual(BODIES - 3, t)
            sp.wait_ge(tr_ps.sem, tr_ps.at(BODIES - 1, 4))
            sp.dma_start(xin[0:TD, 0, :], x_sample.rearrange("b l d -> (b l) d")).then_inc(d_ld, 16)
            sp.dma_start(xin[0:NB, 1, 0:DA], state_rglru_h[0]).then_inc(d_ld, 16)
            sp.dma_start(xin[0:NB * (CW - 1), 1, DA:D], state_rglru_conv[0].rearrange("b j c -> (b j) c")).then_inc(d_ld, 16)
            for t in range(NT):
                residual(BODIES - 2, t)
            sp.wait_ge(dv("proj_ps"), 1)
            for b in range(NB):
                sp.dma_start(s0[:, b, :].rearrange("p (h v) -> p h v", h=HB),
                             state_hgrn_S[0, b].rearrange("h k v -> k h v")).then_inc(d_s0, 16)
            sp.wait_ge(dv("gb_d"), 1)
            sp.dma_start(xrd, x_sample.rearrange("b l d -> (b l) d")).then_inc(dv("xres"), 16)
            sp.wait_ge(s_upd.sem, s_upd.at(BODIES, 0))
            sp.dma_start(S_prompt[0, 0].rearrange("h k v -> k h v"), st[:, :, :]).then_inc(fin, 16)
            for t in range(NT):
                residual(BODIES - 1, t)
            for b in range(NB):
                sp.wait_ge(dv("s_new"), HB * (b + 1))
                sp.dma_start(S_sample[0, b].rearrange("h k v -> k h v"),
                             s0[:, b, :].rearrange("p (h v) -> p h v", h=HB)).then_inc(fin, 16)
                if b == 5:
                    sp.wait_ge(dv("y_rows"), 1)
                    sp.dma_start(y_sample.rearrange("b l d -> (b l) d"), xrd).then_inc(fin, 16)
                    sp.wait_ge(dv("rows_sb"), 4)
                    sp.dma_start(conv_sample[0].rearrange("b j c -> (b j) c"), rows_out[0][0:NB * (CW - 1), :]).then_inc(fin, 16)
                    sp.dma_start(h_sample[0], rows_out[1][0:NB, :]).then_inc(fin, 16)
                    sp.dma_start(conv_prompt[0, 0], rows_out[2][0:CW - 1, :]).then_inc(fin, 16)
                    sp.dma_start(h_prompt[0].rearrange("a (c p) -> (a c) p", p=P), rows_out[3][0:CT, 0:P]).then_inc(fin, 16)
            sp.wait_ge(fin, 16 * (2 + NB + 4))

        @block.tensor
        def _(pe):
            mm = nc.tensor.matmul

            def split3(out, lh, ll, rh, rl, ks, start, stop):
                last = None
                for k in ks:
                    for j, (a, b) in enumerate(((lh, rh), (lh, rl), (ll, rh))):
                        last = mm(out, a(k), b(k), start=start and k == ks[0] and j == 0,
                                  stop=stop and k == ks[-1] and j == 2)
                return last

            def project(bank, col, c, n=None):
                lo = col + P * c
                for j in range(KT // 2):
                    if n is not None:
                        pe.wait_ge(hn_lo.sem, hn_lo.at(n, j + 1))
                    last = split3(bank[:, T * c:T * c + T], lambda k: wih[:, k, lo:lo + P], lambda k: wil[:, k, lo:lo + P],
                                  lambda k: hnh[:, k, :], lambda k: hnl[:, k, :], range(2 * j, 2 * j + 2),
                                  j == 0, j == KT // 2 - 1)
                return last

            def project_rows(bank, col, t, half):
                lo = P * t
                ks = range(KT // 2) if half == 0 else range(KT // 2, KT)
                return split3(bank[:, :], lambda k: hnh[:, k, lo:lo + P], lambda k: hnl[:, k, lo:lo + P],
                              lambda k: wih[:, k, col:col + DA], lambda k: wil[:, k, col:col + DA], ks,
                              half == 0, half == 1)

            def out_rows(bank, t, cols, ks):
                lo, co = P * t, 512 * cols
                return split3(bank[:, :], lambda k: yh[:, k, lo:lo + P], lambda k: yl[:, k, lo:lo + P],
                              lambda k: woh[:, k, co:co + 512], lambda k: wol[:, k, co:co + 512], ks,
                              ks[0] == 0, ks[-1] == KT - 1)

            def turn_x(m, j):
                if j == 0:
                    pe.wait_ge(xn_ok.sem, xn_ok.at(m, NT))
                bank = x_banks[j]
                for k in (2 * j, 2 * j + 1):
                    for t in range(NT):
                        last = nc.tensor.transpose(bank[:, (k % 2) * T + P * t:(k % 2) * T + P * t + P],
                                                   xin[:, t, P * k:P * k + P], ident[:, :])
                last.then_inc(tr_ps.sem, 1)

            def turn_y(n, j):
                if j == 0:
                    pe.wait_ge(yb_ok.sem, yb_ok.at(n, 8))
                    pe.wait_ge(r_sig.sem, r_sig.at(n, 4))
                else:
                    pe.wait_ge(i_sig.sem, i_sig.at(n, 4))
                for h in range(2):
                    for t in range(NT):
                        last = nc.tensor.transpose(aux[j][:, T * h + P * t:T * h + P * t + P],
                                                   gbs[:, t, P * (2 * j + h):P * (2 * j + h) + P], ident[:, :])
                last.then_inc(yt_ps.sem, 1)

            def level(n, p, l):
                i = p * (LEVELS + 1) + l
                if i >= 2 or not isinstance(n, int) or n > 0:
                    pe.wait_ge(amask.sem, amask.at(n, i - 1))
                if l == 0:
                    pe.wait_ge(q_sb.sem, q_sb.at(n, p + 1))
                    pe.wait_ge(k_ok.sem, k_ok.at(n, 2 * p + 2))
                elif l == 1:
                    pe.wait_ge(q_f.sem, q_f.at(n, p + 1))
                else:
                    pe.wait_ge(q_upd.sem, q_upd.at(n, LEVELS * p + l - 1))
                    pe.wait_ge(k_upd.sem, k_upd.at(n, LEVELS * p + l - 1))
                m = 1 << (l - 1) if l else 0
                for hc in range(4):
                    q, k = qq[:, P * hc:P * hc + P], kk[:, P * hc:P * hc + P]
                    if l == 0:
                        last = mm(lev[i % 2][:, P * hc:P * hc + P], k, q, start=True, stop=True)
                    elif m < 32:
                        last = mm(lev[i % 2][:, P // 2 * hc:P // 2 * hc + P // 2], k, blocks(q, m)[:, :, 1, :],
                                  start=True, stop=True)
                    else:
                        for s in range(0, P, 2 * m):
                            o = P // 2 * hc + s // 2
                            last = mm(lev[i % 2][s:s + m, o:o + m], k[:, s:s + m], q[:, s + m:s + 2 * m],
                                      start=True, stop=True)
                last.then_inc(lev_ps.sem, 1)

            def turn_k(n, p):
                pe.wait_ge(q_upd.sem, q_upd.at(n, LEVELS * p + LEVELS))
                pe.wait_ge(k_upd.sem, k_upd.at(n, LEVELS * p + LEVELS))
                for hc in range(4):
                    last = nc.tensor.transpose(aux[p][:, P * hc:P * hc + P], kk[:, P * hc:P * hc + P], ident[:, :])
                last.then_inc(kt_ps.sem, 1)

            def unit(n, p, c):
                ui = 2 * p + c
                pe.wait_ge(amask.sem, amask.at(n, 8 * p + 8))
                pe.wait_ge(v_sb.sem, v_sb.at(n, c + 1))
                pe.wait_ge(kt_sb.sem, kt_sb.at(n, p + 1))
                pe.wait_ge(yb_ok.sem, yb_ok.at(n, 4 * p))
                pe.wait_ge(s_upd.sem, s_upd.at(n, 2 * ui))
                for h in range(2):
                    hc, hd = 2 * h + c, 2 * p + h
                    v = vv[:, c, P * hd:P * hd + P]
                    mm(okv[c][:, P * h:P * h + P], am[:, hc, :], v, start=True, stop=False)
                    mm(okv[c][:, P * h:P * h + P], qq[:, P * hc:P * hc + P], st[:, hd, :], start=False, stop=True)
                    last = mm(okv[c][:, 2 * P + P * h:3 * P + P * h], ktr[:, hc, :], v, start=True, stop=True)
                last.then_inc(u_ps.sem, 1)

            def gates(n, p):
                pe.wait_ge(cvc.sem, cvc.at(n, 8 * p + 8))
                for w, s in ((0, gr_ps), (1, gi_ps)):
                    if p == 0 and w == 0:
                        if not isinstance(n, int) or n > 0:
                            pe.wait_ge(ytl.sem, ytl.at(n - 1, 2))
                    elif w == 1:
                        pe.wait_ge(kt_sb.sem, kt_sb.at(n, p + 1))
                    elif not (isinstance(n, int) and n == BODIES - 1):
                        pe.wait_ge(hn_lo.sem, hn_lo.at(n + 1, 2))
                    for c in range(2):
                        last = mm(aux[(1 + w + p) % 2][:, T * c:T * c + T], wg[:, w, 2 * p + c, :], xc[:, c, :],
                                  start=True, stop=True)
                    last.then_inc(s.sem, 1)

            def ada(i, bank):
                if i < len(early):
                    pe.wait_ge(early_ld[i], 16)
                    w = early[i]
                else:
                    pe.wait_ge(st_ld[place["ada", i]], landed["ada", i])
                    w = stage[place["ada", i]]
                o = 256 * (i % 2)
                for k in range(KT):
                    last = mm(bank[0:NS, o:o + 256], siluc[:, k, :], w[:, k, :], start=k == 0, stop=k == KT - 1)
                last.then_inc(ada_ps, 1)

            def turn_mod(b, bank, o):
                pe.wait_ge(mod_sb, b + 1)
                for j in range(4):
                    last = nc.tensor.transpose(bank[:, o + NS * j:o + NS * j + NS], mod_rows[b][0:NS, P * j:P * j + P],
                                               ident[0:NS, 0:NS])
                last.then_inc(mod_ps, 1)

            def turn_decode():
                pe.wait_ge(dv("xn"), 1)
                pe.wait_ge(d_ld, 48)
                for k in range(KT):
                    nc.tensor.transpose(aux[0][:, TD * k:TD * k + TD], xin[0:TD, 0, P * k:P * k + P], ident[0:TD, 0:TD])
                for c in range(CT):
                    nc.tensor.transpose(aux[1][:, NB * c:NB * c + NB], xin[0:NB, 1, P * c:P * c + P], ident[0:NB, 0:NB])
                nj = NB * (CW - 1)
                for c in range(CT):
                    last = nc.tensor.transpose(aux[1][:, TD + nj * c:TD + nj * c + nj],
                                               xin[0:nj, 1, DA + P * c:DA + P * c + P], ident[0:nj, 0:nj])
                last.then_inc(dv("turned"), 1)

            def body(n, first, last_body):
                def weights(i):
                    if first:
                        pe.wait_ge(w_lo, i)

                weights(1)
                if not first:
                    pe.wait_ge(i_sig.sem, i_sig.at(n - 1, 4))
                project(ring[0], FR, 0, n)
                project(ring[0], FR, 1).then_inc(fr_ps.sem, 1)
                if not first:
                    turn_y(n - 1, 0)
                    turn_y(n - 1, 1)
                weights(2)
                project(ring[1], Q_, 0)
                project(ring[1], Q_, 1).then_inc(q_ps.sem, 1)
                pe.wait_ge(k_sig.sem, k_sig.at(n, 1))
                weights(4)
                project_rows(ring[0], IV, 0, 0)
                project_rows(ring[0], IV, 0, 1).then_inc(iv_ps.sem, 1)
                level(n, 0, 0)
                pe.wait_ge(q_sb.sem, q_sb.at(n, 1))
                project_rows(ring[1], IV, 1, 0)
                level(n, 0, 1)
                project_rows(ring[1], IV, 1, 1).then_inc(iv_ps.sem, 1)
                level(n, 0, 2)
                pe.wait_ge(v_sb.sem, v_sb.at(n, 1))
                weights(6)
                project_rows(ring[0], GB, 0, 0)
                level(n, 0, 3)
                project_rows(ring[0], GB, 0, 1).then_inc(gb_ps.sem, 1)
                level(n, 0, 4)
                pe.wait_ge(v_sb.sem, v_sb.at(n, 2))
                project_rows(ring[1], GB, 1, 0)
                level(n, 0, 5)
                project_rows(ring[1], GB, 1, 1).then_inc(gb_ps.sem, 1)
                level(n, 0, 6)
                if not first:
                    pe.wait_ge(wo_lo, NWO)
                    pe.wait_ge(yl_ok.sem, yl_ok.at(n - 1, 1))
                    pe.wait_ge(ytl.sem, ytl.at(n - 1, 2))
                    pe.wait_ge(gb_sil.sem, gb_sil.at(n, 1))
                    out_rows(ring[0], 0, 0, range(KT // 2))
                else:
                    pe.wait_ge(gb_sil.sem, gb_sil.at(0, 1))
                    ada(NEARLY, ring[0])
                level(n, 0, 7)
                if not first:
                    out_rows(ring[0], 0, 0, range(KT // 2, KT)).then_inc(e_ps.sem, 1)
                if not first:
                    pe.wait_ge(ytl.sem, ytl.at(n - 1, 1))
                else:
                    ada(NEARLY + 1, ring[0])
                turn_k(n, 0)
                if first:
                    pe.wait_ge(gb_sil.sem, gb_sil.at(0, 2))
                    ada(NEARLY + 2, ring[1])
                else:
                    pe.wait_ge(gb_sil.sem, gb_sil.at(n, 2))
                    out_rows(ring[1], 0, 1, range(KT // 2))
                unit(n, 0, 0)
                if not first:
                    out_rows(ring[1], 0, 1, range(KT // 2, KT)).then_inc(e_ps.sem, 1)
                else:
                    ada(NEARLY + 3, ring[1])
                unit(n, 0, 1)
                if first:
                    pe.wait_ge(mod_sb, 5)
                weights(7)
                pe.wait_ge(gb_sil.sem, gb_sil.at(n, 1))
                if not first:
                    pe.wait_ge(esq[0].sem, esq[0].at(n - 1, 1))
                project(ring[0], FR + 2 * P, 0)
                project(ring[0], FR + 2 * P, 1).then_inc(fr_ps.sem, 1)
                pe.wait_ge(gb_sil.sem, gb_sil.at(n, 2))
                if not first:
                    pe.wait_ge(esq[1].sem, esq[1].at(n - 1, 1))
                if first:
                    pe.wait_ge(kt_sb.sem, kt_sb.at(0, 1))
                    for b in (4, 5):
                        turn_mod(b, aux[0], 4 * NS * (b - 4))
                weights(8)
                project(ring[1], Q_ + 2 * P, 0)
                project(ring[1], Q_ + 2 * P, 1).then_inc(q_ps.sem, 1)
                if first:
                    pe.wait_ge(gate_ok, 1)
                    for k in range(KT):
                        last = mm(lev[k // 4][:, P * (k % 4):P * (k % 4) + P], gpt[:, k, 0:1].to_broadcast([P, P]),
                                  ident[:, :], start=True, stop=True)
                    last.then_inc(gp_ps, 1)
                pe.wait_ge(k_sig.sem, k_sig.at(n, 2))
                weights(9)
                project(ring[0], XA, 0)
                project(ring[0], XA, 1).then_inc(xa_ps.sem, 1)
                if first:
                    pe.wait_ge(gp_sb, 1)
                level(n, 1, 0)
                pe.wait_ge(q_sb.sem, q_sb.at(n, 2))
                weights(10)
                project(ring[1], GA, 0)
                level(n, 1, 1)
                project(ring[1], GA, 1).then_inc(ga_ps.sem, 1)
                level(n, 1, 2)
                pe.wait_ge(xa_sb.sem, xa_sb.at(n, 1))
                weights(11)
                project(ring[0], XA + 2 * P, 0)
                level(n, 1, 3)
                gates(n, 0)
                project(ring[0], XA + 2 * P, 1).then_inc(xa_ps.sem, 1)
                level(n, 1, 4)
                pe.wait_ge(ga_sil.sem, ga_sil.at(n, 1))
                weights(12)
                project(ring[1], GA + 2 * P, 0)
                level(n, 1, 5)
                project(ring[1], GA + 2 * P, 1).then_inc(ga_ps.sem, 1)
                level(n, 1, 6)
                pe.wait_ge(r_sig.sem, r_sig.at(n, 2))
                if not last_body:
                    turn_x(n + 1, 0)
                    pe.wait_ge(i_sig.sem, i_sig.at(n, 2))
                    turn_x(n + 1, 1)
                    pe.wait_ge(yb_ok.sem, yb_ok.at(n, 4))
                    pe.wait_ge(s_upd.sem, s_upd.at(n, 4))
                    turn_x(n + 1, 2)
                    turn_x(n + 1, 3)
                else:
                    pe.wait_ge(i_sig.sem, i_sig.at(n, 2))
                    turn_decode()
                if not first:
                    pe.wait_ge(xa_sb.sem, xa_sb.at(n, 2))
                    out_rows(ring[0], 1, 0, range(KT // 2))
                level(n, 1, 7)
                if not first:
                    out_rows(ring[0], 1, 0, range(KT // 2, KT)).then_inc(e_ps.sem, 1)
                if not first:
                    pe.wait_ge(ga_sil.sem, ga_sil.at(n, 2))
                    out_rows(ring[1], 1, 1, range(KT // 2))
                if last_body:
                    pe.wait_ge(dv("hn"), 1)
                    pe.wait_ge(dv("carried"), 2)
                else:
                    pe.wait_ge(hn_lo.sem, hn_lo.at(n + 1, 1))
                turn_k(n, 1)
                if not first:
                    out_rows(ring[1], 1, 1, range(4, 6))
                gates(n, 1)
                if not last_body:
                    pe.wait_ge(hn_lo.sem, hn_lo.at(n + 1, 4))
                unit(n, 1, 0)
                if not first:
                    out_rows(ring[1], 1, 1, range(6, KT)).then_inc(e_ps.sem, 1)
                unit(n, 1, 1)

            pe.wait_ge(ident_ok, 1)
            pe.wait_ge(c_ld, 32)
            for k in range(KT):
                last = nc.tensor.transpose(aux[1][:, NS * k:NS * k + NS], gp[0:NS, P * k:P * k + P], ident[0:NS, 0:NS])
            last.then_inc(pre_ps, 1)
            siluc = xc[:, 0, 0:KT * NS].rearrange("p (k s) -> p k s", k=KT)
            pe.wait_ge(pre_sb, 1)
            for i in range(NEARLY):
                if i == 2:
                    pe.wait_ge(par_ld, 160)
                    nc.tensor.transpose(aux[0][:, 0:NROW], am[0:NROW, 0, :], ident[0:NROW, 0:NROW]).then_inc(pre_ps, 1)
                ada(i, (okv + lev)[i // 2])
                if i % 2 and i > 1:
                    turn_mod(i // 2 - 1, ring[0], 4 * NS * (i // 2 - 1))
            turn_mod(3, ring[0], 12 * NS)
            for j in range(4):
                turn_x(0, j)
            pe.wait_ge(wg_ld, 64)
            pe.wait_ge(zeroed, 3)
            pe.wait_ge(carry_zero, 2)

            body(0, True, False)
            with pe.Fori(1, BODIES - 1) as n:
                body(n, False, False)
            body(BODIES - 1, False, True)
            n = BODIES
            nj = NB * (CW - 1)

            def d_out_rows(j):
                pe.wait_ge(esq[j % 2].sem, esq[j % 2].at(n - 1, j // 2))
                if j == 1:
                    pe.wait_ge(dv("v_d"), 1)
                out_rows(ring[j % 2], j // 2, j % 2, range(KT // 2))
                out_rows(ring[j % 2], j // 2, j % 2, range(KT // 2, KT)).then_inc(e_ps.sem, 1)

            def d_level(l):
                pe.wait_ge(dv("level_in"), l + 1)
                if l:
                    pe.wait_ge(dv("masked"), l)
                for h in range(HB):
                    q, w = qq[:, TD * h:TD * h + TD], TD
                    if l > 0:
                        q, w = blocks(q, 1 << (l - 1))[:, :, 1, :], TD // 2
                    last = mm(lev[0][0:TD, w * h:w * h + w], kk[:, TD * h:TD * h + TD], q, start=True, stop=True)
                last.then_inc(dv("level_ps"), 1)

            def d_states(b):
                pe.wait_ge(dv("v_seq"), b + 1)
                if b >= 2:
                    pe.wait_ge(dv("s_new"), HB * (b - 1))
                for h in range(HB):
                    last = mm((lev[0], okv[0])[b % 2][:, P * h:P * h + P], ktr[0:TD, h, :], vseq(b)[:, P * h:P * h + P],
                              start=True, stop=True)
                last.then_inc(dv("kv_ps"), 1)

            pe.wait_ge(dv("hn"), 1)
            pe.wait_ge(i_sig.sem, i_sig.at(n - 1, 4))
            for i, col in enumerate([b + P * c for b in (XA, GA, Q_, FR) for c in range(CT)]):
                last = split3(ring[0][:, TD * i:TD * i + TD], lambda k: wih[:, k, col:col + P], lambda k: wil[:, k, col:col + P],
                              lambda k: hnh[:, k, 0:TD], lambda k: hnl[:, k, 0:TD], range(KT), True, True)
            last.then_inc(dv("proj_ps"), 1)
            turn_y(n - 1, 0)
            turn_y(n - 1, 1)
            for bank, col, s in ((ring[1], IV, "iv_d"), (lev[1], GB, "gb_d")):
                split3(bank[0:TD, :], lambda k: hnh[:, k, 0:TD], lambda k: hnl[:, k, 0:TD],
                       lambda k: wih[:, k, col:col + DA], lambda k: wil[:, k, col:col + DA], range(KT), True, True)\
                    .then_inc(dv(s), 1)
            gpr = gprow.rearrange("p (k t) -> p k t", k=KT)
            pe.wait_ge(dv("gprow"), 1)
            for k in range(KT):
                last = mm(okv[k // 4][0:TD, P * (k % 4):P * (k % 4) + P], gpr[:, k, :], ident[:, :], start=True, stop=True)
            last.then_inc(dv("gp_ps"), 1)
            d_level(0)
            pe.wait_ge(yl_ok.sem, yl_ok.at(n - 1, 1))
            pe.wait_ge(ytl.sem, ytl.at(n - 1, 2))
            pe.wait_ge(dv("qfk_d"), 3)
            pe.wait_ge(dv("ga_d"), 1)
            d_out_rows(0)
            d_level(1)
            d_out_rows(1)
            d_level(2)
            pe.wait_ge(dv("gb_sb"), 1)
            pe.wait_ge(dv("conv_d"), 16)
            for w in range(2):
                for c in range(CT):
                    o = TD * CT * w + TD * c
                    last = mm(lev[1][:, o:o + TD], wg[:, w, c, :], xcd[:, TD * c:TD * c + TD], start=True, stop=True)
            last.then_inc(dv("gates_ps"), 1)
            d_out_rows(2)
            pe.wait_ge(dv("level_in"), DLEVELS + 2)
            for h in range(HB):
                last = nc.tensor.transpose(aux[1][0:TD, P * h:P * h + P], kk[:, TD * h:TD * h + TD], ident[:, :])
            last.then_inc(dv("kt_d"), 1)
            d_out_rows(3)
            pe.wait_ge(dv("masked"), DLEVELS + 1)
            pe.wait_ge(dv("gp_sb"), 1)
            pe.wait_ge(dv("qz_ok"), 1)
            pe.wait_ge(d_s0, 16 * NB)
            for h in range(HB):
                o = okv[1][0:TD, P * h:P * h + P]
                mm(o, am[0:TD, h, 0:TD], vv[0:TD, 0, P * h:P * h + P], start=True, stop=False)
                for b in range(NB):
                    last = mm(o, qzh[:, h, TD * b:TD * b + TD], s0[:, b, P * h:P * h + P], start=False, stop=b == NB - 1)
            last.then_inc(dv("o_ps"), 1)
            pe.wait_ge(dv("kt_sbd"), 1)
            d_states(0)
            d_states(1)
            pe.wait_ge(dv("yb_d"), HB)
            for h in range(HB):
                last = nc.tensor.transpose(aux[0][:, TD * h:TD * h + TD], gbs[0:TD, 0, P * h:P * h + P], ident[0:TD, 0:TD])
            last.then_inc(dv("ybt_ps"), 1)
            pe.wait_ge(dv("y_dec"), 4)
            for c in range(2):
                pe.wait_ge(esq[c].sem, esq[c].at(n, 0))
                split3(ring[c][0:TD, :], lambda k: yhd[:, k, :], lambda k: yld[:, k, :],
                       lambda k: woh[:, k, 512 * c:512 * c + 512], lambda k: wol[:, k, 512 * c:512 * c + 512],
                       range(KT), True, True).then_inc(dv("m_ps"), 1)
                d_states(2 + 2 * c)
                d_states(3 + 2 * c)
            for c in range(CT):
                nc.tensor.transpose(aux[0][0:nj, P * c:P * c + P], halod[:, nj * c:nj * c + nj], ident[:, :])
            for c in range(CT):
                nc.tensor.transpose(aux[1][0:NB, P * c:P * c + P], hnew[:, NB * c:NB * c + NB], ident[:, :])
            for c in range(CT):
                nc.tensor.transpose(lev[1][0:CW - 1, P * c:P * c + P], halo[:, c, :], ident[:, :])
            pe.wait_ge(hst_ok.sem, hst_ok.at(BODIES, 0))
            nc.tensor.transpose(okv[1][0:CT, 0:P], hst[:, :], ident[:, :]).then_inc(dv("rows_ps"), 1)
            d_states(6)
            d_states(7)

        @block.scalar
        def _(act):
            A = nc.scalar.activation

            def gate_out(n, p):
                act.wait_ge(fr_ps.sem, fr_ps.at(n, p + 1))
                act.wait_ge(u_ps.sem, u_ps.at(n, 2 * p))
                A(ff[:, :], ring[0][:, :], ACT.Sigmoid).then_inc(f_sig.sem, 1)
                A(kk[:, :], ring[0][:, :], ACT.Sigmoid, scale=-1.0).then_inc(k_sig.sem, 1)

            def q_out(n, p):
                act.wait_ge(q_ps.sem, q_ps.at(n, p + 1))
                A(qq[:, :], ring[1][:, :], ACT.Copy).then_inc(q_sb.sem, 1)

            def squares_m(n, j):
                act.wait_ge(e_ps.sem, e_ps.at(n, j + 1))
                act.wait_ge(mgd.sem, mgd.at(n, j + 1))
                A(ring[j % 2][:, :], ring[j % 2][:, :], ACT.Square, accum_out=essq[:, j:j + 1]).then_inc(esq[j % 2].sem, 1)

            def k_out(n, p):
                act.wait_ge(kt_ps.sem, kt_ps.at(n, p + 1))
                A(ktr[:, :, :], aux[p][:, :].rearrange("p (h k) -> p h k", h=4), ACT.Copy).then_inc(kt_sb.sem, 1)

            def squares_o(n, ui):
                act.wait_ge(s_upd.sem, s_upd.at(n, 2 * ui + 2))
                c = ui % 2
                for h in range(2):
                    act.wait_ge(usq.sem, usq.at(n, 2 * ui + h))
                    A(junk[:, 512:640], okv[c][:, P * h:P * h + P], ACT.Square, accum_out=ussq[:, 2 * c + h:2 * c + h + 1])\
                        .then_inc(usq.sem, 1)

            def xa_out(n, p):
                act.wait_ge(xa_ps.sem, xa_ps.at(n, p + 1))
                act.wait_ge(cvc.sem, cvc.at(n, 8 * p))
                act.wait_ge(hl_sv.sem, hl_sv.at(n, p))
                A(xa[:, :, CW - 1:], ring[0][:, :].rearrange("p (c t) -> p c t", c=2), ACT.Copy).then_inc(xa_sb.sem, 1)

            def ga_out(n, p):
                act.wait_ge(ga_ps.sem, ga_ps.at(n, p + 1))
                act.wait_ge(yl_ok.sem, yl_ok.at(n, 0))
                act.wait_ge(yh_ok.sem, yh_ok.at(n, 0))
                A(sil[:, 2 * p:2 * p + 2, :], ring[1][:, :].rearrange("p (c t) -> p c t", c=2), ACT.Silu)\
                    .then_inc(ga_sil.sem, 1)

            def squares_x(m):
                for t in range(NT):
                    act.wait_ge(xld[t].sem, xld[t].at(m + 1, 0))
                    if t == 0:
                        act.wait_ge(xn_ok.sem, xn_ok.at(m, 0))
                    for c in range(2):
                        act.wait_ge(xsq.sem, xsq.at(m, 2 * t + c))
                        A(junk[:, 0:512], xin[:, t, 512 * c:512 * c + 512], ACT.Square,
                          accum_out=xssq[:, 2 * t + c:2 * t + c + 1]).then_inc(xsq.sem, 1)

            def gates_out(n, p):
                act.wait_ge(gr_ps.sem, gr_ps.at(n, p + 1))
                act.wait_ge(iu.sem, iu.at(n, p))
                for c in range(2):
                    A(rr[:, c, :], aux[(1 + p) % 2][:, T * c:T * c + T], ACT.Sigmoid,
                      bias=pcol("ba", 2 * p + c)).then_inc(r_sig.sem, 1)
                act.wait_ge(gi_ps.sem, gi_ps.at(n, p + 1))
                act.wait_ge(scan.sem, scan.at(n, 2 * p))
                for c in range(2):
                    A(ii[:, c, :], aux[p][:, T * c:T * c + T], ACT.Sigmoid, bias=pcol("bx", 2 * p + c)).then_inc(i_sig.sem, 1)

            def decay(n, p):
                act.wait_ge(r_sig.sem, r_sig.at(n, 2 * p + 2))
                for c in range(2):
                    A(aa[:, c, :], rr[:, c, :], ACT.Exp, scale=cneg[:, 2 * p + c:2 * p + c + 1]).then_inc(a_exp.sem, 1)
                for c in range(2):
                    A(rr[:, c, :], rr[:, c, :], ACT.Tanh, scale=cpos[:, 2 * p + c:2 * p + c + 1]).then_inc(th_ok.sem, 1)

            def root(n, p):
                act.wait_ge(gd.sem, gd.at(n, p + 1))
                A(rr[:, :, :], rr[:, :, :], ACT.Sqrt).then_inc(u_sqrt.sem, 1)

            def hn_out(m, j):
                bank = x_banks[j]
                act.wait_ge(tr_ps.sem, tr_ps.at(m, j + 1))
                for i in range(2):
                    k = 2 * j + i
                    A(bank[:, T * i:T * i + T], bank[:, T * i:T * i + T], ACT.Identity, scale=sc1[:, k, 0:1],
                      bias=shf[:, k, 0:1]).then_inc(aff.sem, 1)
                act.wait_ge(aff.sem, aff.at(m, 2 * j + 2))
                A(hnh[:, 2 * j:2 * j + 2, :], bank[:, :].rearrange("p (k t) -> p k t", k=2), ACT.Copy).then_inc(hn_hi.sem, 1)

            def y_turned(n, j):
                act.wait_ge(yt_ps.sem, yt_ps.at(n, j + 1))
                A(yh[:, CT + 2 * j:CT + 2 * j + 2, :], aux[j][:, :].rearrange("p (k t) -> p k t", k=2), ACT.Copy)\
                    .then_inc(yth.sem, 1)

            def mod_out(b, bank):
                act.wait_ge(ada_ps, 2 * b + 2)
                A(mod_rows[b][0:NS, :], bank[0:NS, :], ACT.Copy).then_inc(mod_sb, 1)

            def head(kind, c):
                s = stage[place[kind, c]]
                act.wait_ge(st_ld[place[kind, c]], landed[kind, c])
                if kind == "wo":
                    act.wait_ge(w_fold, c + 1)
                    act.wait_ge(w_lo, NWI)
                dst, col = (wih, WI_COLS[c]) if kind == "wi" else (woh, 256 * c)
                A(dst[:, :, col:col + 256], s, ACT.Copy).then_inc(w_hi, 1)

            def body(n, first, last_body):
                def weights(kind, *which):
                    if first:
                        for c in which:
                            head(kind, c)

                weights("wi", 3)
                gate_out(n, 0)
                if not first:
                    act.wait_ge(wo_lo, NWO)
                    y_turned(n - 1, 0)
                    y_turned(n - 1, 1)
                q_out(n, 0)
                weights("wi", 4)
                for t in range(NT):
                    act.wait_ge(iv_ps.sem, iv_ps.at(n, t + 1))
                    A(vv[:, t, :], ring[t][:, :], ACT.Copy).then_inc(v_sb.sem, 1)
                    if t == 0:
                        weights("wi", 5)
                for t in range(NT):
                    act.wait_ge(gb_ps.sem, gb_ps.at(n, t + 1))
                    A(gbs[:, t, :], ring[t][:, :], ACT.Silu).then_inc(gb_sil.sem, 1)
                if not first:
                    squares_m(n - 1, 0)
                else:
                    head("wi", 6)
                    mod_out(4, ring[0])
                k_out(n, 0)
                squares_o(n, 0)
                if not first:
                    squares_m(n - 1, 1)
                else:
                    mod_out(5, ring[1])
                squares_o(n, 1)
                weights("wi", 7)
                if not last_body:
                    squares_x(n + 1)
                else:
                    act.wait_ge(d_ld, 16 * 3)
                    for c in range(2):
                        if c:
                            act.wait_ge(dv("xsq_d"), 1)
                        A(junk[0:TD, 0:512], xin[0:TD, 0, 512 * c:512 * c + 512], ACT.Square, accum_out=xssq[0:TD, c:c + 1])\
                            .then_inc(dv("xsq_d"), 1)
                weights("wi", 8)
                gate_out(n, 1)
                q_out(n, 1)
                weights("wi", 9, 10)
                if first:
                    act.wait_ge(gp_ps, 1)
                    for i in range(2):
                        last = A(gp[:, 512 * i:512 * i + 512], lev[i][:, :], ACT.Copy)
                    last.then_inc(gp_sb, 1)
                xa_out(n, 0)
                weights("wi", 11)
                ga_out(n, 0)
                gates_out(n, 0)
                weights("wo", 0)
                xa_out(n, 1)
                decay(n, 0)
                root(n, 0)
                ga_out(n, 1)
                if not last_body:
                    for j in range(4):
                        hn_out(n + 1, j)
                weights("wo", 1)
                k_out(n, 1)
                if not first:
                    squares_m(n - 1, 2)
                gates_out(n, 1)
                weights("wo", 2)
                squares_o(n, 2)
                if not first:
                    squares_m(n - 1, 3)
                squares_o(n, 3)
                decay(n, 1)
                root(n, 1)
                weights("wo", 3)

            act.wait_ge(pre_ps, 1)
            A(xc[:, 0, 0:KT * NS], aux[1][:, 0:KT * NS], ACT.Silu).then_inc(pre_sb, 1)
            act.wait_ge(pre_ps, 2)
            A(par[:, :], aux[0][:, 0:NROW], ACT.Copy).then_inc(pre_sb, 1)
            act.wait_ge(chain_dve, 3)
            A(tmp[:, 1, :], tmp[:, 0, :], ACT.Exp, scale=-1.0).then_inc(pre_sb, 1)
            A(tmp[:, 3, :], tmp[:, 2, :], ACT.Exp).then_inc(pre_sb, 1)
            for b in range(2):
                mod_out(b, (okv + lev)[b])
            squares_x(0)
            mod_out(2, lev[0])
            head("wi", 0)
            mod_out(3, lev[1])
            head("wi", 1)
            act.wait_ge(mod_ok, 1)
            for j in range(4):
                hn_out(0, j)
            head("wi", 2)

            body(0, True, False)
            with act.Fori(1, BODIES - 1) as n:
                body(n, False, False)
            body(BODIES - 1, False, True)
            n = BODIES
            act.wait_ge(dv("proj_ps"), 1)
            A(xad[:, :, :, CW - 1:], ring[0][:, 0:W4].rearrange("p (c b l) -> p c b l", c=CT, b=NB), ACT.Copy)\
                .then_inc(dv("xa_d"), 1)
            A(qq[:, 0:W4], ring[0][:, 2 * W4:3 * W4], ACT.Copy).then_inc(dv("qfk_d"), 1)
            A(ff[:, 0:W4], ring[0][:, 3 * W4:4 * W4], ACT.Sigmoid).then_inc(dv("qfk_d"), 1)
            A(kk[:, 0:W4], ring[0][:, 3 * W4:4 * W4], ACT.Sigmoid, scale=-1.0).then_inc(dv("qfk_d"), 1)
            y_turned(n - 1, 0)
            y_turned(n - 1, 1)
            A(sild, ring[0][:, W4:2 * W4], ACT.Silu).then_inc(dv("ga_d"), 1)
            act.wait_ge(dv("iv_d"), 1)
            A(vv[0:TD, 0, :], ring[1][0:TD, :], ACT.Copy).then_inc(dv("v_d"), 1)
            act.wait_ge(dv("gb_d"), 1)
            A(gbs[0:TD, 0, :], lev[1][0:TD, :], ACT.Silu).then_inc(dv("gb_sb"), 1)
            act.wait_ge(dv("gp_ps"), 1)
            for i in range(2):
                last = A(gpd[:, 512 * i:512 * i + 512], okv[i][0:TD, :], ACT.Copy)
            last.then_inc(dv("gp_sb"), 1)
            squares_m(n - 1, 0)
            squares_m(n - 1, 1)
            act.wait_ge(dv("gates_ps"), 1)
            for w, dst, bias in ((0, rrd, "ba"), (1, iid, "bx")):
                for c in range(CT):
                    o = W4 * w + TD * c
                    A(dst[:, TD * c:TD * c + TD], lev[1][:, o:o + TD], ACT.Sigmoid, bias=pcol(bias, c)).then_inc(dv("ri_d"), 1)
            act.wait_ge(dv("ri_d"), 2 * CT)
            for c in range(CT):
                A(aad[:, TD * c:TD * c + TD], rrd[:, TD * c:TD * c + TD], ACT.Exp, scale=cneg[:, c:c + 1]).then_inc(dv("a_d"), 1)
            for c in range(CT):
                A(rrd[:, TD * c:TD * c + TD], rrd[:, TD * c:TD * c + TD], ACT.Tanh, scale=cpos[:, c:c + 1]).then_inc(dv("a_d"), 1)
            squares_m(n - 1, 2)
            act.wait_ge(dv("kt_d"), 1)
            A(ktr[0:TD, :, :], aux[1][0:TD, :].rearrange("p (h k) -> p h k", h=HB), ACT.Copy).then_inc(dv("kt_sbd"), 1)
            act.wait_ge(dv("guard_d"), 1)
            A(rrd, rrd, ACT.Sqrt).then_inc(dv("root_d"), 1)
            squares_m(n - 1, 3)
            act.wait_ge(dv("o_ps"), 1)
            for h in range(HB):
                if h:
                    act.wait_ge(dv("usq_d"), h)
                A(junk[0:TD, 512:640], okv[1][0:TD, P * h:P * h + P], ACT.Square, accum_out=dsum[:, h:h + 1])\
                    .then_inc(dv("usq_d"), 1)
            for c in range(2):
                act.wait_ge(dv("m_ps"), c + 1)
                act.wait_ge(dv("mg_d"), c + 1)
                A(ring[c][0:TD, :], ring[c][0:TD, :], ACT.Square, accum_out=dsum[:, c:c + 1]).then_inc(dv("msq_d"), 1)
            act.wait_ge(dv("rows_ps"), 1)
            for bank, m, w, out in ((aux[0], NB * (CW - 1), DA, rows_out[0]), (aux[1], NB, DA, rows_out[1]),
                                    (lev[1], CW - 1, DA, rows_out[2]), (okv[1], CT, P, rows_out[3])):
                A(out[0:m, 0:w], bank[0:m, 0:w], ACT.Copy).then_inc(dv("rows_sb"), 1)

        @block.vector
        def _(dve):
            V = nc.vector

            def rsqrt_steps(w, ssq, out, count, base, s):
                y, v, t = out[:, 0, :], out[:, 1, :], out[:, 2, :]
                k = 0

                def done(ins):
                    nonlocal k
                    k += 1
                    ins.then_inc(s, 1)
                    dve.wait_ge(s, base + k)
                done(V.tensor_scalar(v, ssq, 1.0 / count, EPS, ALU.mult, ALU.add))
                done(V.tensor_scalar(t.bitcast(I32), v.bitcast(I32), 1, None, ALU.logical_shift_right))
                done(V.tensor_scalar(y.bitcast(I32), t.bitcast(I32), -1.0, MAGIC, ALU.mult, ALU.add))
                for _ in range(3):
                    done(V.tensor_tensor(t, y, y, ALU.mult))
                    done(V.scalar_tensor_tensor(t, t, -0.5, v, ALU.mult, ALU.mult))
                    done(V.scalar_tensor_tensor(y, t, 1.5, y, ALU.add, ALU.mult))

            def y_rest(n, j):
                dve.wait_ge(yth.sem, yth.at(n, j + 1))
                V.tensor_tensor(yl[:, CT + 2 * j:CT + 2 * j + 2, :], aux[j][:, :].rearrange("p (k t) -> p k t", k=2),
                                yh[:, CT + 2 * j:CT + 2 * j + 2, :], ALU.subtract).then_inc(ytl.sem, 1)

            def forget(n, p):
                dve.wait_ge(f_af.sem, f_af.at(n, 2 * p + 2))
                V.tensor_scalar_max(ff[:, :], ff[:, :], F_MIN).then_inc(f_ok.sem, 1)

            def take(n, p, l):
                i = p * (LEVELS + 1) + l
                dve.wait_ge(lev_ps.sem, lev_ps.at(n, i + 1))
                if l == 0:
                    dve.wait_ge(u_ps.sem, u_ps.at(n, 2 * p))
                    dve.wait_ge(f_ok.sem, f_ok.at(n, p + 1))
                    V.tensor_tensor(qq[:, :], qq[:, :], ff[:, :], ALU.mult).then_inc(q_f.sem, 1)
                    V.copy_predicated(am[:, :, :], eye[:, :].unsqueeze(1).to_broadcast([P, 4, P]),
                                      lev[i % 2][:, :].rearrange("p (h t) -> p h t", h=4)).then_inc(amask.sem, 1)
                    return
                dve.wait_ge(amask.sem, amask.at(n, i))
                m = 1 << (l - 1)
                nb = 2 * T // (2 * m)
                j = LEVELS * p + l
                if l == 1:
                    dve.wait_ge(q_f.sem, q_f.at(n, p + 1))
                else:
                    dve.wait_ge(q_upd.sem, q_upd.at(n, j - 1))
                    dve.wait_ge(k_upd.sem, k_upd.at(n, j - 1))
                    dve.wait_ge(g_upd.sem, g_upd.at(n, j - 1))
                g = products(m)
                qo, ke = blocks(qq[:, :], m)[:, :, 1, :], blocks(kk[:, :], m)[:, :, 0, :]
                V.tensor_tensor(qo, qo, g[:, :, 0:1].to_broadcast([P, nb, m]), ALU.mult).then_inc(q_upd.sem, 1)
                V.tensor_tensor(ke, ke, g[:, :, 1:2].to_broadcast([P, nb, m]), ALU.mult).then_inc(k_upd.sem, 1)
                o = goff(2 * m)
                V.tensor_tensor(gg[:, o:o + nb], g[:, :, 0], g[:, :, 1], ALU.mult).then_inc(g_upd.sem, 1)
                r = m if m == P // 2 else P
                a = am[0:r, :, :].rearrange("p h (b two m) -> p h b two m", two=2, m=m)
                x = lev[i % 2][0:r, 0:256].rearrange("p (h b m) -> p h b m", h=4, m=m)
                msk = lmask[0:r, l - 1, :].rearrange("p (b m) -> p b m", m=m).unsqueeze(1).to_broadcast([r, 4, P // (2 * m), m])
                V.copy_predicated(a[:, :, :, 1, :], msk, x).then_inc(amask.sem, 1)

            def state(n, p, c):
                ui = 2 * p + c
                dve.wait_ge(u_ps.sem, u_ps.at(n, ui + 1))
                dve.wait_ge(g_upd.sem, g_upd.at(n, LEVELS * p + LEVELS))
                dve.wait_ge(s_upd.sem, s_upd.at(n, 2 * ui))
                for h in range(2):
                    hd, o = 2 * p + h, goff(P) + 2 * h + c
                    V.scalar_tensor_tensor(st[:, hd, :], st[:, hd, :], gg[:, o:o + 1],
                                           okv[c][:, 2 * P + P * h:3 * P + P * h],
                                           ALU.mult, ALU.add).then_inc(s_upd.sem, 1)

            def rows(n, p):
                dve.wait_ge(usq.sem, usq.at(n, 4 * p + 4))
                rsqrt_steps(4, ussq, urs, P, newt_u.at(n, NEWTON * p), newt_u.sem)
                dve.wait_ge(gb_sil.sem, gb_sil.at(n, 2))
                for c in range(2):
                    for h in range(2):
                        y = gbs[:, c, P * (2 * p + h):P * (2 * p + h) + P]
                        V.scalar_tensor_tensor(y, okv[c][:, P * h:P * h + P], urs[:, 0, 2 * c + h:2 * c + h + 1], y,
                                               ALU.mult, ALU.mult).then_inc(yb_ok.sem, 1)

            def m_out(n, j):
                dve.wait_ge(e_ps.sem, e_ps.at(n, j + 1))
                if j == 2:
                    dve.wait_ge(eo.sem, eo.at(n, 1))
                c = j % 2
                V.tensor_tensor(mg[:, 512 * c:512 * c + 512], ring[c][:, :], gp[:, 512 * c:512 * c + 512], ALU.mult)\
                    .then_inc(mgd.sem, 1)

            def x_out(n, t):
                for c in range(2):
                    dve.wait_ge(esq[c].sem, esq[c].at(n, t + 1))
                base = newt_e.at(n, (NEWTON + 1) * t)
                V.tensor_tensor(essq[:, 2 * t:2 * t + 1], essq[:, 2 * t:2 * t + 1], essq[:, 2 * t + 1:2 * t + 2], ALU.add)\
                    .then_inc(newt_e.sem, 1)
                dve.wait_ge(newt_e.sem, base + 1)
                rsqrt_steps(1, essq[:, 2 * t:2 * t + 1], ers, D, base + 1, newt_e.sem)
                dve.wait_ge(mgd.sem, mgd.at(n, 2 * t + 2))
                dve.wait_ge(xrl.sem, xrl.at(n, 16 * t + 16))
                V.scalar_tensor_tensor(xr, mg, ers[:, 0, 0:1], xr, ALU.mult, ALU.add).then_inc(eo.sem, 1)

            def conv(n, p):
                dve.wait_ge(xa_sb.sem, xa_sb.at(n, p + 1))
                dve.wait_ge(hl_in.sem, hl_in.at(n, p + 1))
                dve.wait_ge(hst_ok.sem, hst_ok.at(n, p))
                dve.wait_ge(y_ok.sem, y_ok.at(n, p))
                for j in range(CW):
                    if j:
                        dve.wait_ge(cvc.sem, cvc.at(n, 8 * p + 2 * j))
                    for c in range(2):
                        src, w = xa[:, c, j:j + T], pcol("cw", CT * j + 2 * p + c)
                        if j == 0:
                            V.tensor_scalar(xc[:, c, :], src, w, pcol("cb", 2 * p + c), ALU.mult, ALU.add).then_inc(cvc.sem, 1)
                        else:
                            V.scalar_tensor_tensor(xc[:, c, :], src, w, xc[:, c, :], ALU.mult, ALU.add).then_inc(cvc.sem, 1)

            def input_scale(n, p):
                dve.wait_ge(a_sq.sem, a_sq.at(n, p + 1))
                dve.wait_ge(th_ok.sem, th_ok.at(n, 2 * p + 2))
                V.scalar_tensor_tensor(rr[:, :, :], xc[:, :, :], 1.0, rr[:, :, :], ALU.add, ALU.mult).then_inc(rx.sem, 1)
                dve.wait_ge(rx.sem, rx.at(n, p + 1))
                V.tensor_scalar_max(rr[:, :, :], rr[:, :, :], 0.0).then_inc(gd.sem, 1)

            def recur(n, p):
                dve.wait_ge(u_sqrt.sem, u_sqrt.at(n, p + 1))
                dve.wait_ge(ix_ok.sem, ix_ok.at(n, p + 1))
                V.tensor_tensor(ii[:, :, :], rr[:, :, :], ii[:, :, :], ALU.mult).then_inc(iu.sem, 1)
                dve.wait_ge(iu.sem, iu.at(n, p + 1))
                for c in range(2):
                    V.tensor_tensor_scan(xc[:, c, :], aa[:, c, :], ii[:, c, :], hst[:, 2 * p + c:2 * p + c + 1],
                                         ALU.mult, ALU.add).then_inc(scan.sem, 1)
                dve.wait_ge(scan.sem, scan.at(n, 2 * p + 2))
                dve.wait_ge(ga_sil.sem, ga_sil.at(n, p + 1))
                s = sil[:, 2 * p:2 * p + 2, :]
                V.tensor_tensor(s, xc[:, :, :], s, ALU.mult).then_inc(y_ok.sem, 1)

            def y_split(n):
                dve.wait_ge(yh_ok.sem, yh_ok.at(n, 1))
                V.tensor_tensor(yl[:, 0:CT, :], sil[:, :, :], yh[:, 0:CT, :], ALU.subtract).then_inc(yl_ok.sem, 1)

            def x_norm(m):
                dve.wait_ge(xsq.sem, xsq.at(m, 4))
                base = newt_x.at(m, 0)
                pairs = xssq[:, :].rearrange("p (t c) -> p t c", c=2)
                V.tensor_tensor(xssq[:, 0:2], pairs[:, :, 0], pairs[:, :, 1], ALU.add).then_inc(newt_x.sem, 1)
                dve.wait_ge(newt_x.sem, base + 1)
                rsqrt_steps(2, xssq[:, 0:2], xrs, D, base + 1, newt_x.sem)
                for t in range(NT):
                    V.tensor_scalar(xin[:, t, :], xin[:, t, :], xrs[:, 0, t:t + 1], None, ALU.mult).then_inc(xn_ok.sem, 1)

            def hn_rest(m, j):
                dve.wait_ge(hn_hi.sem, hn_hi.at(m, j + 1))
                V.tensor_tensor(hnl[:, 2 * j:2 * j + 2, :], x_banks[j][:, :].rearrange("p (k t) -> p k t", k=2),
                                hnh[:, 2 * j:2 * j + 2, :], ALU.subtract).then_inc(hn_lo.sem, 1)

            def rest(c):
                cols = slice(WI_COLS[c], WI_COLS[c] + 256)
                dve.wait_ge(w_hi, c + 1)
                V.tensor_tensor(wil[:, :, cols], stage[place["wi", c]], wih[:, :, cols], ALU.subtract).then_inc(w_lo, 1)

            def decode_in():
                dve.wait_ge(dv("turned"), 1)
                nj = NB * (CW - 1)
                link(V.tensor_copy(h0, aux[1][:, 0:TD]))
                V.tensor_copy(xad[:, :, :, 0:CW - 1],
                              aux[1][:, TD:TD + CT * nj].rearrange("p (c b j) -> p c b j", c=CT, b=NB)).then_inc(dv("carried"), 2)
                hx4 = hx.rearrange("p (k b l) -> p k b l", k=KT, b=NB)
                hx3 = hx.rearrange("p (k t) -> p k t", k=KT)
                seqs = lambda t: t[:, :, 1:].unsqueeze(3).to_broadcast([P, KT, NB, NL])
                link(V.tensor_tensor(hx4, aux[0][:, 0:KT * TD].rearrange("p (k b l) -> p k b l", k=KT, b=NB), seqs(sc1), ALU.mult))
                link(V.tensor_tensor(hx4, hx4, seqs(shf), ALU.add))
                link(V.tensor_copy(hnh[:, :, 0:TD], hx3))
                V.tensor_tensor(hnl[:, :, 0:TD], hx3, hnh[:, :, 0:TD], ALU.subtract).then_inc(dv("hn"), 1)
                V.tensor_copy(gprow.rearrange("p (k b l) -> p k b l", k=KT, b=NB), seqs(gpt)).then_inc(dv("gprow"), 1)

            def fold(c):
                dve.wait_ge(st_ld[place["wo", c]], landed["wo", c])
                v = stage[place["wo", c]][:, CT:, :]
                onw = par[:, ROW["onw"]:ROW["onw"] + CT].unsqueeze(2).to_broadcast([P, CT, 256])
                V.tensor_tensor(v, v, onw, ALU.mult).then_inc(w_fold, 1)

            def body(n, first, last_body):
                def weights(*which):
                    if first:
                        for c in which:
                            rest(c)

                if not first:
                    recur(n - 1, 1)
                weights(3)
                forget(n, 0)
                weights(4)
                if not first:
                    y_rest(n - 1, 0)
                    y_rest(n - 1, 1)
                    y_split(n - 1)
                for l in range(LEVELS + 1):
                    take(n, 0, l)
                    if l == 0:
                        weights(5)
                weights(6)
                if not first:
                    m_out(n - 1, 0)
                state(n, 0, 0)
                if not first:
                    m_out(n - 1, 1)
                state(n, 0, 1)
                rows(n, 0)
                weights(7, 8)
                if first:
                    dve.wait_ge(mod_ps, 6)
                    gate = aux[0][:, 0:KT * NS].rearrange("p (k s) -> p k s", s=NS)
                    link(V.tensor_tensor(gpt[:, :, :], gate, adab[:, 2 * KT:3 * KT, :], ALU.add))
                    V.tensor_tensor(gpt[:, :, :], gpt[:, :, :], post, ALU.mult).then_inc(gate_ok, 1)
                else:
                    x_out(n - 1, 0)
                forget(n, 1)
                weights(9, 10)
                take(n, 1, 0)
                conv(n, 0)
                weights(11)
                take(n, 1, 1)
                take(n, 1, 2)
                if first:
                    fold(0)
                    fold(1)
                if not last_body:
                    x_norm(n + 1)
                else:
                    dve.wait_ge(dv("xsq_d"), 2)
                    link(V.tensor_tensor(xssq[0:TD, 0:1], xssq[0:TD, 0:1], xssq[0:TD, 1:2], ALU.add))
                    rsqrt_steps(1, xssq[0:TD, 0:1], xrs[0:TD, :, 0:1], D, 0, dv("newt_xd"))
                    V.tensor_scalar(xin[0:TD, 0, :], xin[0:TD, 0, :], xrs[0:TD, 0, 0:1], None, ALU.mult).then_inc(dv("xn"), 1)
                take(n, 1, 3)
                take(n, 1, 4)
                take(n, 1, 5)
                input_scale(n, 0)
                take(n, 1, 6)
                recur(n, 0)
                if not last_body:
                    hn_rest(n + 1, 0)
                else:
                    decode_in()
                take(n, 1, 7)
                conv(n, 1)
                if not last_body:
                    hn_rest(n + 1, 1)
                    hn_rest(n + 1, 2)
                    hn_rest(n + 1, 3)
                if first:
                    fold(2)
                else:
                    m_out(n - 1, 2)
                state(n, 1, 0)
                if not first:
                    m_out(n - 1, 3)
                state(n, 1, 1)
                rows(n, 1)
                input_scale(n, 1)
                if first:
                    fold(3)
                else:
                    x_out(n - 1, 1)

            chain = [0]

            def link(ins):
                chain[0] += 1
                ins.then_inc(chain_dve, 1)
                dve.wait_ge(chain_dve, chain[0])

            dve.wait_ge(pre_sb, 2)
            lam, lbl = par[:, ROW["lam"]:ROW["lam"] + CT], par[:, ROW["lbl"]:ROW["lbl"] + CT]
            link(V.tensor_scalar(tmp[:, 4, :], lam, -1.0, None, ALU.mult))
            link(V.tensor_tensor(tmp[:, 0, :], lam, tmp[:, 4, :], ALU.max))
            link(V.tensor_tensor(tmp[:, 2, :], lbl, lbl, ALU.subtract))
            V.memset(st[:, :, :], 0.0).then_inc(carry_zero, 1)
            V.memset(halo[:, :, :], 0.0).then_inc(carry_zero, 1)
            dve.wait_ge(pre_sb, 4)
            e, z, z2, s = tmp[:, 1, :], tmp[:, 5, :], tmp[:, 6, :], tmp[:, 7, :]
            link(V.tensor_scalar(s, e, 2.0, None, ALU.add))
            link(V.reciprocal(s, s))
            link(V.tensor_tensor(z, e, s, ALU.mult))
            link(V.tensor_tensor(z2, z, z, ALU.mult))
            link(V.tensor_scalar(s, z2, 1.0 / 17, None, ALU.mult))
            for d in (15, 13, 11, 9, 7, 5, 3):
                link(V.scalar_tensor_tensor(s, s, 1.0 / d, z2, ALU.add, ALU.mult))
            link(V.scalar_tensor_tensor(s, s, 1.0, z, ALU.add, ALU.mult))
            link(V.tensor_scalar(tmp[:, 4, :], tmp[:, 4, :], 0.0, None, ALU.max))
            link(V.scalar_tensor_tensor(s, s, 2.0, tmp[:, 4, :], ALU.mult, ALU.add))
            link(V.tensor_scalar(cpos[:, :], s, C_RGLRU, None, ALU.mult))
            link(V.tensor_scalar(cneg[:, :], s, -C_RGLRU, None, ALU.mult))
            link(V.reciprocal(s, tmp[:, 3, :]))
            link(V.tensor_tensor(s, tmp[:, 3, :], s, ALU.mult))
            link(V.tensor_tensor(lb[:, :], s, s, ALU.subtract))
            V.tensor_scalar(omlb[:, :], lb[:, :], -1.0, 1.0, ALU.mult, ALU.add).then_inc(lb_ok, 1)
            x_norm(0)
            rest(0)
            dve.wait_ge(mod_ps, 4)
            adab = par[:, ROW["adab"]:ROW["adab"] + 3 * KT].unsqueeze(2).to_broadcast([P, 3 * KT, NS])
            pre = par[:, ROW["pre"]:ROW["pre"] + KT].unsqueeze(2).to_broadcast([P, KT, NS])
            post = par[:, ROW["post"]:ROW["post"] + KT].unsqueeze(2).to_broadcast([P, KT, NS])
            mod = ring[0][:, 0:2 * KT * NS].rearrange("p (k s) -> p k s", s=NS)
            link(V.tensor_tensor(shf[:, :, :], mod[:, 0:KT, :], adab[:, 0:KT, :], ALU.add))
            link(V.tensor_tensor(sc1[:, :, :], mod[:, KT:2 * KT, :], adab[:, KT:2 * KT, :], ALU.add))
            V.scalar_tensor_tensor(sc1[:, :, :], sc1[:, :, :], 1.0, pre, ALU.add, ALU.mult).then_inc(mod_ok, 1)
            rest(1)
            for j in range(4):
                hn_rest(0, j)
            rest(2)
            dve.wait_ge(zeroed, 3)

            body(0, True, False)
            with dve.Fori(1, BODIES - 1) as n:
                body(n, False, False)
            body(BODIES - 1, False, True)
            n = BODIES

            def d_keep(l):
                dve.wait_ge(dv("level_ps"), l + 1)
                if l == 0:
                    V.copy_predicated(am[0:TD, :, 0:TD], eye[0:TD, 0:TD].unsqueeze(1).to_broadcast([TD, HB, TD]),
                                      lev[0][0:TD, 0:W4].rearrange("p (h t) -> p h t", h=HB)).then_inc(dv("masked"), 1)
                    V.tensor_tensor(qq[:, 0:W4], qq[:, 0:W4], ff[:, 0:W4], ALU.mult).then_inc(dv("level_in"), 1)
                    dve.wait_ge(dv("level_in"), 2)
                    return
                m = 1 << (l - 1)
                g = (ff[:, 0:W4] if m == 1 else gg[:, 0:W4 // 2]).rearrange("p (b two) -> p b two", two=2)
                nb = W4 // (2 * m)
                a = am[0:TD, :, 0:TD].rearrange("p h (b two m) -> p h b two m", two=2, m=m)
                x = lev[0][0:TD, 0:W4 // 2].rearrange("p (h b m) -> p h b m", h=HB, m=m)
                msk = lmask[0:TD, l - 1, 0:TD // 2].rearrange("p (b m) -> p b m", m=m).unsqueeze(1)\
                    .to_broadcast([TD, HB, TD // (2 * m), m])
                dve.wait_ge(dv("masked"), l)
                V.copy_predicated(a[:, :, :, 1, :], msk, x).then_inc(dv("masked"), 1)
                qo, ke = blocks(qq[:, 0:W4], m)[:, :, 1, :], blocks(kk[:, 0:W4], m)[:, :, 0, :]
                link(V.tensor_tensor(qo, qo, g[:, :, 0:1].to_broadcast([P, nb, m]), ALU.mult))
                link(V.tensor_tensor(gg[:, (m - 1) * W4 // 2:(m - 1) * W4 // 2 + nb], g[:, :, 0], g[:, :, 1], ALU.mult))
                V.tensor_tensor(ke, ke, g[:, :, 1:2].to_broadcast([P, nb, m]), ALU.mult).then_inc(dv("level_in"), 1)
                dve.wait_ge(dv("level_in"), l + 2)

            def d_states(b):
                dve.wait_ge(dv("kv_ps"), b + 1)
                for h in range(HB):
                    s_ = s0[:, b, P * h:P * h + P]
                    V.scalar_tensor_tensor(s_, s_, g4[:, NB * h + b:NB * h + b + 1], (lev[0], okv[0])[b % 2][:, P * h:P * h + P],
                                           ALU.mult, ALU.add).then_inc(dv("s_new"), 1)

            g4 = gg[:, W4 // 2:W4 // 2 + HB * NB]
            recur(n - 1, 1)
            link(V.memset(am[0:TD, :, 0:TD], 0.0))
            y_rest(n - 1, 0)
            y_rest(n - 1, 1)
            y_split(n - 1)
            dve.wait_ge(dv("qfk_d"), 3)
            heads = lambda t: t[:, 0:W4].rearrange("p (h t) -> p h t", h=HB)
            percol = lambda t: t[:, :].unsqueeze(2).to_broadcast([P, HB, TD])
            link(V.tensor_tensor(heads(ff), heads(ff), percol(omlb), ALU.mult))
            link(V.tensor_tensor(heads(ff), heads(ff), percol(lb), ALU.add))
            link(V.tensor_scalar_max(ff[:, 0:W4], ff[:, 0:W4], F_MIN))
            V.tensor_tensor(heads(kk), heads(kk), percol(omlb), ALU.mult).then_inc(dv("level_in"), 1)
            dve.wait_ge(dv("level_in"), 1)
            dve.wait_ge(dv("xa_d"), 1)
            for j in range(CW):
                for c in range(CT):
                    src, w = xad[:, c, :, j:j + NL], pcol("cw", CT * j + c)
                    dst = xcd[:, TD * c:TD * c + TD].rearrange("p (b l) -> p b l", b=NB)
                    if j == 0:
                        V.tensor_scalar(dst, src, w, pcol("cb", c), ALU.mult, ALU.add).then_inc(dv("conv_d"), 1)
                    else:
                        V.scalar_tensor_tensor(dst, src, w, dst, ALU.mult, ALU.add).then_inc(dv("conv_d"), 1)
                dve.wait_ge(dv("conv_d"), CT * (j + 1))
            link(V.tensor_copy(halod.rearrange("p (c b j) -> p c b j", c=CT, b=NB), xad[:, :, :, NL:]))
            d_keep(0)
            m_out(n - 1, 0)
            d_keep(1)
            m_out(n - 1, 1)
            d_keep(2)
            dve.wait_ge(dv("qz_zero"), 1)
            V.tensor_copy(qz[:, :, :, 0:NL], qq[:, 0:W4].rearrange("p (h b l) -> p h b l", h=HB, b=NB)).then_inc(dv("qz_ok"), 1)
            x_out(n - 1, 0)
            dve.wait_ge(dv("a_d"), 2 * CT)
            dve.wait_ge(dv("ri_d"), 2 * CT)
            link(V.tensor_tensor(iid, iid, xcd, ALU.mult))
            link(V.tensor_tensor(xcd, aad, aad, ALU.mult))
            link(V.scalar_tensor_tensor(rrd, xcd, 1.0, rrd, ALU.add, ALU.mult))
            V.tensor_scalar_max(rrd, rrd, 0.0).then_inc(dv("guard_d"), 1)
            m_out(n - 1, 2)
            dve.wait_ge(dv("root_d"), 1)
            link(V.tensor_tensor(iid, iid, rrd, ALU.mult))
            a0, u0 = (t.rearrange("p (s l) -> p s l", l=NL)[:, :, 0] for t in (aad, iid))
            link(V.tensor_tensor(h0, h0, a0, ALU.mult))
            link(V.tensor_tensor(u0, u0, h0, ALU.add))
            link(V.memset(a0, 0.0))
            link(V.tensor_tensor_scan(xcd, aad, iid, 0.0, ALU.mult, ALU.add))
            link(V.tensor_copy(hnew, xcd.rearrange("p (s l) -> p s l", l=NL)[:, :, NL - 1]))
            dve.wait_ge(dv("ga_d"), 1)
            link(V.tensor_tensor(sild, xcd, sild, ALU.mult))
            yd = sild.rearrange("p (c t) -> p c t", c=CT)
            V.tensor_copy(yhd[:, 0:CT, :], yd).then_inc(dv("y_dec"), 1)
            dve.wait_ge(dv("y_dec"), 1)
            V.tensor_tensor(yld[:, 0:CT, :], yd, yhd[:, 0:CT, :], ALU.subtract).then_inc(dv("y_dec"), 1)
            m_out(n - 1, 3)
            dve.wait_ge(dv("usq_d"), HB)
            rsqrt_steps(HB, dsum, drs, P, 0, dv("newt_ud"))
            dve.wait_ge(dv("gb_sb"), 1)
            for h in range(HB):
                y = gbs[0:TD, 0, P * h:P * h + P]
                V.scalar_tensor_tensor(y, okv[1][0:TD, P * h:P * h + P], drs[:, 0, h:h + 1], y, ALU.mult, ALU.mult)\
                    .then_inc(dv("yb_d"), 1)
            dve.wait_ge(dv("ybt_ps"), 1)
            src = aux[0][:, 0:W4].rearrange("p (c t) -> p c t", c=CT)
            V.tensor_copy(yhd[:, CT:, :], src).then_inc(dv("y_dec"), 1)
            dve.wait_ge(dv("y_dec"), 3)
            V.tensor_tensor(yld[:, CT:, :], src, yhd[:, CT:, :], ALU.subtract).then_inc(dv("y_dec"), 1)
            x_out(n - 1, 1)
            for c in range(2):
                d_states(2 * c)
                d_states(2 * c + 1)
                dve.wait_ge(dv("m_ps"), c + 1)
                V.tensor_tensor(mgr[:, 512 * c:512 * c + 512], ring[c][0:TD, :], gpd[:, 512 * c:512 * c + 512], ALU.mult)\
                    .then_inc(dv("mg_d"), 1)
            d_states(4)
            d_states(5)
            dve.wait_ge(dv("msq_d"), 2)
            link(V.tensor_tensor(dsum[:, 0:1], dsum[:, 0:1], dsum[:, 1:2], ALU.add))
            rsqrt_steps(1, dsum[:, 0:1], drs[:, :, 0:1], D, 0, dv("newt_md"))
            dve.wait_ge(dv("mg_d"), 2)
            dve.wait_ge(dv("xres"), 16)
            V.scalar_tensor_tensor(xrd, mgr, drs[:, 0, 0:1], xrd, ALU.mult, ALU.add).then_inc(dv("y_rows"), 1)
            d_states(6)
            d_states(7)

        @block.gpsimd
        def _(pool):
            G = nc.gpsimd

            def copy(out, src):
                ones = one[:, 0:1]
                for _ in range(len(src.shape) - 2):
                    ones = ones.unsqueeze(1)
                return G.tensor_tensor(out, src, ones.to_broadcast(list(src.shape)), ALU.mult)

            def bounds(n, p):
                pool.wait_ge(k_sig.sem, k_sig.at(n, p + 1))
                for h in range(2):
                    hd, cols = 2 * p + h, slice(T * h, T * h + T)
                    G.tensor_tensor(kk[:, cols], kk[:, cols], omlb[:, hd:hd + 1].to_broadcast([P, T]), ALU.mult)\
                        .then_inc(k_ok.sem, 1)
                for h in range(2):
                    hd, cols = 2 * p + h, slice(T * h, T * h + T)
                    G.tensor_scalar(ff[:, cols], ff[:, cols], omlb[:, hd:hd + 1], lb[:, hd:hd + 1], ALU.mult, ALU.add)\
                        .then_inc(f_af.sem, 1)

            def halo_in(n, p):
                pool.wait_ge(cvc.sem, cvc.at(n, 8 * p))
                pool.wait_ge(hl_sv.sem, hl_sv.at(n, p))
                copy(xa[:, :, 0:CW - 1], halo[:, 2 * p:2 * p + 2, :]).then_inc(hl_in.sem, 1)

            def halo_save(n, p):
                pool.wait_ge(xa_sb.sem, xa_sb.at(n, p + 1))
                pool.wait_ge(hl_in.sem, hl_in.at(n, p + 1))
                copy(halo[:, 2 * p:2 * p + 2, :], xa[:, :, T:T + CW - 1]).then_inc(hl_sv.sem, 1)

            def gated(n, p):
                pool.wait_ge(i_sig.sem, i_sig.at(n, 2 * p + 2))
                G.tensor_tensor(ii[:, :, :], ii[:, :, :], xc[:, :, :], ALU.mult).then_inc(ix_ok.sem, 1)
                pool.wait_ge(a_exp.sem, a_exp.at(n, 2 * p + 2))
                pool.wait_ge(ix_ok.sem, ix_ok.at(n, p + 1))
                G.tensor_tensor(xc[:, :, :], aa[:, :, :], aa[:, :, :], ALU.mult).then_inc(a_sq.sem, 1)

            def h_save(n, p):
                pool.wait_ge(scan.sem, scan.at(n, 2 * p + 2))
                copy(hst[:, 2 * p:2 * p + 2], xc[:, :, T - 1]).then_inc(hst_ok.sem, 1)

            def y_head(n):
                pool.wait_ge(y_ok.sem, y_ok.at(n, 2))
                pool.wait_ge(u_ps.sem, u_ps.at(n, 4))
                pool.wait_ge(wo_lo, NWO)
                copy(yh[:, 0:CT, :], sil[:, :, :]).then_inc(yh_ok.sem, 1)

            def rest(c):
                cols = slice(256 * c, 256 * c + 256)
                pool.wait_ge(w_lo, NWI)
                pool.wait_ge(w_hi, NWI + c + 1)
                G.tensor_tensor(wol[:, :, cols], stage[place["wo", c]], woh[:, :, cols], ALU.subtract).then_inc(wo_lo, 1)

            def body(n, first):
                bounds(n, 0)
                if not first:
                    h_save(n - 1, 1)
                    y_head(n - 1)
                halo_in(n, 0)
                bounds(n, 1)
                halo_save(n, 0)
                gated(n, 0)
                halo_in(n, 1)
                if first:
                    rest(0)
                h_save(n, 0)
                halo_save(n, 1)
                if first:
                    rest(1)
                gated(n, 1)
                if first:
                    rest(2)
                    rest(3)

            gc = [0]

            def link(ins):
                gc[0] += 1
                ins.then_inc(chain_pool, 1)
                pool.wait_ge(chain_pool, gc[0])

            link(G.memset(one[:, :], 1.0))
            link(G.memset(ident[:, :], 0.0))
            G.affine_select(out=ident[:, :], in_=ident[:, :], pattern=[[-1, P]], compare_op=ALU.not_equal, fill=1.0,
                            base=0, channel_multiplier=1).then_inc(ident_ok, 1)
            G.memset(wg[:, :, :, :], 0.0).then_inc(zeroed, 1)
            pool.wait_ge(ident_ok, 1)
            link(G.tensor_copy(eye[:, :], ident[:, :]))
            mf = ktr[:, 0, 0:P // 2]
            for l in range(LEVELS):
                m = 1 << l
                v = mf.rearrange("p (b m) -> p b m", m=m)
                pat = [[-2 * m, P // (2 * m)], [0, m]]
                link(G.memset(mf, 1.0))
                link(G.affine_select(out=v, in_=v, pattern=pat, compare_op=ALU.is_ge, fill=0.0, base=0, channel_multiplier=1))
                link(G.affine_select(out=v, in_=v, pattern=[[2 * m, P // (2 * m)], [0, m]], compare_op=ALU.is_ge, fill=0.0,
                                     base=m - 1, channel_multiplier=-1))
                link(G.tensor_copy(lmask[:, l, :], mf))
            sm = ktr[0:TD, 1, 0:NB]
            link(G.memset(sm, 1.0))
            link(G.affine_select(out=sm, in_=sm, pattern=[[-NL, NB]], compare_op=ALU.is_ge, fill=0.0, base=0, channel_multiplier=1))
            link(G.affine_select(out=sm, in_=sm, pattern=[[NL, NB]], compare_op=ALU.is_ge, fill=0.0, base=NL - 1,
                                 channel_multiplier=-1))
            link(G.tensor_copy(smask[:, :], sm))
            G.memset(hst[:, :], 0.0).then_inc(zeroed, 1)
            pool.wait_ge(pre_ps, 2)
            G.memset(am[:, :, :], 0.0).then_inc(zeroed, 1)
            pool.wait_ge(carry_zero, 2)
            pool.wait_ge(lb_ok, 1)

            body(0, True)
            with pool.Fori(1, BODIES - 1) as n:
                body(n, False)
            body(BODIES - 1, False)
            h_save(BODIES - 1, 1)
            y_head(BODIES - 1)
            pool.wait_ge(dv("gb_d"), 1)
            G.memset(qzh, 0.0).then_inc(dv("qz_zero"), 1)
            pool.wait_ge(dv("v_d"), 1)
            pool.wait_ge(dv("gb_sb"), 1)
            for b in range(NB):
                if b >= 2:
                    pool.wait_ge(dv("kv_ps"), b - 1)
                G.tensor_scalar(vseq(b), vv[0:TD, 0, :], smask[:, b:b + 1], None, ALU.mult).then_inc(dv("v_seq"), 1)


_INS = ['x_prompt', 'x_sample', 'state_rglru_h', 'state_rglru_conv', 'state_hgrn_S', 'c_prompt', 'c_sample', 'ada_w',
        'ada_b', 'pre_norm_w', 'post_norm_w', 'w_in', 'conv_w', 'conv_b', 'rg_wa', 'rg_ba', 'rg_wx', 'rg_bx',
        'rg_lambda', 'hg_lb_logits', 'hg_onorm_w', 'w_out']
_OUTS = [(1, SEQ, D), (NB, NL, D), (1, 1, DA), (1, 1, CW - 1, DA), (1, 1, HB, P, P), (1, NB, DA), (1, NB, CW - 1, DA),
         (1, NB, HB, P, P)]


def kernel(**inputs):
    import numpy as _np
    import concourse.bacc as _bacc
    from concourse import mybir as _mybir
    from concourse.bass_utils import run_bass_kernel_spmd as _run

    nc = _bacc.Bacc("TRN2", target_bir_lowering=False, num_devices=1)
    arrays, args = {}, []
    for name in _INS:
        a = _np.ascontiguousarray(inputs[name])
        arrays[f"in_{name}_dram"] = a
        args.append(nc.dram_tensor(f"in_{name}_dram", a.shape, _mybir.dt.from_np(a.dtype), kind="ExternalInput").ap())
    for i, shape in enumerate(_OUTS):
        args.append(nc.dram_tensor(f"out_{i}_dram", shape, _mybir.dt.float32, kind="ExternalOutput").ap())
    build(nc, *args)
    r = _run(nc, [arrays], core_ids=[0])
    return tuple(r.results[0][f"out_{i}_dram"] for i in range(len(_OUTS)))
```
